# Optimizing a Trainium2 kernel written in Bass

```python
import math
import jax, jax.numpy as jnp
from jax import lax
import numpy as np

D_MODEL = 1024
BATCH = 1
SEQ = 256
DEPTH = 2

N_BRANCH = 4
BRANCH_W = D_MODEL // 4
GM_CHUNK = 128
GM_GROUPS = 4
ATT_HEAD_DIM = 64
ATT_HEADS = BRANCH_W // ATT_HEAD_DIM
IDX_HEADS = 4
IDX_DIM = 64
TOPK_MAX = 256
Q_BLOCK = 128
ROPE_THETA = 500000.0
ROPE_FRAC = 4
S5_GROUP = 16
S5_GROUPS = BRANCH_W // S5_GROUP
S5_STATE = 64
SSD_HEAD_DIM = 64
SSD_HEADS = BRANCH_W // SSD_HEAD_DIM
SSD_GROUPS = 2
SSD_STATE = 64
SSD_CONV = 4
SSD_CHUNK = 128
SSD_XBC = BRANCH_W + 2 * SSD_GROUPS * SSD_STATE
N_EXPERTS = 32
TOP_K = 8
N_EXPERT_GROUPS = 8
TOPK_GROUPS = 4
EXPERT_FF = D_MODEL // 4
SHARED_FF = EXPERT_FF
ROUTED_SCALE = 2.5
DN_ALPHA = (2 * DEPTH) ** 0.25
DN_BETA = (8 * DEPTH) ** -0.25
LN_EPS = 1e-5
RMS_EPS = 1e-6

IN_SPLITS = (BRANCH_W, BRANCH_W,
             ATT_HEADS * ATT_HEAD_DIM, ATT_HEAD_DIM, ATT_HEAD_DIM,
             IDX_HEADS * IDX_DIM, IDX_DIM, IDX_HEADS,
             BRANCH_W,
             BRANCH_W, SSD_XBC, SSD_HEADS)
D_IN = sum(IN_SPLITS)

kernel_name = "hybrid_gated_gmlp_dsa_s5_ssd_moe"

def layer_norm(x, g, b):
    xf = x.astype(jnp.float32)
    mu = jnp.mean(xf, -1, keepdims=True)
    var = jnp.mean(jnp.square(xf - mu), -1, keepdims=True)
    return ((xf - mu) * lax.rsqrt(var + LN_EPS) * g.astype(jnp.float32) + b.astype(jnp.float32)).astype(x.dtype)

def rope_tables(positions):
    rot = ATT_HEAD_DIM // ROPE_FRAC
    inv = ROPE_THETA ** (-jnp.arange(0, rot, 2, dtype=jnp.float32) / rot)
    ang = positions.astype(jnp.float32)[..., None] * inv
    return jnp.cos(ang), jnp.sin(ang)

def apply_partial_rope(t, cos, sin):
    half = cos.shape[-1]
    shp = cos.shape[:2] + (1,) * (t.ndim - 3) + (half,)
    cs, sn = cos.reshape(shp), sin.reshape(shp)
    tf = t.astype(jnp.float32)
    t1, t2 = tf[..., :half], tf[..., half:2 * half]
    return jnp.concatenate([t1 * cs - t2 * sn, t2 * cs + t1 * sn, tf[..., 2 * half:]], -1).astype(t.dtype)

def gmlp_mixer(u, v, ln_g, ln_b, sg_w, sg_b):
    B_, S_, W = u.shape
    u = jax.nn.gelu(u)
    v = layer_norm(jax.nn.gelu(v), ln_g, ln_b)
    v = v.reshape(B_, S_ // GM_CHUNK, GM_CHUNK, GM_GROUPS, W // GM_GROUPS)
    w = sg_w * jnp.tril(jnp.ones((GM_CHUNK, GM_CHUNK), sg_w.dtype))
    sv = jnp.einsum('gts,bnsgc->bntgc', w, v) + sg_b.T[:, :, None]
    return u * sv.reshape(B_, S_, W)

def dsa_attention(q, k, v, qi, ki, wi):
    B_, S_ = q.shape[:2]
    n_sel = min(TOPK_MAX, S_ // 4)
    nb = S_ // Q_BLOCK
    wi = wi.astype(jnp.float32) * (IDX_HEADS ** -0.5 * IDX_DIM ** -0.5)
    key_pos = jnp.arange(S_)

    def blocks(t):
        return jnp.moveaxis(t.reshape((B_, nb, Q_BLOCK) + t.shape[2:]), 1, 0)

    def one_block(args):
        qb, qib, wib, start = args
        qpos = start + jnp.arange(Q_BLOCK)
        idx_logits = jnp.einsum('bqhd,bsd->bqhs', qib, ki).astype(jnp.float32)
        score = jnp.einsum('bqhs,bqh->bqs', jax.nn.relu(idx_logits), wib)
        causal = key_pos[None, :] <= qpos[:, None]
        score = jnp.where(causal[None], score, -jnp.inf)
        _, sel = lax.top_k(score, n_sel)
        k_sel = jax.vmap(lambda kb, ib: kb[ib])(k, sel)
        v_sel = jax.vmap(lambda vb, ib: vb[ib])(v, sel)
        valid = sel <= qpos[None, :, None]
        logits = jnp.einsum('bqhd,bqnd->bhqn', qb, k_sel).astype(jnp.float32) * ATT_HEAD_DIM ** -0.5
        logits = jnp.where(valid[:, None], logits, -jnp.inf)
        p = jax.nn.softmax(logits, axis=-1).astype(v.dtype)
        return jnp.einsum('bhqn,bqnd->bqhd', p, v_sel)

    starts = jnp.arange(nb) * Q_BLOCK
    out = lax.map(one_block, (blocks(q), blocks(qi), blocks(wi), starts))
    return jnp.moveaxis(out, 0, 1).reshape(B_, S_, ATT_HEADS * ATT_HEAD_DIM)

def s5_mixer(u, lam_re, lam_im, log_step, b_re, b_im, c_re, c_im, d_skip, glu_w, glu_b):
    B_, S_, W = u.shape
    f32 = jnp.float32
    uf = u.astype(f32)
    ug = uf.reshape(B_, S_, S5_GROUPS, S5_GROUP)
    lr, li = lam_re.astype(f32), lam_im.astype(f32)
    step = jnp.exp(log_step.astype(f32))[:, None]
    mag = jnp.exp(lr * step)
    ab_re, ab_im = mag * jnp.cos(li * step), mag * jnp.sin(li * step)
    den = lr * lr + li * li
    nr = ab_re - 1.0
    cr = (nr * lr + ab_im * li) / den
    ci = (ab_im * lr - nr * li) / den
    br, bi = b_re.astype(f32), b_im.astype(f32)
    bb_re = cr[..., None] * br - ci[..., None] * bi
    bb_im = cr[..., None] * bi + ci[..., None] * br
    x_re = jnp.einsum('bsgc,gpc->bsgp', ug, bb_re)
    x_im = jnp.einsum('bsgc,gpc->bsgp', ug, bb_im)
    a_re = jnp.broadcast_to(ab_re, x_re.shape)
    a_im = jnp.broadcast_to(ab_im, x_im.shape)

    def combine(e1, e2):
        a1r, a1i, b1r, b1i = e1
        a2r, a2i, b2r, b2i = e2
        return (a2r * a1r - a2i * a1i, a2r * a1i + a2i * a1r,
                a2r * b1r - a2i * b1i + b2r, a2r * b1i + a2i * b1r + b2i)

    _, _, h_re, h_im = lax.associative_scan(combine, (a_re, a_im, x_re, x_im), axis=1)
    y = (jnp.einsum('bsgp,gcp->bsgc', h_re, c_re.astype(f32))
         - jnp.einsum('bsgp,gcp->bsgc', h_im, c_im.astype(f32)))
    y = y.reshape(B_, S_, W) + d_skip.astype(f32) * uf
    y = jax.nn.gelu(y).astype(u.dtype)
    return y * jax.nn.sigmoid(y @ glu_w + glu_b)

def segsum(a):
    T = a.shape[-1]
    ar = jnp.broadcast_to(a[..., None], a.shape + (T,))
    strict = jnp.tril(jnp.ones((T, T), bool), -1)
    cs = jnp.cumsum(jnp.where(strict, ar, 0.0), axis=-2)
    return jnp.where(jnp.tril(jnp.ones((T, T), bool)), cs, -jnp.inf)

def ssd_mixer(z, xbc, dt, conv_w, conv_b, dt_bias, a_log, d_skip, norm_g):
    B_, S_, _ = xbc.shape
    f32 = jnp.float32
    conv = lax.conv_general_dilated(xbc, conv_w[:, None, :], window_strides=(1,),
                                    padding=[(SSD_CONV - 1, 0)],
                                    dimension_numbers=('NWC', 'WIO', 'NWC'),
                                    feature_group_count=xbc.shape[-1])
    xbc = jax.nn.silu(conv + conv_b)
    x, bm, cm = jnp.split(xbc, [BRANCH_W, BRANCH_W + SSD_GROUPS * SSD_STATE], axis=-1)
    hpg = SSD_HEADS // SSD_GROUPS
    nc = S_ // SSD_CHUNK
    dt = jax.nn.softplus(dt.astype(f32) + dt_bias.astype(f32))
    a = -jnp.exp(a_log.astype(f32))
    xf = x.astype(f32)
    X = xf.reshape(B_, nc, SSD_CHUNK, SSD_GROUPS, hpg, SSD_HEAD_DIM)
    Xdt = X * dt.reshape(B_, nc, SSD_CHUNK, SSD_GROUPS, hpg)[..., None]
    Adt = (dt * a).reshape(B_, nc, SSD_CHUNK, SSD_GROUPS, hpg).transpose(0, 3, 4, 1, 2)
    Bm = bm.astype(f32).reshape(B_, nc, SSD_CHUNK, SSD_GROUPS, SSD_STATE)
    Cm = cm.astype(f32).reshape(B_, nc, SSD_CHUNK, SSD_GROUPS, SSD_STATE)
    a_cum = jnp.cumsum(Adt, axis=-1)
    Lmat = jnp.exp(segsum(Adt))
    y_diag = jnp.einsum('bclgn,bcsgn,bgjcls,bcsgjp->bclgjp', Cm, Bm, Lmat, Xdt)
    decay_states = jnp.exp(a_cum[..., -1:] - a_cum)
    states = jnp.einsum('bclgn,bgjcl,bclgjp->bcgjpn', Bm, decay_states, Xdt)
    states = jnp.concatenate([jnp.zeros_like(states[:, :1]), states], axis=1)
    chunk_a = jnp.pad(a_cum[..., -1], ((0, 0), (0, 0), (0, 0), (1, 0)))
    decay_chunk = jnp.exp(segsum(chunk_a))
    states = jnp.einsum('bgjzc,bcgjpn->bzgjpn', decay_chunk, states)[:, :-1]
    y_off = jnp.einsum('bclgn,bcgjpn,bgjcl->bclgjp', Cm, states, jnp.exp(a_cum))
    y = (y_diag + y_off).reshape(B_, S_, SSD_HEADS, SSD_HEAD_DIM)
    y = y + d_skip.astype(f32)[:, None] * xf.reshape(B_, S_, SSD_HEADS, SSD_HEAD_DIM)
    y = (y.reshape(B_, S_, BRANCH_W) * jax.nn.silu(z.astype(f32))).reshape(B_, S_, SSD_GROUPS, -1)
    y = y * lax.rsqrt(jnp.mean(jnp.square(y), -1, keepdims=True) + RMS_EPS)
    return (y.reshape(B_, S_, BRANCH_W) * norm_g.astype(f32)).astype(z.dtype)

def hybrid_mixer(h, cos, sin, w_in, gm_ln_g, gm_ln_b, gm_w, gm_b,
                 s5_lam_re, s5_lam_im, s5_log_step, s5_b_re, s5_b_im, s5_c_re, s5_c_im, s5_d,
                 s5_glu_w, s5_glu_b, ssd_conv_w, ssd_conv_b, ssd_dt_bias, ssd_a_log, ssd_d, ssd_norm_g,
                 w_branch, w_gate, w_out):
    B_, S_, _ = h.shape
    proj = h @ w_in
    cuts = [int(i) for i in np.cumsum(IN_SPLITS)[:-1]]
    gm_u, gm_v, q, k, v, qi, ki, wi, s5_u, z, xbc, dt = jnp.split(proj, cuts, axis=-1)
    y_a = gmlp_mixer(gm_u, gm_v, gm_ln_g, gm_ln_b, gm_w, gm_b)
    q = apply_partial_rope(q.reshape(B_, S_, ATT_HEADS, ATT_HEAD_DIM), cos, sin)
    k = apply_partial_rope(k, cos, sin)
    qi = apply_partial_rope(qi.reshape(B_, S_, IDX_HEADS, IDX_DIM), cos, sin)
    ki = apply_partial_rope(ki, cos, sin)
    y_b = dsa_attention(q, k, v, qi, ki, wi)
    y_c = s5_mixer(s5_u, s5_lam_re, s5_lam_im, s5_log_step, s5_b_re, s5_b_im, s5_c_re, s5_c_im,
                   s5_d, s5_glu_w, s5_glu_b)
    y_d = ssd_mixer(z, xbc, dt, ssd_conv_w, ssd_conv_b, ssd_dt_bias, ssd_a_log, ssd_d, ssd_norm_g)
    branches = (y_a, y_b, y_c, y_d)
    merged = jax.nn.sigmoid(h @ w_gate[0]) * (branches[0].astype(h.dtype) @ w_branch[0])
    for i in range(1, N_BRANCH):
        merged = merged + jax.nn.sigmoid(h @ w_gate[i]) * (branches[i].astype(h.dtype) @ w_branch[i])
    return merged @ w_out

def moe_ffn(h, router_w, router_bias, w1, w3, w2, sw1, sw3, sw2):
    B_, S_, _ = h.shape
    f32 = jnp.float32
    scores = jax.nn.sigmoid((h @ router_w).astype(f32))
    biased = scores + router_bias.astype(f32)
    grp = biased.reshape(B_, S_, N_EXPERT_GROUPS, N_EXPERTS // N_EXPERT_GROUPS)
    grp_score = jnp.sum(lax.top_k(grp, 2)[0], -1)
    _, gidx = lax.top_k(grp_score, TOPK_GROUPS)
    gmask = jnp.sum(jax.nn.one_hot(gidx, N_EXPERT_GROUPS, dtype=f32), -2) > 0
    emask = jnp.repeat(gmask, N_EXPERTS // N_EXPERT_GROUPS, axis=-1)
    _, eidx = lax.top_k(jnp.where(emask, biased, -jnp.inf), TOP_K)
    w = jnp.take_along_axis(scores, eidx, axis=-1)
    w = w / jnp.sum(w, -1, keepdims=True) * ROUTED_SCALE
    gates = jnp.sum(jax.nn.one_hot(eidx, N_EXPERTS, dtype=f32) * w[..., None], -2)

    def per_seq(args):
        hs, gs = args
        a = jnp.einsum('sd,edf->sef', hs, w1)
        b = jnp.einsum('sd,edf->sef', hs, w3)
        act = jax.nn.silu(a) * b * gs[..., None].astype(hs.dtype)
        return jnp.einsum('sef,efd->sd', act, w2)

    routed = lax.map(per_seq, (h, gates))
    shared = (jax.nn.silu(h @ sw1) * (h @ sw3)) @ sw2
    return routed + shared

def adaln(c, w, b):
    m = c @ w + b
    shift, scale, gate = jnp.split(m, 3, axis=-1)
    return shift[:, None], scale[:, None], gate[:, None]

def setup_inputs(seed: int = 0) -> dict:
    key = jax.random.key(seed)
    keys = jax.random.split(key, 64)
    cnt = [0]
    f32 = jnp.float32
    L, D, W = DEPTH, D_MODEL, BRANCH_W

    def nk():
        k = keys[cnt[0]]
        cnt[0] += 1
        return k

    def nrm(shape, scale):
        return jax.random.normal(nk(), shape, f32) * scale

    def near_one(shape, s=0.02):
        return 1.0 + nrm(shape, s)

    x = nrm((BATCH, SEQ, D), 1.0)
    c = nrm((BATCH, D), 1.0)
    offset = jax.random.randint(nk(), (BATCH, 1), 0, 4096)
    positions = (offset + jnp.arange(SEQ)[None, :]).astype(jnp.int32)

    mod1_w = nrm((L, D, 3 * D), 0.2 * D ** -0.5)
    mod1_b = nrm((L, 3 * D), 0.02)
    w_in = nrm((L, D, D_IN), D ** -0.5)
    gm_ln_g = near_one((L, W))
    gm_ln_b = nrm((L, W), 0.02)
    gm_w = nrm((L, GM_GROUPS, GM_CHUNK, GM_CHUNK), GM_CHUNK ** -0.5)
    gm_b = near_one((L, GM_GROUPS, GM_CHUNK), 0.1)

    s5_lam_re = -0.5 + nrm((L, S5_GROUPS, S5_STATE), 0.01)
    s5_lam_im = math.pi * jnp.arange(S5_STATE, dtype=f32) + nrm((L, S5_GROUPS, S5_STATE), 0.01)
    s5_log_step = jax.random.uniform(nk(), (L, S5_GROUPS), f32, math.log(1e-3), math.log(1e-1))
    s5_b_re = nrm((L, S5_GROUPS, S5_STATE, S5_GROUP), (2 * S5_GROUP) ** -0.5)
    s5_b_im = nrm((L, S5_GROUPS, S5_STATE, S5_GROUP), (2 * S5_GROUP) ** -0.5)
    s5_c_re = nrm((L, S5_GROUPS, S5_GROUP, S5_STATE), S5_STATE ** -0.5)
    s5_c_im = nrm((L, S5_GROUPS, S5_GROUP, S5_STATE), S5_STATE ** -0.5)
    s5_d = nrm((L, W), 1.0)
    s5_glu_w = nrm((L, W, W), W ** -0.5)
    s5_glu_b = nrm((L, W), 0.02)

    ssd_conv_w = nrm((L, SSD_CONV, SSD_XBC), SSD_CONV ** -0.5)
    ssd_conv_b = nrm((L, SSD_XBC), 0.02)
    dt0 = jnp.exp(jax.random.uniform(nk(), (L, SSD_HEADS), f32, math.log(1e-3), math.log(1e-1)))
    ssd_dt_bias = dt0 + jnp.log(-jnp.expm1(-dt0))
    ssd_a_log = jnp.log(jax.random.uniform(nk(), (L, SSD_HEADS), f32, 1.0, 16.0))
    ssd_d = near_one((L, SSD_HEADS), 0.1)
    ssd_norm_g = near_one((L, W))

    w_branch = nrm((L, N_BRANCH, W, D), W ** -0.5)
    w_gate = nrm((L, N_BRANCH, D, D), D ** -0.5)
    w_out = nrm((L, D, D), D ** -0.5 * DN_BETA)
    ln1_g = near_one((L, D))
    ln1_b = nrm((L, D), 0.02)

    mod2_w = nrm((L, D, 3 * D), 0.2 * D ** -0.5)
    mod2_b = nrm((L, 3 * D), 0.02)
    router_w = nrm((L, D, N_EXPERTS), D ** -0.5)
    router_bias = nrm((L, N_EXPERTS), 0.01)
    exp_w1 = nrm((L, N_EXPERTS, D, EXPERT_FF), D ** -0.5)
    exp_w3 = nrm((L, N_EXPERTS, D, EXPERT_FF), D ** -0.5)
    exp_w2 = nrm((L, N_EXPERTS, EXPERT_FF, D), EXPERT_FF ** -0.5 * DN_BETA)
    sh_w1 = nrm((L, D, SHARED_FF), D ** -0.5)
    sh_w3 = nrm((L, D, SHARED_FF), D ** -0.5)
    sh_w2 = nrm((L, SHARED_FF, D), SHARED_FF ** -0.5 * DN_BETA)
    ln2_g = near_one((L, D))
    ln2_b = nrm((L, D), 0.02)

    return {"x": x, "c": c, "positions": positions,
            "mod1_w": mod1_w, "mod1_b": mod1_b, "w_in": w_in,
            "gm_ln_g": gm_ln_g, "gm_ln_b": gm_ln_b, "gm_w": gm_w, "gm_b": gm_b,
            "s5_lam_re": s5_lam_re, "s5_lam_im": s5_lam_im, "s5_log_step": s5_log_step,
            "s5_b_re": s5_b_re, "s5_b_im": s5_b_im, "s5_c_re": s5_c_re, "s5_c_im": s5_c_im,
            "s5_d": s5_d, "s5_glu_w": s5_glu_w, "s5_glu_b": s5_glu_b,
            "ssd_conv_w": ssd_conv_w, "ssd_conv_b": ssd_conv_b, "ssd_dt_bias": ssd_dt_bias,
            "ssd_a_log": ssd_a_log, "ssd_d": ssd_d, "ssd_norm_g": ssd_norm_g,
            "w_branch": w_branch, "w_gate": w_gate, "w_out": w_out, "ln1_g": ln1_g, "ln1_b": ln1_b,
            "mod2_w": mod2_w, "mod2_b": mod2_b, "router_w": router_w, "router_bias": router_bias,
            "exp_w1": exp_w1, "exp_w3": exp_w3, "exp_w2": exp_w2,
            "sh_w1": sh_w1, "sh_w3": sh_w3, "sh_w2": sh_w2, "ln2_g": ln2_g, "ln2_b": ln2_b}

def reference(x, c, positions, mod1_w, mod1_b, w_in, gm_ln_g, gm_ln_b, gm_w, gm_b,
              s5_lam_re, s5_lam_im, s5_log_step, s5_b_re, s5_b_im, s5_c_re, s5_c_im,
              s5_d, s5_glu_w, s5_glu_b, ssd_conv_w, ssd_conv_b, ssd_dt_bias, ssd_a_log, ssd_d, ssd_norm_g,
              w_branch, w_gate, w_out, ln1_g, ln1_b, mod2_w, mod2_b, router_w, router_bias,
              exp_w1, exp_w3, exp_w2, sh_w1, sh_w3, sh_w2, ln2_g, ln2_b):
    cos, sin = rope_tables(positions)
    for l in range(DEPTH):
        shift, scale, gate = adaln(c, mod1_w[l], mod1_b[l])
        h = x * (1.0 + scale) + shift
        mix = hybrid_mixer(h, cos, sin, w_in[l], gm_ln_g[l], gm_ln_b[l], gm_w[l], gm_b[l],
                           s5_lam_re[l], s5_lam_im[l], s5_log_step[l], s5_b_re[l], s5_b_im[l],
                           s5_c_re[l], s5_c_im[l], s5_d[l], s5_glu_w[l], s5_glu_b[l],
                           ssd_conv_w[l], ssd_conv_b[l], ssd_dt_bias[l], ssd_a_log[l], ssd_d[l],
                           ssd_norm_g[l], w_branch[l], w_gate[l], w_out[l])
        x = layer_norm(DN_ALPHA * x + (1.0 + gate) * mix, ln1_g[l], ln1_b[l])

        shift, scale, gate = adaln(c, mod2_w[l], mod2_b[l])
        h = x * (1.0 + scale) + shift
        ffn = moe_ffn(h, router_w[l], router_bias[l], exp_w1[l], exp_w3[l], exp_w2[l],
                      sh_w1[l], sh_w3[l], sh_w2[l])
        x = layer_norm(DN_ALPHA * x + (1.0 + gate) * ffn, ln2_g[l], ln2_b[l])
    return x


_drawn_inputs = setup_inputs


def setup_inputs(seed=0):
    import zlib

    import numpy as np

    out = dict(_drawn_inputs(seed))
    spreads = {}
    factors = {'gm_ln_g': 3.223,
     'gm_ln_b': 5.559,
     's5_lam_re': 8.0,
     's5_c_re': 3.106,
     's5_c_im': 2.723,
     's5_glu_b': 8.0,
     'ssd_norm_g': 3.08}
    for name, (base, spread) in spreads.items():
        noise = np.random.default_rng([zlib.crc32(name.encode()), seed]).standard_normal(out[name].shape)
        drawn = base * np.exp(spread * noise) if base else spread * noise
        out[name] = __import__('jax').numpy.asarray(drawn.astype(out[name].dtype))
    for name, factor in factors.items():
        out[name] = (out[name] * factor).astype(out[name].dtype)
    return out
```

```python
import math
from contextlib import ExitStack

import numpy as np

import concourse.bass as bass
from concourse import mybir

F32 = mybir.dt.float32
F32R = mybir.dt.float32r
I32 = mybir.dt.int32
ACT = mybir.ActivationFunctionType
ALU = mybir.AluOpType
AX = mybir.AxisListType

P = 128
D = 1024
KD = D // P
S = 256
NB = S // P
DEPTH = 2
W = 256
CW = W // P
E = 32
TOPK = 8
NSEL = 64
EPS_LN = 1e-5
EPS_RMS = 1e-6
ALPHA = (2 * DEPTH) ** 0.25
NPROJ = 9
NGATE = 16
N_W1S = NPROJ + NGATE + 4 + 4
NUNIT = N_W1S + 3 * (E + 1)
UC = 2048
MODH = 1536
TWO_PI = 2 * math.pi
PI_A = 6.28125
PI_B = float(np.float32(TWO_PI - PI_A) - np.float32(TWO_PI - PI_A) % np.float32(2.0 ** -20))
PI_C = TWO_PI - PI_A - PI_B
ROUND = 1.5 * 2.0 ** 23
ROUND14 = 1.5 * 2.0 ** 9
FLOOR = -3.0e38
TAKEN = -3.4e38
AWAY = 1.0e30

CONST_COLS = dict(ident=128, upper=128, lower=128, floor=128, ones=128, time=256, inv=8, before=64)
PARAM_COLS = dict(conv_w=16, conv_b=4, dt_bias=4, a_log=4, ssd_d=4, s5_d=2, glu_b=2, gm_g=256, gm_b=256,
                  norm_g=256, sg_b=256, sg_w=512, s5_b=512, s5_c=512, glu_w=512)
AHEAD_COLS = dict(lam_re=8, lam_im=8, log_step=8, mod_b=32, norm_g=16, norm_b=16)
TINY_COLS = dict(var=2, mv=4, stats=24, phi_hi=8, phi_lo=8, s5a=8, s5b=8, s5c=8, s5d=8, sin=8, half=8, rope_a=16,
                 rope_b=16, dt_v=8, dt_e=8, dt=8, shift=1, exp_a=4, adt=8, acum=8, acum_e=4, ms=4, wi=8, top=8, neg=8,
                 den=8, glu_hb=2, mvg=4)


def columns(table):
    at, out = 0, {}
    for name, n in table.items():
        out[name] = slice(at, at + n)
        at += n
    return out, at


ORDER = ("P0 P1 P2 P3 ssd1 P4 ssd2 P6 att1 P7 gm index ssd3 P8 ssd4 G0 G1 logits G2 ssd5 G3 B0 G4 G5 att3 P5 att4 "
         "G6 s50 G7 B1 s51 G8 G9 s52 G10 G11 B2 s53 G12 G13 s54 G14 glu G15 B3 O0 O1 O2 O3").split()
ACT_ORDER = ("P0 P1 P2 silu_xbc softplus P3 x_tok P4 decay P6 qk_t v_root P7 relu state P8 G0 rms_root G1 G2 y0 G3 "
             "B0 y1 G4 exp G5 prob_t P5 G6 G7 B1 y2 G8 G9 G10 G11 B2 G12 G13 gelu G14 tanh y3 G15 B3 O0 O1 O2 O3"
             ).split()
UNITS = [x for x in ORDER if x[0] in "PGBO"]
TURNS = [(x, part) for x in UNITS if x[0] != "O" for part in range(4 if x[0] == "B" else 1)]
BRANCH_OF = (3, 0, 1, 2)


def made(n):
    return n // 3


def uses(n):
    return n // 3 + 1


def loads(n):
    return n // 2 - (n % 2 == 0)


def turn(x, part=0):
    return TURNS.index((x, part))


def bass_trunk(nc, x, pos, cvec, consts, params, router_w, router_b, gate_b, ahead, norms, mods, stream, gate_rows, gates_t,
               out):
    CC, NCONST = columns(CONST_COLS)
    PC, NPARAM = columns(PARAM_COLS)
    TC, NTINY = columns(TINY_COLS)
    AC, NAHEAD = columns(AHEAD_COLS)

    ctx = ExitStack()
    with ctx:
        layer_go = ctx.enter_context(nc.semaphore("layer_go"))
        counters = []

        def sem(name):
            counters.append(ctx.enter_context(nc.semaphore(name)))
            return counters[-1]

        layer_done = sem("layer_done")
        raw_in = [sem(f"raw_in{i}") for i in range(2)]
        hi_done = [sem(f"hi_done{i}") for i in range(3)]
        lo_done = [sem(f"lo_done{i}") for i in range(3)]
        used = [sem(f"used{i}") for i in range(3)]
        turn_free = [sem(f"turn_free{i}") for i in range(2)]
        mod_in = [sem(f"mod_in{i}") for i in range(4)]
        mod_used = [sem(f"mod_used{i}") for i in range(4)]
        g_in = [sem(f"g_in{i}") for i in range(2)]
        const_in, c_in, pos_in, x_in = sem("const_in"), sem("c_in"), sem("pos_in"), sem("x_in")
        ahead_in, params_in, router_in, gate_b_in, norm_in = (
            sem("ahead_in"), sem("params_in"), sem("router_in"), sem("gate_b_in"), sem("norm_in"))
        angle_ready, acc_zero = sem("angle_ready"), sem("acc_zero")
        step_exp, decay_in, turns_ready, trig_ready, phase_ready, sines_ready = (
            sem("step_exp"), sem("decay_in"), sem("turns_ready"), sem("trig_ready"), sem("phase_ready"),
            sem("sines_ready"))
        sums_ps, sums_sb, cols_ps, rows_ps, rows_sb, rows_out, sc_ready = (
            sem("sums_ps"), sem("sums_sb"), sem("cols_ps"), sem("rows_ps"), sem("rows_sb"), sem("rows_out"), sem("sc_ready"))
        xt_ps, h_hi, h_ready = sem("xt_ps"), sem("h_hi"), sem("h_ready")
        conv_ready, xbc_ready, dt_abs, dt_log, adt_ready = (
            sem("conv_ready"), sem("xbc_ready"), sem("dt_abs"), sem("dt_log"), sem("adt_ready"))
        ssd1_ps, x_tok, ssd2_ps, decay_log, decay_exp, mask_ready, ssd3_ps, state_sb, ssd4_ps = (
            sem("ssd1_ps"), sem("x_tok"), sem("ssd2_ps"), sem("decay_log"), sem("decay_exp"), sem("mask_ready"),
            sem("ssd3_ps"), sem("state_sb"), sem("ssd4_ps"))
        rms_sq, rms_root, ssd_ready, ssd5_ps = sem("rms_sq"), sem("rms_root"), sem("ssd_ready"), sem("ssd5_ps")
        qk_ready, att1_ps, qk_t, index_ps, logit_ps, relu_sb, logit_max, exp_ready, prob_ready, att3_ps, prob_t, \
            att4_ps = (sem("qk_ready"), sem("att1_ps"), sem("qk_t"), sem("index_ps"), sem("logit_ps"),
                       sem("relu_sb"), sem("logit_max"), sem("exp_ready"), sem("prob_ready"), sem("att3_ps"),
                       sem("prob_t"), sem("att4_ps"))
        v_var, v_root, v_ready, gm_ps, gm_ready = (
            sem("v_var"), sem("v_root"), sem("v_ready"), sem("gm_ps"), sem("gm_ready"))
        c_ready, s5v_ps, s5v_read, s5h_ready, s5y_ps, s5y_ready, s5_gelu, glu_ps, glu_tanh, glu_ready = (
            sem("c_ready"), sem("s5v_ps"), sem("s5v_read"), sem("s5h_ready"), sem("s5y_ps"), sem("s5y_ready"),
            sem("s5_gelu"), sem("glu_ps"), sem("glu_tanh"), sem("glu_ready"))
        y_hi, y_lo, y_used, branch_ps, merged, mix_hi, mix_ready, wout_ps = (
            sem("y_hi"), sem("y_lo"), sem("y_used"), sem("branch_ps"), sem("merged"), sem("mix_hi"),
            sem("mix_ready"), sem("wout_ps"))
        ln_var, ln_root, ln_scale, xn0_ready, xn1_ready, ln_done = (
            sem("ln_var"), sem("ln_root"), sem("ln_scale"), sem("xn0_ready"), sem("xn1_ready"), sem("ln_done"))
        router_w_in, router_hi, router_ready, route_ps, sig_ready, sig_ps, gates_ready, gates_ps, gates_sb, gates_out = (
            sem("router_w_in"), sem("router_hi"), sem("router_ready"), sem("route_ps"), sem("sig_ready"), sem("sig_ps"),
            sem("gates_ready"),
            sem("gates_ps"), sem("gates_sb"), sem("gates_out"))
        silu_done, b_read, act_ready, act_hi, act_lo, moe_ps = (
            sem("silu_done"), sem("b_read"), sem("act_ready"), sem("act_hi"), sem("act_lo"),
            sem("moe_ps"))
        numbers = sorted(s.num for s in counters)
        assert numbers == list(range(numbers[0], numbers[-1] + 1))
        out_in = ctx.enter_context(nc.semaphore("out_in"))

        class Region:
            def __init__(self, at):
                self.at = at

            def put(self, name, cols, dt=F32):
                t = nc.alloc_sbuf_tensor_at(name, [P, cols], dt, offset=self.at)
                self.at += -(-4 * cols // 32) * 32
                return t[:, :]

        keep = Region(-(-nc.sbuf_base // 32) * 32)
        X = keep.put("X", NB * D)
        HH, HL = keep.put("HH", KD * S, F32R), keep.put("HL", KD * S, F32R)
        RAW = [keep.put(f"RAW{i}", UC) for i in range(2)]
        WH = [keep.put(f"WH{i}", UC, F32R) for i in range(3)]
        WL = [keep.put(f"WL{i}", UC, F32R) for i in range(3)]
        COS, SIN = keep.put("COS", 8 * S), keep.put("SIN", 8 * S)
        YH, YL = [keep.put("YH0", 512, F32R)], [keep.put("YL0", 512, F32R)]
        CON = keep.put("CON", NCONST)
        ROUT = keep.put("ROUT", E)
        SC = keep.put("SC", 32)
        AHEAD, S5D = keep.put("AHEAD", NAHEAD), keep.put("S5D", 24)
        TINY = keep.put("TINY", NTINY)
        CVEC = keep.put("CVEC", KD)
        ROPE = keep.put("ROPE", 32)

        mix = Region(keep.at)
        SIG = mix.put("SIG", NGATE * 512)
        PAR = mix.put("PAR", NPARAM)
        MISC = mix.put("MISC", 512)
        QK = mix.put("QK", NB * 12 * 64)
        UT, V, GU, Z = (mix.put(n, 512) for n in ("UT", "V", "GU", "Z"))
        conv_at = mix.at
        CIN = mix.put("CIN", 4 * (S + 4))
        XBC = mix.put("XBC", 4 * S)
        WORK = mix.put("WORK", 3072)
        QT = mix.put("QT", 1536)
        SCORE = [mix.put("SCORE0", P), mix.put("SCORE1", S)]
        LEFT = [mix.put("LEFT0", P), mix.put("LEFT1", S)]
        CRE, CIM = mix.put("CRE", 256), mix.put("CIM", 256)
        MG = Region(conv_at).put("MG", KD * S)

        moe = Region(keep.at)
        stage_at = [moe.at]
        NRM = moe.put("NRM", 3 * D)
        acc_at = moe.at
        ACC = moe.put("ACC", 2 * 3 * D)
        stage_at.append(moe.at)
        MODR = [moe.put(f"MODR{i}", MODH) for i in range(2)]
        stage_at.append(moe.at)
        G = [moe.put(f"G{i}", S) for i in range(2)]
        SL = [moe.put(f"SL{i}", 512) for i in range(2)]
        T = [moe.put(f"T{i}", 512) for i in range(2)]
        YH.append(moe.put("YH1", 512, F32R))
        YL.append(moe.put("YL1", 512, F32R))
        GT = moe.put("GT", S)
        RT = moe.put("RT", 1024)
        HT = moe.put("HT", KD * S)
        GROW, GBR = moe.put("GROW", 512), moe.put("GBR", 512)
        stage_at.append(moe.at)
        STAGE = [Region(at).put(f"STAGE{i}", 3 * D) for i, at in enumerate(stage_at)]
        router_at = Region(stage_at[3])
        RW, RWH, RWL = (router_at.put("RW", KD * P), router_at.put("RWH", KD * P, F32R),
                        router_at.put("RWL", KD * P, F32R))
        XN = Region(acc_at).put("XN", NB * D)
        LNT = Region(stage_at[1]).put("LNT", NB * D)
        moe.at += 4 * 3 * D
        assert max(mix.at, moe.at) <= nc.sbuf_usable_end, (mix.at, moe.at, nc.sbuf_usable_end)

        PS = ctx.enter_context(nc.psum_tensor("PS", [P, 8, 512], F32))

        def con(name):
            return CON[:, CC[name]]

        def par(name):
            return PAR[:, PC[name]]

        def tiny(name, a=0, b=None):
            s = TC[name]
            return TINY[:, s.start + a:s.stop if b is None else s.start + b]

        def wide(ap, n):
            return ap.unsqueeze(2).broadcast_to([ap.shape[0], ap.shape[1], n])

        def rep(ap, n):
            return ap.unsqueeze(1).broadcast_to([ap.shape[0], n, ap.shape[1]])

        X3 = X.rearrange("p (b d) -> p b d", b=NB)
        hh, hl = (t.rearrange("p (k t) -> p k t", k=KD) for t in (HH, HL))
        sc4 = SC.rearrange("p (j s k) -> p j s k", j=2, s=2)
        acc3 = ACC.rearrange("p (j n) -> p j n", j=2)
        qk4 = QK.rearrange("p (b g d) -> p b g d", b=NB, g=12)
        misc3 = MISC.rearrange("p (b n) -> p b n", b=NB)
        cin3 = CIN.rearrange("p (c t) -> p c t", c=4)
        xbc3 = XBC.rearrange("p (c t) -> p c t", c=4)
        XT, BT, LM = WORK[:, 0:512], WORK[:, 512:640], WORK[:, 640:1664]
        XDT, DECX, ST, YS = WORK[:, 1664:2176], WORK[:, 2176:2432], WORK[:, 2432:2560], WORK[:, 2560:3072]
        RL = [QK[:, 0:512], QK[:, 512:1536]]
        PT = [QT[:, 0:512], QT[:, 512:1536]]
        B5 = [WORK[:, 512 * i:512 * i + 512] for i in range(6)]
        NKEY = (P, S)

        def psum(a, b=None):
            return PS[:, a:(b or a + 1), :].rearrange("p a n -> p (a n)")

        def turn_wait(eng, i):
            if i >= 2:
                eng.wait_ge(turn_free[i % 2], i // 2)

        def end_of_layer(eng, l):
            eng.drain().then_inc(layer_done, 1)
            if eng is nc.sync:
                eng.wait_ge(layer_done, 5)
                eng.sem_clear(range(numbers[0], numbers[-1] + 1))
                eng.drain().then_inc(layer_go, 1)
            else:
                eng.wait_ge(layer_go, l + 1)

        block = ctx.enter_context(nc.Block())

        @block.sync
        def _(sp):
            sp.dma_start(CON, consts).then_inc(const_in, 16)
            sp.dma_start(RT[:, 0:NB].bitcast(I32), pos).then_inc(pos_in, 16)
            sp.dma_start(AHEAD, ahead[0]).then_inc(ahead_in, 16)
            sp.dma_start(CVEC, cvec).then_inc(c_in, 16)

            def mod_whole(kk, i):
                if not isinstance(kk, int):
                    sp.wait_ge(mod_used[i], kk)
                sp.dma_start(STAGE[i], mods[0, 2 * kk + i // 2, i % 2]).then_inc(mod_in[i], 16)

            def mod_half(layer, k, i):
                if i >= 2 or not isinstance(k, int):
                    sp.wait_ge(mod_used[i % 2], 2 * k + i // 2)
                half = slice(i % 2 * MODH, i % 2 * MODH + MODH)
                sp.dma_start(MODR[i % 2], mods[layer, k, i // 2, :, half]).then_inc(mod_in[i % 2], 16)

            def load_gate_b(layer):
                for r in range(4):
                    sp.dma_start(GBR[32 * r:32 * r + 32, :], gate_b[layer, r:r + 1, :].to_broadcast([32, 512])
                                 ).then_inc(gate_b_in, 16)

            def store_gate_rows():
                sp.wait_ge(rows_sb, 1)
                for r in range(4):
                    sp.dma_start(gate_rows[r // 2:r // 2 + 1, r % 2 * 512:r % 2 * 512 + 512],
                                 GROW[32 * r:32 * r + 1, :]).then_inc(rows_out, 16)
                sp.wait_ge(rows_out, 64)

            for i in range(4):
                mod_whole(0, i)
            sp.dma_start(X3, x.rearrange("(b p) d -> p b d", p=P)).then_inc(x_in, 16)
            load_gate_b(0)
            with sp.Fori(1, KD // 2) as kk:
                for i in range(4):
                    mod_whole(kk, i)
            sp.dma_start(RAW[0], stream[0]).then_inc(raw_in[0], 16)
            sp.dma_start(RAW[1], stream[1]).then_inc(raw_in[1], 16)
            sp.wait_ge(hi_done[0], 1)
            sp.wait_ge(lo_done[0], 1)
            sp.dma_start(RAW[0], stream[2]).then_inc(raw_in[0], 16)
            store_gate_rows()
            end_of_layer(sp, 0)

            with sp.Fori(0, DEPTH) as l:
                def unit(n, k=0):
                    if n >= 5:
                        sp.wait_ge(hi_done[(n - 2) % 3], 4 * k + made(n - 2))
                        sp.wait_ge(lo_done[(n - 2) % 3], 4 * k + made(n - 2))
                    sp.dma_start(RAW[n % 2], stream[NUNIT * l + 12 * k + n]).then_inc(raw_in[n % 2], 16)

                unit(3)
                unit(4)
                sp.dma_start(PAR, params[l]).then_inc(params_in, 16)
                sp.dma_start(AHEAD, ahead[l + 1]).then_inc(ahead_in, 16)
                sp.dma_start(ROUT, router_b[l]).then_inc(router_in, 16)
                for n in range(5, N_W1S + 1):
                    unit(n)

                def load_norm(which):
                    for r in range(2):
                        sp.dma_start(NRM[:, r * D:(r + 1) * D],
                                     norms[l, which:which + 1, r * D:(r + 1) * D].to_broadcast([P, D])
                                     ).then_inc(norm_in, 16)
                    sp.dma_start(NRM[:, 2 * D:3 * D], gate_rows[which:which + 1, :].to_broadcast([P, D])
                                 ).then_inc(norm_in, 16)

                sp.wait_ge(merged, 4)
                load_norm(0)
                sp.dma_start(RW, router_w[l]).then_inc(router_w_in, 16)
                unit(N_W1S + 1)
                unit(N_W1S + 2)
                unit(N_W1S + 3)

                def store_gates():
                    sp.wait_ge(gates_sb, 1)
                    sp.dma_start(gates_t, GT[0:E, :]).then_inc(gates_out, 16)
                    sp.wait_ge(gates_out, 16)

                def four_experts(k):
                    for i in range(4):
                        for u in range(1, 4):
                            first = i == 0 and isinstance(k, int)
                            if u > 1 or not first:
                                unit(N_W1S + 2 + 3 * i + u, k)
                            if u == 2 and first:
                                load_gate_b(l + 1)
                                sp.wait_ge(ln_done, 2)
                                load_norm(1)
                                store_gates()
                        if i or not isinstance(k, int):
                            sp.wait_ge(act_ready, 4 * k + i)
                        sp.dma_start(G[(i + 1) % 2], gates_t[bass.ds(4 * k + i, 1), :].to_broadcast([P, S])
                                     ).then_inc(g_in[(i + 1) % 2], 16)
                        mod_half(l + 1, k, i)

                four_experts(0)
                with sp.Fori(1, KD) as k:
                    four_experts(k)
                for n in range(NUNIT, NUNIT + 3):
                    unit(n)
                sp.wait_ge(norm_in, 96)
                store_gate_rows()
                end_of_layer(sp, l + 1)
            sp.dma_start(out.rearrange("(b p) d -> p b d", p=P), X3).then_inc(out_in, 16)
            sp.wait_ge(out_in, 16)

        @block.gpsimd
        def _(pool):
            def tables():
                cos3, sin3 = (t.rearrange("p (j t) -> p j t", j=8) for t in (COS, SIN))
                time = rep(con("time"), 8)

                def fraction():
                    pool.drain()
                    pool.tensor_scalar(SIN, COS, ROUND, ROUND, ALU.add, ALU.subtract)
                    pool.drain()
                    pool.tensor_tensor(COS, COS, SIN, ALU.subtract)
                    pool.drain()

                pool.wait_ge(turns_ready, 1)
                pool.tensor_tensor(cos3, wide(tiny("phi_hi"), S), time, ALU.mult)
                fraction()
                pool.tensor_tensor(sin3, wide(tiny("phi_lo"), S), time, ALU.mult)
                pool.drain()
                pool.tensor_tensor(COS, COS, SIN, ALU.add)
                fraction()
                pool.drain().then_inc(phase_ready, 1)
                pool.wait_ge(sines_ready, 1)
                pool.tensor_tensor(COS, COS, COS, ALU.mult)
                pool.drain()
                pool.tensor_scalar(COS, COS, -2.0, 1.0, ALU.mult, ALU.add)

            def lo_part(n, times):
                pool.wait_ge(hi_done[n % 3], times)
                pool.tensor_tensor(WL[n % 3], RAW[n % 2], WH[n % 3].bitcast(F32), ALU.subtract
                                   ).then_inc(lo_done[n % 3], 1)

            def affine(i):
                pool.wait_ge(xn1_ready, i)
                pool.tensor_tensor(X[:, 3 * 512:], XN[:, 3 * 512:], NRM[:, 512:D], ALU.mult)
                pool.drain()
                pool.tensor_tensor(X[:, 3 * 512:], X[:, 3 * 512:], NRM[:, D + 512:2 * D], ALU.add)
                pool.drain().then_inc(ln_done, 1)

            pool.memset(ACC, 0.0).then_inc(acc_zero, 1)
            tables()
            for n in range(3):
                lo_part(n, 1)
            end_of_layer(pool, 0)
            with pool.Fori(0, DEPTH) as l:
                for n in range(3, N_W1S + 1):
                    lo_part(n, made(n))
                affine(1)
                lo_part(N_W1S + 2, made(N_W1S + 2))
                lo_part(N_W1S + 3, made(N_W1S + 3))
                pool.wait_ge(ln_done, 2)
                pool.wait_ge(h_ready, 8)
                pool.memset(ACC, 0.0).then_inc(acc_zero, 1)
                tables()
                lo_part(NUNIT, made(NUNIT))
                lo_part(NUNIT + 1, made(NUNIT + 1))
                lo_part(NUNIT + 2, made(NUNIT + 2))
                affine(2)
                end_of_layer(pool, l + 1)

        @block.scalar
        def _(act):
            def hi_part(n, k=0):
                act.wait_ge(raw_in[n % 2], 16 * (6 * k + loads(n)))
                act.wait_ge(used[n % 3], 4 * k + uses(n - 3))
                act.activation(WH[n % 3], RAW[n % 2], ACT.Copy).then_inc(hi_done[n % 3], 1)

            def step(times):
                act.wait_ge(ahead_in, 16 * times)
                act.activation(tiny("half"), AHEAD[:, AC["log_step"]], ACT.Exp).then_inc(step_exp, 1)

            def tables():
                act.wait_ge(turns_ready, 1)
                act.activation(S5D[:, 0:8], tiny("s5a"), ACT.Exp)
                act.activation(tiny("sin"), tiny("s5b"), ACT.Sin)
                act.activation(tiny("half"), tiny("s5b"), ACT.Sin, scale=0.5)
                act.drain().then_inc(trig_ready, 1)
                act.wait_ge(phase_ready, 1)
                act.activation(SIN, COS, ACT.Sin, scale=TWO_PI)
                act.drain()
                act.activation(COS, COS, ACT.Sin, scale=math.pi).then_inc(sines_ready, 1)

            def copy_sums():
                act.wait_ge(sums_ps, 1)
                act.activation(HT[:, 0:D], psum(6, 8), ACT.Copy).then_inc(sums_sb, 1)

            ht3 = HT.rearrange("p (k t) -> p k t", k=KD)

            def make_h(j, banks, quarters, transposed=0):
                for g in quarters:
                    if j or g < 2:
                        act.wait_ge(xt_ps, transposed + g + 1)
                    for dst in (hh, ht3) if g == 3 else (hh,):
                        for k in (2 * g, 2 * g + 1):
                            ins = act.activation(dst[:, k, :], PS[:, banks[g], k % 2 * S:k % 2 * S + S], ACT.Identity,
                                                 scale=sc4[:, j, 1, k:k + 1], bias=sc4[:, j, 0, k:k + 1])
                    ins.then_inc(h_hi, 1)

            step(1)
            act.wait_ge(angle_ready, 1)
            act.activation(ROPE[:, 16:32], tiny("rope_a"), ACT.Sin)
            act.activation(ROPE[:, 0:16], tiny("rope_a"), ACT.Sin, scale=0.5)
            act.drain().then_inc(angle_ready, 1)
            tables()
            for n in range(2):
                act.wait_ge(raw_in[n], 16)
                act.activation(WH[n], RAW[n], ACT.Copy).then_inc(hi_done[n], 1)
            copy_sums()
            act.wait_ge(sc_ready, 1)
            make_h(0, (4, 5, 6, 7), range(2))
            act.wait_ge(raw_in[0], 32)
            act.activation(WH[2], RAW[0], ACT.Copy).then_inc(hi_done[2], 1)
            end_of_layer(act, 0)

            with act.Fori(0, DEPTH) as l:
                def evacuate(name):
                    n, i = UNITS.index(name), turn(name)
                    act.wait_ge(used[n % 3], uses(n))
                    src = psum(i % 2)
                    src3 = src.rearrange("p (c t) -> p c t", c=2)
                    if name in ("P0", "P1"):
                        c0 = 2 * int(name[1])
                        ins = act.activation(cin3[:, c0:c0 + 2, 3:3 + S], src3, ACT.Copy)
                    elif name == "P5":
                        ins = act.activation(UT, src, ACT.Copy)
                    elif name == "P6":
                        ins = act.activation(V, src, ACT.Gelu_apprx_tanh)
                    elif name == "P7":
                        ins = act.activation(GU, src, ACT.Gelu_apprx_tanh)
                    elif name == "P8":
                        ins = act.activation(Z, src, ACT.Silu)
                    else:
                        g = int(name[1:])
                        ins = act.activation(SIG[:, g * 512:(g + 1) * 512], src, ACT.Tanh, scale=0.5)
                    ins.then_inc(turn_free[i % 2], 1)

                def branch_hi(i, src, scale=1.0):
                    if i:
                        act.wait_ge(y_used, i)
                    act.activation(YH[0], src, ACT.Copy, scale=scale).then_inc(y_hi, 1)

                def relu_index(b):
                    act.wait_ge(index_ps, b + 1)
                    act.activation(RL[b], psum(5) if b == 0 else psum(2, 4), ACT.Relu).then_inc(relu_sb, 1)

                def softmax_exp(b):
                    n = NKEY[b]
                    act.wait_ge(logit_max, b + 1)
                    for h in range(4):
                        act.activation(RL[b][:, h * n:(h + 1) * n], RL[b][:, h * n:(h + 1) * n], ACT.Exp,
                                       bias=tiny("neg", 4 * b + h, 4 * b + h + 1),
                                       accum_out=tiny("den", 4 * b + h, 4 * b + h + 1))
                    act.drain().then_inc(exp_ready, 1)

                make_h(0, (4, 5, 6, 7), range(2, 4))
                for name in ACT_ORDER:
                    if name == "silu_xbc":
                        act.wait_ge(conv_ready, 1)
                        act.activation(XBC, XBC, ACT.Silu).then_inc(xbc_ready, 1)
                    elif name == "softplus":
                        act.wait_ge(dt_abs, 1)
                        act.activation(tiny("dt_e"), tiny("dt_e"), ACT.Exp, scale=-1.0)
                        act.activation(tiny("exp_a"), par("a_log"), ACT.Exp)
                        act.drain()
                        act.activation(tiny("dt_e"), tiny("dt_e"), ACT.Ln, bias=1.0)
                        act.drain().then_inc(dt_log, 1)
                    elif name == "x_tok":
                        act.wait_ge(ssd1_ps, 1)
                        act.activation(XT, psum(2), ACT.Copy)
                        act.activation(BT, PS[:, 3, 0:P], ACT.Copy)
                        act.drain().then_inc(x_tok, 1)
                    elif name == "decay":
                        act.wait_ge(decay_log, 1)
                        act.activation(LM, LM, ACT.Exp)
                        act.activation(tiny("acum_e"), tiny("acum", 4, 8), ACT.Exp)
                        act.drain().then_inc(decay_exp, 1)
                    elif name == "state":
                        act.wait_ge(ssd3_ps, 1)
                        act.activation(ST, PS[:, 7, 0:P], ACT.Copy).then_inc(state_sb, 1)
                    elif name == "rms_root":
                        act.wait_ge(rms_sq, 1)
                        act.activation(tiny("ms"), tiny("ms"), ACT.Sqrt).then_inc(rms_root, 1)
                    elif name == "y0":
                        act.wait_ge(ssd5_ps, 1)
                        branch_hi(0, psum(6))
                    elif name == "v_root":
                        act.wait_ge(v_var, 1)
                        act.activation(tiny("mvg", 0, 2), tiny("mvg", 0, 2), ACT.Sqrt).then_inc(v_root, 1)
                    elif name == "qk_t":
                        act.wait_ge(att1_ps, 1)
                        act.activation(QT[:, 0:1024], psum(2, 4), ACT.Copy)
                        act.activation(QT[:, 1024:1536], psum(5), ACT.Copy)
                        act.drain().then_inc(qk_t, 1)
                    elif name == "y1":
                        act.wait_ge(gm_ready, 1)
                        branch_hi(1, V)
                    elif name == "relu":
                        relu_index(0)
                        relu_index(1)
                    elif name == "exp":
                        softmax_exp(0)
                        softmax_exp(1)
                    elif name == "prob_t":
                        act.wait_ge(att3_ps, 1)
                        act.activation(PT[0], psum(7), ACT.Copy).then_inc(prob_t, 1)
                        act.wait_ge(att3_ps, 2)
                        act.activation(PT[1], psum(5, 7), ACT.Copy).then_inc(prob_t, 1)
                    elif name == "y2":
                        act.wait_ge(att4_ps, 1)
                        branch_hi(2, psum(4))
                    elif name == "gelu":
                        act.wait_ge(s5y_ready, 1)
                        act.activation(B5[0], B5[0], ACT.Gelu_apprx_tanh).then_inc(s5_gelu, 1)
                    elif name == "tanh":
                        act.wait_ge(glu_ps, 1)
                        for c in range(CW):
                            act.activation(B5[1][:, c * S:(c + 1) * S], PS[:, 4, c * S:(c + 1) * S], ACT.Tanh,
                                           scale=0.5, bias=tiny("glu_hb", c, c + 1))
                        act.drain().then_inc(glu_tanh, 1)
                    elif name == "y3":
                        act.wait_ge(glu_ready, 1)
                        branch_hi(3, B5[2], 0.5)
                    if name[0] in "PG" and name not in ("P2", "P3", "P4"):
                        evacuate(name)
                    if name == "B3":
                        for g in range(4):
                            act.wait_ge(merged, g + 1)
                            act.activation(HH[:, g * 512:(g + 1) * 512], MG[:, g * 512:(g + 1) * 512], ACT.Copy,
                                           scale=0.5).then_inc(mix_hi, 1)
                    if name == "O2":
                        act.wait_ge(router_w_in, 16)
                        act.activation(RWH, RW, ACT.Copy).then_inc(router_hi, 1)
                    if name[0] in "PGBO" and UNITS.index(name) + 3 < N_W1S + 1:
                        hi_part(UNITS.index(name) + 3)

                def norm(i):
                    act.wait_ge(ln_var, 2 * i - 1)
                    act.activation(tiny("var", 0, 1), tiny("var", 0, 1), ACT.Sqrt).then_inc(ln_root, 1)
                    act.wait_ge(ln_scale, i)
                    act.activation(XN[:, 0:D], X[:, 0:D], ACT.Identity, scale=tiny("var", 0, 1), bias=tiny("shift")
                                   ).then_inc(xn0_ready, 1)
                    act.wait_ge(ln_var, 2 * i)
                    act.activation(tiny("var", 1, 2), tiny("var", 1, 2), ACT.Sqrt).then_inc(ln_root, 1)

                norm(1)
                make_h(1, (6, 7, 0, 1), range(4))
                hi_part(N_W1S + 1)
                hi_part(N_W1S + 2)
                act.wait_ge(route_ps, 1)
                act.activation(GT[0:E, :], PS[0:E, 3, 0:S], ACT.Sigmoid).then_inc(sig_ready, 1)
                step(1)

                def silu(x, k=0):
                    n = N_W1S - 1 + 3 * x if x else N_W1S
                    act.wait_ge(used[n % 3], 4 * k + uses(n))
                    if x > 1 or not isinstance(k, int):
                        act.wait_ge(b_read, 4 * k + x - 1)
                    act.activation(SL[x % 2], psum(4 + 2 * (x % 2)), ACT.Silu).then_inc(silu_done, 1)

                def activation_hi(x, k=0):
                    act.wait_ge(act_ready, 4 * k + x + 1)
                    act.wait_ge(used[1], 4 * k + uses(N_W1S + 1) - 1 + x)
                    act.activation(YH[x % 2], T[x % 2], ACT.Copy).then_inc(act_hi, 1)

                def four_experts(k):
                    for i in range(4):
                        n = N_W1S + 2 + 3 * i
                        hi_part(n + 1, k)
                        activation_hi(i, k)
                        hi_part(n + 2, k)
                        silu(i + 1, k)
                        hi_part(n + 3, k)

                silu(0)
                four_experts(0)
                tables()
                with act.Fori(1, KD) as k:
                    four_experts(k)
                hi_part(NUNIT)
                activation_hi(E)
                copy_sums()
                hi_part(NUNIT + 1)
                hi_part(NUNIT + 2)
                norm(2)
                act.wait_ge(sc_ready, 1)
                make_h(0, (4, 5, 6, 7), range(2), 4)
                end_of_layer(act, l + 1)

        @block.vector
        def _(dve):
            def lo_part(n, k=0):
                dve.wait_ge(hi_done[n % 3], 4 * k + made(n))
                dve.tensor_tensor(WL[n % 3], RAW[n % 2], WH[n % 3].bitcast(F32), ALU.subtract
                                  ).then_inc(lo_done[n % 3], 1)

            def reduce_angle(a, turns):
                dve.tensor_scalar(turns, a, 1 / TWO_PI, ROUND, ALU.mult, ALU.add)
                dve.drain()
                dve.tensor_scalar(turns, turns, ROUND, None, ALU.subtract)
                for part in (PI_A, PI_B, PI_C):
                    dve.drain()
                    dve.scalar_tensor_tensor(a, turns, -part, a, ALU.mult, ALU.add)
                dve.drain()

            lam_re, lam_im = AHEAD[:, AC["lam_re"]], AHEAD[:, AC["lam_im"]]
            decay, factor_re, factor_im = S5D[:, 0:8], S5D[:, 8:16], S5D[:, 16:24]

            def phase():
                a, b, cc = tiny("s5a"), tiny("s5b"), tiny("s5c")
                dve.wait_ge(step_exp, 1)
                dve.tensor_tensor(a, lam_re, tiny("half"), ALU.mult)
                dve.tensor_tensor(b, lam_im, tiny("half"), ALU.mult)
                dve.drain()
                reduce_angle(b, cc)
                dve.tensor_scalar(cc, b, 1 / TWO_PI, None, ALU.mult)
                dve.drain()
                dve.tensor_scalar(tiny("phi_hi"), cc, ROUND14, ROUND14, ALU.add, ALU.subtract)
                dve.drain()
                dve.tensor_tensor(tiny("phi_lo"), cc, tiny("phi_hi"), ALU.subtract)
                dve.drain().then_inc(turns_ready, 1)

            def factor():
                a, b, cc, d = tiny("s5a"), tiny("s5b"), tiny("s5c"), tiny("s5d")
                dve.wait_ge(trig_ready, 1)
                dve.tensor_tensor(a, tiny("half"), tiny("half"), ALU.mult)
                dve.drain()
                dve.tensor_scalar(a, a, -2.0, 1.0, ALU.mult, ALU.add)
                dve.tensor_tensor(b, tiny("sin"), decay, ALU.mult)
                dve.drain()
                dve.tensor_tensor(a, a, decay, ALU.mult)
                dve.tensor_tensor(cc, lam_re, lam_re, ALU.mult)
                dve.tensor_tensor(d, lam_im, lam_im, ALU.mult)
                dve.drain()
                dve.tensor_scalar(a, a, -1.0, None, ALU.add)
                dve.tensor_tensor(cc, cc, d, ALU.add)
                dve.drain()
                dve.reciprocal(cc, cc)
                dve.tensor_tensor(factor_re, a, lam_re, ALU.mult)
                dve.tensor_tensor(d, b, lam_im, ALU.mult)
                dve.tensor_tensor(factor_im, b, lam_re, ALU.mult)
                dve.tensor_tensor(a, a, lam_im, ALU.mult)
                dve.drain()
                dve.tensor_tensor(factor_re, factor_re, d, ALU.add)
                dve.tensor_tensor(factor_im, factor_im, a, ALU.subtract)
                dve.drain()
                dve.tensor_tensor(factor_re, factor_re, cc, ALU.mult)
                dve.tensor_tensor(factor_im, factor_im, cc, ALU.mult)
                dve.drain()

            def mod_half(k, i):
                dve.wait_ge(mod_in[i % 2], 16 * (2 * k + i // 2 + 1))
                half = acc3[:, i // 2, i % 2 * MODH:(i % 2 + 1) * MODH]
                dve.scalar_tensor_tensor(half, MODR[i % 2], CVEC[:, bass.ds(k, 1)], half, ALU.mult, ALU.add
                                         ).then_inc(mod_used[i % 2], 1)

            def make_columns(times):
                norm_g, norm_b = (AHEAD[:, AC[x]].rearrange("p (j k) -> p j k", j=2) for x in ("norm_g", "norm_b"))
                dve.wait_ge(ahead_in, 16 * times)
                dve.wait_ge(cols_ps, 1)
                dve.tensor_tensor(SC.rearrange("p (r k) -> p r k", r=4), psum(6, 8).rearrange(
                    "p (k r x) -> p r k x", k=KD, r=4)[:, :, :, 0], AHEAD[:, AC["mod_b"]].rearrange(
                        "p (r k) -> p r k", r=4), ALU.add)
                dve.drain()
                dve.tensor_scalar(sc4[:, :, 1, :], sc4[:, :, 1, :], 1.0, None, ALU.add)
                dve.drain()
                shifted = tiny("rope_b").rearrange("p (j k) -> p j k", j=2)
                dve.tensor_tensor(shifted, sc4[:, :, 1, :], norm_b, ALU.mult)
                dve.drain()
                dve.tensor_tensor(sc4[:, :, 1, :], sc4[:, :, 1, :], norm_g, ALU.mult)
                dve.tensor_tensor(sc4[:, :, 0, :], sc4[:, :, 0, :], shifted, ALU.add)
                dve.drain().then_inc(sc_ready, 1)
                dve.wait_ge(rows_ps, 1)
                dve.wait_ge(gate_b_in, 64)
                dve.scalar_tensor_tensor(GROW, psum(4), 1.0, GBR, ALU.add, ALU.add).then_inc(rows_sb, 1)

            def make_h(j, banks):
                ht3 = HT.rearrange("p (k t) -> p k t", k=KD)
                for g in range(4):
                    if j or g >= 2:
                        dve.wait_ge(h_hi, 2 + g + 1 if j else g - 1)
                    if g < 3:
                        for k in (2 * g, 2 * g + 1):
                            dve.tensor_scalar(ht3[:, k, :], PS[:, banks[g], k % 2 * S:k % 2 * S + S],
                                              sc4[:, j, 1, k:k + 1], sc4[:, j, 0, k:k + 1], ALU.mult, ALU.add)
                        dve.drain()
                    dve.tensor_tensor(HL[:, g * 512:(g + 1) * 512], HT[:, g * 512:(g + 1) * 512],
                                      HH[:, g * 512:(g + 1) * 512].bitcast(F32), ALU.subtract).then_inc(h_ready, 1)

            dve.wait_ge(const_in, 16)
            dve.wait_ge(pos_in, 16)
            dve.tensor_copy(RT[:, 2:4], RT[:, 0:NB].bitcast(I32))
            dve.drain()
            dve.tensor_tensor(tiny("rope_a").rearrange("p (b i) -> p b i", b=NB), wide(RT[:, 2:4], 8),
                              rep(con("inv"), NB), ALU.mult)
            dve.drain()
            reduce_angle(tiny("rope_a"), tiny("rope_b"))
            dve.drain().then_inc(angle_ready, 1)
            dve.wait_ge(ahead_in, 16)
            phase()
            dve.wait_ge(angle_ready, 2)
            dve.tensor_tensor(ROPE[:, 0:16], ROPE[:, 0:16], ROPE[:, 0:16], ALU.mult)
            dve.drain()
            dve.tensor_scalar(ROPE[:, 0:16], ROPE[:, 0:16], -2.0, 1.0, ALU.mult, ALU.add)
            dve.wait_ge(c_in, 16)
            dve.wait_ge(acc_zero, 1)
            with dve.Fori(0, KD // 2) as kk:
                for i in range(4):
                    sums = acc3[:, i % 2, :]
                    dve.drain()
                    dve.wait_ge(mod_in[i], 16 * (kk + 1))
                    dve.scalar_tensor_tensor(sums, STAGE[i], CVEC[:, bass.ds(2 * kk + i // 2, 1)], sums, ALU.mult,
                                             ALU.add).then_inc(mod_used[i], 1)
            factor()
            make_columns(1)
            end_of_layer(dve, 0)

            with dve.Fori(0, DEPTH) as l:
                make_h(0, (4, 5, 6, 7))

                def projection(name):
                    n, i = UNITS.index(name), turn(name)
                    dve.wait_ge(used[n % 3], uses(n))
                    return psum(i % 2).rearrange("p (b n) -> p b n", b=NB), turn_free[i % 2]

                dve.memset(cin3[:, :, 0:3], 0.0)
                dve.wait_ge(params_in, 16)
                dve.wait_ge(turn_free[0], 1)
                dve.wait_ge(turn_free[1], 1)
                dve.drain()
                for tap in range(4):
                    for c in range(4):
                        w = par("conv_w")[:, 4 * c + tap:4 * c + tap + 1]
                        src = cin3[:, c, tap:tap + S]
                        if tap == 0:
                            dve.tensor_scalar(xbc3[:, c, :], src, w, par("conv_b")[:, c:c + 1], ALU.mult, ALU.add)
                        else:
                            dve.scalar_tensor_tensor(xbc3[:, c, :], src, w, xbc3[:, c, :], ALU.mult, ALU.add)
                    dve.drain()
                dve.drain().then_inc(conv_ready, 1)

                src, free = projection("P2")
                dve.tensor_copy(misc3[:, :, 0:200], src[:, :, 0:200]).then_inc(free, 1)
                dve.drain()
                dt_v, dt_e = tiny("dt_v"), tiny("dt_e")
                dt_v3 = dt_v.rearrange("p (b h) -> p b h", b=NB)
                dve.tensor_tensor(dt_v3, misc3[:, :, 196:200], rep(par("dt_bias"), NB), ALU.add)
                dve.tensor_scalar(tiny("wi").rearrange("p (b h) -> p b h", b=NB), misc3[:, :, 192:196], 1 / 16, None,
                                  ALU.mult)
                dve.tensor_scalar(tiny("glu_hb"), par("glu_b"), 0.5, None, ALU.mult)
                dve.drain()
                dve.scalar_tensor_tensor(dt_e, dt_v, -1.0, dt_v, ALU.mult, ALU.max).then_inc(dt_abs, 1)
                for g in (8, 9):
                    dve.tensor_copy(qk4[:, :, g, :], misc3[:, :, 0:64])
                    dve.tensor_copy(qk4[:, :, g + 2, :], misc3[:, :, 128:192])
                def rope_source(name, g):
                    src, free = projection(name)
                    dve.tensor_copy(qk4[:, :, g:g + 4, :], src.rearrange("p b (g d) -> p b g d", g=4)).then_inc(free, 1)

                rope_source("P3", 0)
                dt, adt = tiny("dt"), tiny("adt")
                dve.wait_ge(dt_log, 1)
                dve.scalar_tensor_tensor(dt, dt_v, 0.0, dt_e, ALU.max, ALU.add)
                dve.drain()
                dve.scalar_tensor_tensor(adt.rearrange("p (b h) -> p b h", b=NB), dt.rearrange("p (b h) -> p b h", b=NB),
                                         -1.0, rep(tiny("exp_a"), NB), ALU.mult, ALU.mult)
                dve.drain().then_inc(adt_ready, 1)
                rope_source("P4", 4)
                dve.drain()
                cos, sin = (ROPE[:, a:a + 16].rearrange("p (b i) -> p b i", b=NB).unsqueeze(2)
                            .broadcast_to([P, NB, 12, 8]) for a in (0, 16))
                first, second = qk4[:, :, :, 0:8], qk4[:, :, :, 8:16]
                r = [WORK[:, 2304 + 192 * i:2496 + 192 * i].rearrange("p (b g i) -> p b g i", b=NB, g=12) for i in range(4)]
                dve.tensor_tensor(r[0], first, cos, ALU.mult)
                dve.tensor_tensor(r[1], second, sin, ALU.mult)
                dve.tensor_tensor(r[2], second, cos, ALU.mult)
                dve.tensor_tensor(r[3], first, sin, ALU.mult)
                dve.drain()
                dve.tensor_tensor(first, r[0], r[1], ALU.subtract)
                dve.tensor_tensor(second, r[2], r[3], ALU.add)
                dve.drain().then_inc(qk_ready, 1)

                dve.wait_ge(x_tok, 1)
                heads = lambda t, n: t.rearrange("p (h d) -> p h d", h=n)
                dve.tensor_tensor(heads(XDT, 8), heads(XT, 8), wide(dt, 64), ALU.mult)
                dve.tensor_tensor(YS.rearrange("p (b h d) -> p b h d", b=NB, h=4), XT.rearrange(
                    "p (b h d) -> p b h d", b=NB, h=4), wide(par("ssd_d"), 64).unsqueeze(1).broadcast_to(
                        [P, NB, 4, 64]), ALU.mult)
                dve.wait_ge(ssd2_ps, 1)
                dve.tensor_copy(tiny("acum"), PS[:, 4, 0:8])
                dve.drain()
                for bh in range(8):
                    dve.tensor_scalar(LM[:, bh * P:(bh + 1) * P], PS[:, 5 + bh // 4, bh % 4 * P:bh % 4 * P + P],
                                      tiny("acum", bh, bh + 1), 0.0, ALU.subtract, ALU.min)
                dve.drain().then_inc(decay_log, 1)
                dve.wait_ge(decay_exp, 1)
                dve.tensor_tensor(heads(DECX, 4), heads(XDT[:, 0:256], 4), heads(LM[:, 0:512], 4)[:, :, P - 1:P]
                                  .broadcast_to([P, 4, 64]), ALU.mult)
                dve.drain()
                dve.tensor_tensor(heads(LM, 8), heads(LM, 8), rep(con("upper"), 8), ALU.mult)
                dve.drain()
                dve.tensor_tensor(LM.rearrange("p (g j l) -> p g j l", g=4, j=2),
                                  LM.rearrange("p (g j l) -> p g j l", g=4, j=2),
                                  psum(7).rearrange("p (g l) -> p g l", g=4).unsqueeze(2).broadcast_to([P, 4, 2, P]),
                                  ALU.mult)
                dve.drain().then_inc(mask_ready, 1)
                def norm_stats(src, b, width, mv):
                    st = tiny("stats", 12 * b, 12 * b + 12)
                    for c in range(width // 512 or 1):
                        dve.bn_stats(st[:, 6 * c:6 * c + 6], src[:, 512 * c:512 * c + min(width, 512)])
                    dve.drain()
                    dve.bn_aggr(mv, st[:, 0:6 * (width // 512 or 1)])

                vi = turn("P6")
                dve.wait_ge(turn_free[vi % 2], vi // 2 + 1)
                for b in range(NB):
                    norm_stats(V[:, b * W:(b + 1) * W], b, W, tiny("mv", 2 * b, 2 * b + 2))
                dve.drain()
                means = tiny("mv").rearrange("p (b s) -> p b s", b=NB)
                dve.tensor_scalar(tiny("mvg", 0, 2), means[:, :, 1], EPS_LN, None, ALU.add)
                dve.drain().then_inc(v_var, 1)
                dve.wait_ge(v_root, 1)
                dve.reciprocal(tiny("mvg", 0, 2), tiny("mvg", 0, 2))
                dve.drain()
                for b in range(NB):
                    dve.tensor_scalar(V[:, b * W:(b + 1) * W], V[:, b * W:(b + 1) * W], tiny("mv", 2 * b, 2 * b + 1),
                                      tiny("mvg", b, b + 1), ALU.subtract, ALU.mult)
                dve.drain()
                dve.tensor_tensor(heads(V, 2), heads(V, 2), rep(par("gm_g"), 2), ALU.mult)
                dve.drain()
                dve.tensor_tensor(heads(V, 2), heads(V, 2), rep(par("gm_b"), 2), ALU.add)
                dve.tensor_tensor(heads(par("sg_w"), 4), heads(par("sg_w"), 4), rep(con("upper"), 4), ALU.mult)
                dve.drain().then_inc(v_ready, 1)

                def branch_lo(i, src, scale=None):
                    dve.wait_ge(y_hi, i + 1)
                    if scale is None:
                        ins = dve.tensor_tensor(YL[0], src, YH[0].bitcast(F32), ALU.subtract)
                    else:
                        ins = dve.scalar_tensor_tensor(YL[0], src, scale, YH[0].bitcast(F32), ALU.mult, ALU.subtract)
                    ins.then_inc(y_lo, 1)

                def mix_lo(g):
                    at = slice(g * 512, (g + 1) * 512)
                    dve.wait_ge(mix_hi, g + 1)
                    dve.scalar_tensor_tensor(HL[:, at], MG[:, at], 0.5, HH[:, at].bitcast(F32), ALU.mult,
                                             ALU.subtract).then_inc(mix_ready, 1)

                def merge(i):
                    for part in range(4):
                        t, gate = turn(f"B{i}", part), turn(f"G{4 * i + part}")
                        dve.wait_ge(turn_free[gate % 2], gate // 2 + 1)
                        sig = SIG[:, (4 * i + part) * 512:(4 * i + part + 1) * 512]
                        mg = MG[:, part * 512:(part + 1) * 512]
                        dve.wait_ge(branch_ps, 4 * i + part + 1)
                        dve.scalar_tensor_tensor(V if i else mg, sig, 1.0, psum(t % 2), ALU.add, ALU.mult
                                                 ).then_inc(turn_free[t % 2], 1)
                        dve.drain()
                        if i:
                            ins = dve.tensor_tensor(mg, mg, V, ALU.add)
                            if i == 3:
                                ins.then_inc(merged, 1)
                            dve.drain()
                        if i == 3 and part:
                            mix_lo(part - 1)

                dve.wait_ge(gm_ps, 1)
                dve.tensor_tensor(V.rearrange("p (c b t) -> p c b t", c=2, b=NB), psum(6).rearrange(
                    "p (c b t) -> p c b t", c=2, b=NB), heads(par("sg_b"), 2).unsqueeze(2).broadcast_to([P, 2, NB, P]),
                    ALU.add)
                dve.drain()
                ui = turn("P7")
                dve.wait_ge(turn_free[ui % 2], ui // 2 + 1)
                dve.tensor_tensor(V, V, GU, ALU.mult).then_inc(gm_ready, 1)
                def score(b):
                    n, s, left = NKEY[b], SCORE[b], LEFT[b]
                    dve.wait_ge(relu_sb, b + 1)
                    for h in range(4):
                        w = tiny("wi", 4 * b + h, 4 * b + h + 1)
                        rl = RL[b][:, h * n:(h + 1) * n]
                        if h == 0:
                            dve.tensor_scalar(s, rl, w, None, ALU.mult)
                        else:
                            dve.scalar_tensor_tensor(s, rl, w, s, ALU.mult, ALU.add)
                        dve.drain()
                    late_keys = s[:, n - P:n]
                    dve.tensor_tensor(late_keys, late_keys, con("lower"), ALU.mult)
                    dve.drain()
                    dve.tensor_tensor(late_keys, late_keys, con("floor"), ALU.add)
                    dve.drain()
                    src = s
                    for _ in range(NSEL // 8):
                        dve.max(tiny("top"), src)
                        dve.drain()
                        dve.match_replace(left, tiny("top"), src, TAKEN)
                        dve.drain()
                        src = left
                    dve.tensor_tensor(left, left, s, ALU.not_equal)
                    dve.drain()
                    dve.tensor_tensor(left[:, n - P:n], left[:, n - P:n], con("lower"), ALU.mult)
                    dve.drain()
                    dve.tensor_scalar(left, left, -1.0, AWAY, ALU.add, ALU.mult)
                    dve.drain()

                def masked_logits(b):
                    n = NKEY[b]
                    dve.wait_ge(logit_ps, b + 1)
                    lg = psum(5) if b == 0 else psum(2, 4)
                    dve.scalar_tensor_tensor(heads(RL[b], 4), heads(lg, 4), 0.125, rep(LEFT[b], 4), ALU.mult, ALU.add)
                    dve.drain()
                    neg = tiny("neg", 4 * b, 4 * b + 4)
                    dve.tensor_reduce(neg, heads(RL[b], 4), AX.X, ALU.max)
                    dve.drain()
                    dve.tensor_scalar(neg, neg, -1.0, None, ALU.mult)
                    dve.drain().then_inc(logit_max, 1)

                def probabilities(b):
                    den = tiny("den", 4 * b, 4 * b + 4)
                    dve.wait_ge(exp_ready, b + 1)
                    dve.reciprocal(den, den)
                    dve.drain()
                    dve.tensor_tensor(heads(RL[b], 4), heads(RL[b], 4), wide(den, NKEY[b]), ALU.mult
                                      ).then_inc(prob_ready, 1)

                score(0)
                dve.wait_ge(ssd3_ps, 1)
                dve.tensor_tensor(YS, YS, psum(4), ALU.add)
                dve.wait_ge(ssd4_ps, 1)
                dve.tensor_tensor(heads(XDT[:, 0:256], 4), heads(PS[:, 7, 0:256], 4), wide(tiny("acum_e"), 64), ALU.mult)
                dve.drain()
                dve.tensor_tensor(YS[:, 256:512], YS[:, 256:512], XDT[:, 0:256], ALU.add)
                dve.drain()
                zi = turn("P8")
                dve.wait_ge(turn_free[zi % 2], zi // 2 + 1)
                dve.tensor_tensor(YS, YS, Z, ALU.mult)
                dve.drain()
                dve.tensor_tensor(XDT, YS, YS, ALU.mult)
                dve.drain()
                dve.tensor_reduce(tiny("ms"), heads(XDT, 4), AX.X, ALU.add)
                dve.drain()
                dve.tensor_scalar(tiny("ms"), tiny("ms"), 1 / 128, EPS_RMS, ALU.mult, ALU.add).then_inc(rms_sq, 1)
                dve.wait_ge(rms_root, 1)
                dve.reciprocal(tiny("ms"), tiny("ms"))
                dve.drain()
                dve.tensor_tensor(heads(YS, 4), heads(YS, 4), wide(tiny("ms"), P), ALU.mult)
                dve.drain()
                dve.tensor_tensor(heads(YS, 2), heads(YS, 2), rep(par("norm_g"), 2), ALU.mult)
                dve.drain().then_inc(ssd_ready, 1)

                score(1)
                branch_lo(0, psum(6))
                merge(0)
                masked_logits(0)
                masked_logits(1)
                probabilities(0)
                probabilities(1)
                branch_lo(1, V)

                s5c = par("s5_c").rearrange("p (r j c) -> p r j c", r=2, j=8)
                fre, fim = (wide(S5D[:, a:a + 8], 32) for a in (8, 16))
                t0, t1 = (B5[i][:, 0:256].rearrange("p (j c) -> p j c", j=8) for i in (0, 1))
                cre, cim = (t.rearrange("p (j c) -> p j c", j=8) for t in (CRE, CIM))
                dve.wait_ge(ssd5_ps, 1)
                dve.tensor_tensor(t0, s5c[:, 0], fre, ALU.mult)
                dve.tensor_tensor(t1, s5c[:, 1], fim, ALU.mult)
                dve.drain()
                dve.tensor_tensor(cre, t0, t1, ALU.subtract)
                dve.drain()
                dve.tensor_tensor(t0, s5c[:, 0], fim, ALU.mult)
                dve.tensor_tensor(t1, s5c[:, 1], fre, ALU.mult)
                dve.drain()
                dve.scalar_tensor_tensor(CIM, B5[0][:, 0:256], -1.0, B5[1][:, 0:256], ALU.mult, ALU.subtract)
                dve.drain().then_inc(c_ready, 1)

                def quarter(i):
                    cos, sin = COS[:, 512 * i:512 * i + 512], SIN[:, 512 * i:512 * i + 512]
                    vre, vim = (psum(2), psum(3)) if i % 2 == 0 else (psum(5), psum(6))
                    dve.wait_ge(s5v_ps, i + 1)
                    dve.tensor_tensor(B5[0], vre, cos, ALU.mult)
                    dve.tensor_tensor(B5[1], vim, sin, ALU.mult)
                    dve.tensor_tensor(B5[2], vim, cos, ALU.mult)
                    dve.tensor_tensor(B5[3], vre, sin, ALU.mult).then_inc(s5v_read, 1)
                    dve.drain()
                    dve.tensor_tensor(B5[0], B5[0], B5[1], ALU.add)
                    dve.tensor_tensor(B5[2], B5[2], B5[3], ALU.subtract)
                    dve.drain()
                    for src, dst in ((B5[0], B5[1]), (B5[2], B5[3])):
                        for c in range(2):
                            at = slice(c * S, (c + 1) * S)
                            j = 2 * i + c
                            dve.tensor_tensor_scan(dst[:, at], S5D[:, j:j + 1].broadcast_to([P, S]), src[:, at], 0.0,
                                                   ALU.mult, ALU.add)
                    dve.drain()
                    if i:
                        dve.wait_ge(s5y_ps, i)
                    dve.tensor_tensor(B5[0], B5[1], cos, ALU.mult)
                    dve.tensor_tensor(B5[2], B5[3], sin, ALU.mult)
                    dve.drain()
                    dve.tensor_tensor(B5[4], B5[0], B5[2], ALU.subtract)
                    dve.drain()
                    dve.tensor_tensor(B5[0], B5[3], cos, ALU.mult)
                    dve.tensor_tensor(B5[2], B5[1], sin, ALU.mult)
                    dve.drain()
                    dve.tensor_tensor(B5[5], B5[0], B5[2], ALU.add)
                    dve.drain().then_inc(s5h_ready, 1)

                quarter(0)
                merge(1)
                branch_lo(2, psum(4))
                quarter(1)
                quarter(2)
                merge(2)
                quarter(3)
                dve.wait_ge(s5y_ps, 4)
                for c in range(CW):
                    at = slice(c * S, (c + 1) * S)
                    dve.scalar_tensor_tensor(B5[0][:, at], UT[:, at], par("s5_d")[:, c:c + 1], PS[:, 7, at], ALU.mult,
                                             ALU.add)
                dve.drain().then_inc(s5y_ready, 1)
                dve.wait_ge(glu_tanh, 1)
                dve.scalar_tensor_tensor(B5[2], B5[1], 1.0, B5[0], ALU.add, ALU.mult)
                dve.drain().then_inc(glu_ready, 1)
                branch_lo(3, B5[2], 0.5)
                merge(3)
                mix_lo(3)

                def norm(i, bank, done):
                    def gated(b):
                        at = slice(b * D, (b + 1) * D)
                        dve.tensor_tensor(LNT[:, at], psum(bank + 2 * b, bank + 2 * b + 2), NRM[:, 2 * D:3 * D], ALU.mult)

                    def residual(b):
                        at = slice(b * D, (b + 1) * D)
                        dve.drain()
                        dve.scalar_tensor_tensor(X[:, at], X[:, at], ALPHA, LNT[:, at], ALU.mult, ALU.add)
                        dve.drain()
                        norm_stats(X[:, at], b, D, tiny("mv", 2 * b, 2 * b + 2))
                        dve.drain()
                        dve.tensor_scalar(tiny("var", b, b + 1), tiny("mv", 2 * b + 1, 2 * b + 2), EPS_LN, None, ALU.add
                                          ).then_inc(ln_var, 1)

                    dve.wait_ge(norm_in, 48 * i)
                    dve.wait_ge(done, 1)
                    gated(0)
                    residual(0)
                    dve.wait_ge(done, 2)
                    gated(1)
                    dve.wait_ge(ln_root, 2 * i - 1)
                    dve.reciprocal(tiny("var", 0, 1), tiny("var", 0, 1))
                    dve.drain()
                    dve.scalar_tensor_tensor(tiny("shift"), tiny("mv", 0, 1), -1.0, tiny("var", 0, 1), ALU.mult, ALU.mult
                                             ).then_inc(ln_scale, 1)
                    residual(1)
                    dve.wait_ge(ln_root, 2 * i)
                    dve.reciprocal(tiny("var", 1, 2), tiny("var", 1, 2))
                    dve.drain()
                    dve.tensor_scalar(XN[:, D:2 * D], X[:, D:2 * D], tiny("mv", 2, 3), tiny("var", 1, 2),
                                      ALU.subtract, ALU.mult).then_inc(xn1_ready, 1)

                def affine(i):
                    dve.wait_ge(xn0_ready, i)
                    for op, a in ((ALU.mult, 0), (ALU.add, D)):
                        src = XN if op == ALU.mult else X
                        dve.drain()
                        dve.tensor_tensor(X[:, 0:D], src[:, 0:D], NRM[:, a:a + D], op)
                        dve.tensor_tensor(X[:, D:3 * 512], src[:, D:3 * 512], NRM[:, a:a + 512], op)
                    dve.drain().then_inc(ln_done, 1)

                norm(1, 2, wout_ps)
                dve.wait_ge(router_hi, 1)
                dve.tensor_tensor(RWL, RW, RWH.bitcast(F32), ALU.subtract).then_inc(router_ready, 1)
                make_h(1, (6, 7, 0, 1))
                lo_part(N_W1S + 1)
                affine(1)

                sig, biased, left = RT[:, 0:64], RT[:, 64:128], RT[:, 128:192]
                m4 = lambda t: t.rearrange("p (g i) -> p g i", i=4)
                hi2, lo2 = RT[:, 192:224], RT[:, 224:256]
                s2 = lambda t: t.rearrange("p (g i) -> p g i", i=2)
                best, second_, both = RT[:, 256:272], RT[:, 272:288], RT[:, 288:304]
                better, equal = RT[:, 320:448], RT[:, 448:576]
                g8 = lambda t: t.rearrange("p (b i) -> p b i", b=NB)
                g88 = lambda t: t.rearrange("p (b i j) -> p b i j", b=NB, i=8)
                dve.wait_ge(sig_ps, 1)
                dve.tensor_copy(sig, PS[:, 2, 0:64])
                dve.tensor_tensor(g8(biased), g8(PS[:, 2, 0:64]), rep(ROUT, NB), ALU.add)
                dve.drain()
                dve.tensor_tensor(s2(hi2), m4(biased)[:, :, 0:2], m4(biased)[:, :, 2:4], ALU.max)
                dve.tensor_tensor(s2(lo2), m4(biased)[:, :, 0:2], m4(biased)[:, :, 2:4], ALU.min)
                dve.drain()
                dve.tensor_tensor(best, s2(hi2)[:, :, 0], s2(hi2)[:, :, 1], ALU.max)
                dve.tensor_tensor(second_, s2(hi2)[:, :, 0], s2(hi2)[:, :, 1], ALU.min)
                dve.tensor_tensor(both, s2(lo2)[:, :, 0], s2(lo2)[:, :, 1], ALU.max)
                dve.drain()
                dve.tensor_tensor(second_, second_, both, ALU.max)
                dve.drain()
                dve.tensor_tensor(both, best, second_, ALU.add)
                dve.drain()
                mine = g8(both).unsqueeze(3).broadcast_to([P, NB, 8, 8])
                other = g8(both).unsqueeze(2).broadcast_to([P, NB, 8, 8])
                dve.tensor_tensor(g88(better), other, mine, ALU.is_gt)
                dve.tensor_tensor(g88(equal), other, mine, ALU.is_equal)
                dve.drain()
                dve.tensor_tensor(g8(equal), g8(equal), rep(con("before"), NB), ALU.mult)
                dve.drain()
                dve.tensor_tensor(better, better, equal, ALU.add)
                dve.drain()
                dve.tensor_reduce(best, better.rearrange("p (g j) -> p g j", j=8), AX.X, ALU.add)
                dve.drain()
                dve.tensor_scalar(best, best, 3.5, None, ALU.is_lt)
                dve.drain()
                dve.tensor_scalar(second_, best, -1.0, AWAY, ALU.add, ALU.mult)
                dve.tensor_tensor(m4(biased), m4(biased), wide(best, 4), ALU.mult)
                dve.drain()
                dve.tensor_tensor(m4(biased), m4(biased), wide(second_, 4), ALU.add)
                dve.drain()
                for b in range(NB):
                    dve.max(tiny("top"), biased[:, b * E:(b + 1) * E])
                    dve.drain()
                    dve.match_replace(left[:, b * E:(b + 1) * E], tiny("top"), biased[:, b * E:(b + 1) * E], TAKEN)
                    dve.drain()
                dve.tensor_tensor(left, left, biased, ALU.not_equal)
                dve.drain()
                dve.tensor_tensor(left, left, sig, ALU.mult)
                dve.drain()
                dve.tensor_reduce(best[:, 0:2], g8(left), AX.X, ALU.add)
                dve.drain()
                dve.reciprocal(best[:, 0:2], best[:, 0:2])
                dve.drain()
                for b in range(NB):
                    dve.tensor_scalar(left[:, b * E:(b + 1) * E], left[:, b * E:(b + 1) * E], best[:, b:b + 1], 2.5,
                                      ALU.mult, ALU.mult)
                dve.memset(G[0], 1.0)
                dve.drain().then_inc(gates_ready, 1)

                def products(x, k, n):
                    dve.wait_ge(silu_done, 4 * k + x + 1)
                    dve.wait_ge(used[n % 3], 4 * k + uses(n))
                    dve.tensor_tensor(T[x % 2], SL[x % 2], psum(5 + 2 * (x % 2)), ALU.mult).then_inc(b_read, 1)
                    dve.drain()
                    if n != N_W1S + 1:
                        dve.wait_ge(g_in[x % 2], 16 * (2 * k + (x + 1) // 2))
                    dve.tensor_tensor(heads(T[x % 2], 2), heads(T[x % 2], 2), rep(G[x % 2], 2), ALU.mult
                                      ).then_inc(act_ready, 1)
                    dve.drain()

                def activation_lo(x, k=0):
                    dve.wait_ge(act_hi, 4 * k + x + 1)
                    dve.tensor_tensor(YL[x % 2], T[x % 2], YH[x % 2].bitcast(F32), ALU.subtract).then_inc(act_lo, 1)

                def four_experts(k):
                    for i in range(4):
                        n = N_W1S + 2 + 3 * i
                        if i or not isinstance(k, int):
                            lo_part(n + 1, k)
                        activation_lo(i, k)
                        lo_part(n + 2, k)
                        products(i + 1, k, n + 1)
                        lo_part(n + 3, k)
                        if i == 0 and isinstance(k, int):
                            dve.wait_ge(acc_zero, 1)
                        mod_half(k, i)

                products(0, 0, N_W1S + 1)
                dve.wait_ge(gates_ps, 1)
                dve.tensor_copy(GT[0:E, :], PS[0:E, 2, 0:S]).then_inc(gates_sb, 1)
                phase()
                four_experts(0)
                factor()
                with dve.Fori(1, KD) as k:
                    four_experts(k)
                activation_lo(E)
                make_columns(1)
                norm(2, 0, moe_ps)
                affine(2)
                end_of_layer(dve, l + 1)

        @block.tensor
        def _(pe):
            def product(out, parts, first=True, last=True):
                total = 3 * len(parts)
                done = 0
                for (wh, wl), (mh, ml) in parts:
                    for a, b in ((wh, mh), (wl, mh), (wh, ml)):
                        ins = pe.matmul(out, a, b, start=first and done == 0, stop=last and done == total - 1)
                        done += 1
                return ins

            def slot(n, k=0):
                if n >= 3:
                    pe.wait_ge(lo_done[n % 3], 4 * k + made(n))
                return WH[n % 3], WL[n % 3]

            def h_times(out, wh, wl, h_from=None):
                for k in range(KD):
                    if h_from is not None and k % 2 == 0:
                        pe.wait_ge(h_ready, h_from + k // 2 + 1)
                    ins = product(out, [((wh[:, k, :], wl[:, k, :]), (hh[:, k, :], hl[:, k, :]))], k == 0, k == KD - 1)
                return ins

            def by_channel(out, wh, wl, h_from=None):
                wh, wl = (t.rearrange("p (k n) -> p k n", k=KD) for t in (wh, wl))
                for m in range(2):
                    at = slice(m * P, (m + 1) * P)
                    ins = h_times(out[:, m * S:(m + 1) * S], wh[:, :, at], wl[:, :, at], None if m else h_from)
                return ins

            def by_token(out, wh, wl, n=W):
                w = [t.rearrange("p (k n) -> p k n", k=KD) for t in (wh, wl)]
                for b in range(NB):
                    ins = product(out[:, b * n:(b + 1) * n],
                                  [((hh[:, k, b * P:(b + 1) * P], hl[:, k, b * P:(b + 1) * P]),
                                    (w[0][:, k, :], w[1][:, k, :])) for k in range(KD)])
                return ins

            def transpose_x(src, b, banks):
                by_k = src.rearrange("p (b q k) -> p b k q", b=NB, k=KD)
                for g in range(4):
                    for k in (2 * g, 2 * g + 1):
                        at = k % 2 * S + b * P
                        ins = pe.transpose(PS[:, banks[g], at:at + P], by_k[:, b, k, :], con("ident"))
                    if b == NB - 1:
                        ins.then_inc(xt_ps, 1)

            def sum_modulations():
                ones = con("ones")[:, 0:32]
                for half in range(2):
                    for r in range(4):
                        at = r % 2 * D + half * 512
                        ins = pe.matmul(PS[32 * r:32 * r + 32, 6 + half, :], ones, acc3[:, r // 2, at:at + 512],
                                        start=True, stop=True)
                ins.then_inc(sums_ps, 1)
                for r in range(4):
                    at = 2 * D + r % 2 * 512
                    ins = pe.matmul(PS[32 * r:32 * r + 32, 4, :], ones, acc3[:, r // 2, at:at + 512],
                                    start=True, stop=True)
                ins.then_inc(rows_ps, 1)
                pe.wait_ge(sums_sb, 1)
                sums = HT[:, 0:D].rearrange("p (q k) -> p k q", k=KD)
                for k in range(KD):
                    ins = pe.transpose(PS[:, 6 + k // 4, k % 4 * P:k % 4 * P + P], sums[:, k, :], con("ident"))
                ins.then_inc(cols_ps, 1)

            for i in range(4):
                pe.wait_ge(mod_used[i], KD // 2)
            sum_modulations()
            pe.wait_ge(sc_ready, 1)
            pe.wait_ge(rows_sb, 1)
            pe.wait_ge(x_in, 16)
            for b in range(NB):
                transpose_x(X, b, (4, 5, 6, 7))
            end_of_layer(pe, 0)
            with pe.Fori(0, DEPTH) as l:
                def xbc_t(c, b):
                    return xbc3[:, c, b * P:(b + 1) * P]

                def qk_rows(chunk, h, a, n):
                    return QT[64 * (h % 2):64 * (h % 2) + 64, chunk * S + a:chunk * S + a + n]

                def heads_by_rows(queries, keys, done):
                    for half in range(2):
                        pe.drain()
                        for h in (half, half + 2):
                            ins = pe.matmul(PS[:, 5, h * P:(h + 1) * P], qk_rows(queries + h // 2, h, 0, P),
                                            qk_rows(keys, h, 0, P), start=True, stop=True)
                        if half:
                            ins.then_inc(done, 1)
                        for h in (half, half + 2):
                            ins = pe.matmul(PS[:, 2 + h // 2, h % 2 * S:h % 2 * S + S],
                                            qk_rows(queries + h // 2, h, P, P), qk_rows(keys, h, 0, S),
                                            start=True, stop=True)
                        if half:
                            ins.then_inc(done, 1)

                def small(name):
                    if name == "ssd1":
                        pe.wait_ge(xbc_ready, 1)
                        for b in range(NB):
                            for c in range(2):
                                pe.transpose(PS[:, 2, b * W + c * P:b * W + (c + 1) * P], xbc_t(c, b), con("ident"))
                        pe.transpose(PS[:, 3, 0:P], xbc_t(2, 0), con("ident")).then_inc(ssd1_ps, 1)
                    elif name == "ssd2":
                        pe.wait_ge(adt_ready, 1)
                        for b in range(NB):
                            pe.matmul(PS[:, 4, 4 * b:4 * b + 4], con("upper"), tiny("adt", 4 * b, 4 * b + 4),
                                      start=True, stop=True)
                            for h in range(4):
                                pe.matmul(PS[:, 5 + b, h * P:(h + 1) * P],
                                          tiny("adt", 4 * b + h, 4 * b + h + 1).broadcast_to([P, P]), con("upper"),
                                          start=True, stop=True)
                        for g in range(2):
                            pe.drain()
                            rows = slice(64 * g, 64 * g + 64)
                            for b in range(NB):
                                ins = pe.matmul(PS[:, 7, (2 * b + g) * P:(2 * b + g + 1) * P],
                                                xbc3[rows, 2, b * P:(b + 1) * P], xbc3[rows, 3, b * P:(b + 1) * P],
                                                start=True, stop=True)
                        ins.then_inc(ssd2_ps, 1)
                    elif name == "ssd3":
                        pe.wait_ge(mask_ready, 1)
                        for bh in range(8):
                            pe.matmul(PS[:, 4, bh * 64:(bh + 1) * 64], LM[:, bh * P:(bh + 1) * P],
                                      XDT[:, bh * 64:(bh + 1) * 64], start=True, stop=True)
                        for h in range(4):
                            g = h // 2
                            ins = pe.matmul(PS[64 * g:64 * g + 64, 7, h % 2 * 64:h % 2 * 64 + 64],
                                            BT[:, 64 * g:64 * g + 64], DECX[:, h * 64:(h + 1) * 64],
                                            start=True, stop=True)
                        ins.then_inc(ssd3_ps, 1)
                    elif name == "ssd4":
                        pe.wait_ge(state_sb, 1)
                        for h in range(4):
                            if h % 2 == 0:
                                pe.drain()
                            rows = slice(64 * (h // 2), 64 * (h // 2) + 64)
                            ins = pe.matmul(PS[:, 7, h * 64:(h + 1) * 64], xbc3[rows, 3, P:S],
                                            ST[rows, h % 2 * 64:h % 2 * 64 + 64], start=True, stop=True)
                        ins.then_inc(ssd4_ps, 1)
                    elif name == "ssd5":
                        pe.wait_ge(ssd_ready, 1)
                        for b in range(NB):
                            for c in range(CW):
                                ins = pe.transpose(PS[:, 6, c * S + b * P:c * S + (b + 1) * P],
                                                   YS[:, b * W + c * P:b * W + (c + 1) * P], con("ident"))
                        ins.then_inc(ssd5_ps, 1)
                    elif name == "att1":
                        pe.wait_ge(qk_ready, 1)
                        pe.wait_ge(x_tok, 1)
                        pe.wait_ge(decay_log, 1)
                        for c in range(6):
                            for b in range(NB):
                                bank = (2, 2, 3, 3, 5, 5)[c]
                                at = c % 2 * S + b * P
                                ins = pe.transpose(PS[:, bank, at:at + P],
                                                   QK[:, b * 768 + c * P:b * 768 + (c + 1) * P], con("ident"))
                        ins.then_inc(att1_ps, 1)
                    elif name == "gm":
                        pe.wait_ge(v_ready, 1)
                        for b in range(NB):
                            for g in range(4):
                                at = g // 2 * S + b * P
                                ins = pe.matmul(PS[64 * (g % 2):64 * (g % 2) + 64, 6, at:at + P],
                                                V[:, b * W + g * 64:b * W + (g + 1) * 64],
                                                par("sg_w")[:, g * P:(g + 1) * P], start=True, stop=True)
                        ins.then_inc(gm_ps, 1)
                    elif name == "index":
                        pe.wait_ge(qk_t, 1)
                        heads_by_rows(2, 5, index_ps)
                    elif name == "logits":
                        pe.wait_ge(relu_sb, 2)
                        heads_by_rows(0, 4, logit_ps)
                    elif name == "att3":
                        pe.wait_ge(prob_ready, 1)
                        for h in range(4):
                            ins = pe.transpose(PS[:, 7, h * P:(h + 1) * P], RL[0][:, h * P:(h + 1) * P], con("ident"))
                        ins.then_inc(att3_ps, 1)
                        pe.wait_ge(prob_ready, 2)
                        for i in range(8):
                            ins = pe.transpose(PS[:, 5 + i // 4, i % 4 * P:i % 4 * P + P], RL[1][:, i * P:(i + 1) * P],
                                               con("ident"))
                        ins.then_inc(att3_ps, 1)
                    elif name == "att4":
                        pe.wait_ge(prob_t, 2)
                        for h in range(4):
                            rows = slice(64 * (h % 2), 64 * (h % 2) + 64)
                            for b in range(NB):
                                out_ = PS[rows, 4, h // 2 * S + b * P:h // 2 * S + (b + 1) * P]
                                for s in range(b + 1):
                                    prob = PT[b][:, (h * (b + 1) + s) * P:(h * (b + 1) + s + 1) * P]
                                    ins = pe.matmul(out_, misc3[:, s, 64:128], prob, start=s == 0, stop=s == b)
                        ins.then_inc(att4_ps, 1)
                    elif name == "glu":
                        pe.wait_ge(s5_gelu, 1)
                        glu = par("glu_w").rearrange("p (k n) -> p k n", k=2)
                        for c in range(CW):
                            for k in range(CW):
                                ins = pe.matmul(PS[:, 4, c * S:(c + 1) * S], glu[:, k, c * P:(c + 1) * P],
                                                B5[0][:, k * S:(k + 1) * S], start=k == 0, stop=k == CW - 1)
                        ins.then_inc(glu_ps, 1)

                def s5_input(i):
                    if i >= 2:
                        pe.wait_ge(s5v_read, i - 1)
                    s5b = par("s5_b").rearrange("p (r c n) -> p r c n", r=2, c=2)
                    for cc in range(2):
                        pe.drain()
                        for part in range(2):
                            j = 2 * i + cc
                            rows, c = slice(32 * (j % 4), 32 * (j % 4) + 32), j // 4
                            ins = pe.matmul(PS[:, (2 if i % 2 == 0 else 5) + part, cc * S:(cc + 1) * S],
                                            s5b[rows, part, c, :], UT[rows, c * S:(c + 1) * S], start=True, stop=True)
                    ins.then_inc(s5v_ps, 1)

                def s5_output(i):
                    if i == 0:
                        pe.wait_ge(c_ready, 1)
                    pe.wait_ge(s5h_ready, i + 1)
                    for cc in range(2):
                        j = 2 * i + cc
                        out_ = PS[32 * (j % 4):32 * (j % 4) + 32, 7, j // 4 * S:(j // 4 + 1) * S]
                        at = slice(cc * S, (cc + 1) * S)
                        pe.matmul(out_, CRE[:, 32 * j:32 * j + 32], B5[4][:, at], start=True, stop=False)
                        ins = pe.matmul(out_, CIM[:, 32 * j:32 * j + 32], B5[5][:, at], start=False, stop=True)
                    ins.then_inc(s5y_ps, 1)

                for name in ORDER:
                    if name[:2] == "s5":
                        i = int(name[2])
                        if i == 0:
                            pe.wait_ge(turn_free[turn("P5") % 2], turn("P5") // 2 + 1)
                            s5_input(0)
                            s5_input(1)
                        else:
                            s5_output(i - 1)
                            if i < 3:
                                s5_input(i + 1)
                        continue
                    if name[0] not in "PGBO":
                        small(name)
                        continue
                    n = UNITS.index(name)
                    if name[0] in "PG":
                        i = turn(name)
                        turn_wait(pe, i)
                        tok = name in ("P2", "P3", "P4", "P6", "P8")
                        wh, wl = slot(n)
                        if tok:
                            ins = by_token(psum(i % 2), wh, wl)
                        else:
                            ins = by_channel(psum(i % 2), wh, wl, 0 if name == "P0" else None)
                        ins.then_inc(used[n % 3], 1)
                    elif name[0] == "B":
                        bi = int(name[1])
                        wh, wl = (t.rearrange("p (k n) -> p k n", k=CW) for t in slot(n))
                        pe.wait_ge(y_lo, bi + 1)
                        for part in range(4):
                            i = turn(name, part)
                            turn_wait(pe, i)
                            for m in range(2):
                                at = slice((2 * part + m) * P, (2 * part + m + 1) * P)
                                ins = product(PS[:, i % 2, m * S:(m + 1) * S],
                                              [((wh[:, k, at], wl[:, k, at]),
                                                (YH[0][:, k * S:(k + 1) * S], YL[0][:, k * S:(k + 1) * S]))
                                               for k in range(CW)])
                            ins.then_inc(branch_ps, 1)
                        pe.drain().then_inc(used[n % 3], 1)
                        pe.drain().then_inc(y_used, 1)
                    else:
                        o = int(name[1])
                        wh, wl = (t.rearrange("p (m n) -> p m n", m=2) for t in slot(n))
                        pe.wait_ge(mix_ready, o + 1)
                        for b in range(NB):
                            for half in range(2):
                                parts = []
                                for m in range(2):
                                    at = slice(b * P, (b + 1) * P)
                                    parts.append(((hh[:, 2 * o + m, at], hl[:, 2 * o + m, at]),
                                                  (wh[:, m, half * 512:(half + 1) * 512],
                                                   wl[:, m, half * 512:(half + 1) * 512])))
                                ins = product(PS[:, 2 + 2 * b + half, :], parts, o == 0, o == 3)
                            if o == 3 and b == 0:
                                ins.then_inc(wout_ps, 1)
                        ins.then_inc(used[n % 3], 1)
                        if o == 3:
                            pe.drain().then_inc(wout_ps, 1)

                def transposed_norm(i, banks):
                    pe.wait_ge(xn0_ready, i)
                    transpose_x(XN, 0, banks)
                    pe.wait_ge(xn1_ready, i)
                    transpose_x(XN, 1, banks)

                transposed_norm(1, (6, 7, 0, 1))
                pe.wait_ge(router_ready, 1)
                rwh, rwl = (t.rearrange("p (k e) -> p k e", k=KD) for t in (RWH, RWL))
                h_times(PS[:, 3, 0:S], rwh, rwl, 4).then_inc(route_ps, 1)

                def up(x, which, n, k=0):
                    wh, wl = slot(n, k)
                    if x > 1 or not isinstance(k, int):
                        pe.wait_ge(b_read if which else silu_done, 4 * k + x - 1)
                    by_channel(psum(4 + 2 * (x % 2) + which), wh, wl).then_inc(used[n % 3], 1)

                def down(x, n, k=0, first=False, last=False):
                    wh, wl = (t.rearrange("p (f n) -> p f n", f=2) for t in slot(n, k))
                    pe.wait_ge(act_lo, 4 * k + x + 1)
                    for b in range(NB):
                        for half in range(2):
                            parts = []
                            for f in range(2):
                                at = slice(f * S + b * P, f * S + (b + 1) * P)
                                parts.append(((YH[x % 2][:, at], YL[x % 2][:, at]),
                                              (wh[:, f, half * 512:(half + 1) * 512],
                                               wl[:, f, half * 512:(half + 1) * 512])))
                            ins = product(PS[:, 2 * b + half, :], parts, first, last)
                        if last and b == 0:
                            ins.then_inc(moe_ps, 1)
                    ins.then_inc(used[n % 3], 1)

                def transposed_gates():
                    pe.wait_ge(gates_ready, 1)
                    for b in range(NB):
                        ins = pe.transpose(PS[0:E, 2, b * P:(b + 1) * P], RT[:, 128 + b * E:128 + (b + 1) * E],
                                           con("ident"))
                    ins.then_inc(gates_ps, 1)

                def four_experts(k):
                    for i in range(4):
                        n = N_W1S + 2 + 3 * i
                        first = i == 0 and isinstance(k, int)
                        up(i + 1, 0, n, k)
                        if first:
                            transposed_gates()
                        up(i + 1, 1, n + 1, k)
                        if first:
                            pe.wait_ge(gates_sb, 1)
                        down(i, n + 2, k, first=first)

                up(0, 0, N_W1S)
                pe.wait_ge(sig_ready, 1)
                for b in range(NB):
                    ins = pe.transpose(PS[:, 2, b * E:(b + 1) * E], GT[0:E, b * P:(b + 1) * P],
                                       CON[0:E, CC["ident"].start:CC["ident"].start + E])
                ins.then_inc(sig_ps, 1)
                up(0, 1, N_W1S + 1)
                four_experts(0)
                with pe.Fori(1, KD) as k:
                    four_experts(k)
                pe.wait_ge(mod_used[0], 2 * KD)
                pe.wait_ge(mod_used[1], 2 * KD)
                pe.wait_ge(silu_done, E + 1)
                pe.wait_ge(b_read, E)
                sum_modulations()
                down(E, NUNIT - 1, last=True)
                pe.drain().then_inc(moe_ps, 1)
                pe.wait_ge(sc_ready, 1)
                pe.wait_ge(rows_sb, 1)
                transposed_norm(2, (4, 5, 6, 7))
                end_of_layer(pe, l + 1)


def _pack(inp):
    f = {k: np.asarray(v) for k, v in inp.items()}
    L = DEPTH
    z = lambda *s: np.zeros(s, np.float32)

    def kp(w):
        return w.reshape(P, KD, -1)

    def rows(w):
        return w.reshape(-1, P, w.shape[-1]).transpose(1, 0, 2)

    def bc(v):
        return np.broadcast_to(v.reshape(1, -1), (P, v.size))

    proj_cols = [(1732, 1988), (1988, 2244), None, (512, 768), (896, 1152), (1220, 1476), (256, 512), (0, 256),
                 (1476, 1732)]
    packed = z(L * NUNIT + 3, P, UC)
    stream = packed[:L * NUNIT].reshape(L, NUNIT, P, UC)
    for l in range(L):
        w_in = kp(f["w_in"][l])
        for n, name in enumerate(UNITS):
            i = int(name[1:])
            if name[0] == "P":
                if proj_cols[i] is None:
                    u = np.concatenate([w_in[:, :, 768:896], w_in[:, :, 1152:1220], w_in[:, :, 2244:2248],
                                        z(P, KD, 56)], 2)
                else:
                    u = w_in[:, :, proj_cols[i][0]:proj_cols[i][1]]
            elif name[0] == "G":
                u = kp(f["w_gate"][l, BRANCH_OF[i // 4]])[:, :, i % 4 * 256:(i % 4 + 1) * 256]
            elif name[0] == "B":
                u = rows(f["w_branch"][l, BRANCH_OF[i]])
            else:
                u = rows(f["w_out"][l])[:, 2 * i:2 * i + 2]
            stream[l, n] = u.reshape(P, UC)
        stream[l, N_W1S] = kp(f["sh_w1"][l]).reshape(P, UC)
        stream[l, N_W1S + 1] = kp(f["sh_w3"][l]).reshape(P, UC)
        n = N_W1S + 2
        stream[l, n:NUNIT - 1:3] = f["exp_w1"][l].reshape(E, P, UC)
        stream[l, n + 1:NUNIT - 1:3] = f["exp_w3"][l].reshape(E, P, UC)
        stream[l, n + 2] = rows(f["sh_w2"][l]).reshape(P, UC)
        w2 = f["exp_w2"][l].reshape(E, 2, P, D).transpose(0, 2, 1, 3).reshape(E, P, UC)
        stream[l, n + 5::3] = w2[:E - 1]
        stream[l, NUNIT - 1] = w2[E - 1]

    PC, NPARAM = columns(PARAM_COLS)
    params = z(L, P, NPARAM)
    router_w, router_b = z(L, P, KD, P), z(L, P, E)
    AC, NAHEAD = columns(AHEAD_COLS)
    ahead = z(L + 1, P, NAHEAD)
    mods = np.empty((L + 1, KD, 2, P, 3 * D), np.float32)
    gate_b = z(L + 1, 4, 512)
    norms = np.empty((L, 2, 2 * D), np.float32)
    for l in range(L):
        q = params[l]
        conv_w = f["ssd_conv_w"][l].reshape(4, 4, P)
        q[:, PC["conv_w"]] = conv_w.transpose(2, 1, 0).reshape(P, 16)
        q[:, PC["conv_b"]] = f["ssd_conv_b"][l].reshape(4, P).T
        for a, b in (("dt_bias", "ssd_dt_bias"), ("a_log", "ssd_a_log"), ("ssd_d", "ssd_d"), ("gm_g", "gm_ln_g"),
                     ("gm_b", "gm_ln_b"), ("norm_g", "ssd_norm_g")):
            q[:, PC[a]] = bc(f[b][l])
        q[:, PC["s5_d"]] = f["s5_d"][l].reshape(2, P).T
        q[:, PC["glu_b"]] = f["s5_glu_b"][l].reshape(2, P).T
        q[:, PC["sg_b"]] = np.repeat(f["gm_b"][l].reshape(2, 2, 1, P), 64, 2).reshape(2, P, P).transpose(
            1, 0, 2).reshape(P, 256)
        q[:, PC["sg_w"]] = f["gm_w"][l].transpose(2, 0, 1).reshape(P, 512)
        for r, (bn, cn) in enumerate((("s5_b_re", "s5_c_re"), ("s5_b_im", "s5_c_im"))):
            b5 = z(8, 2, 16, 2, 64)
            c5 = z(8, 2, 64, 2, 16)
            for gg in range(2):
                b5[:, gg, :, gg] = f[bn][l].reshape(8, 2, 64, 16)[:, gg].transpose(0, 2, 1)
                c5[:, gg, :, gg] = f[cn][l].reshape(8, 2, 16, 64)[:, gg].transpose(0, 2, 1)
            o = PC["s5_b"].start + 256 * r
            q[:, o:o + 256] = b5.reshape(2, P, P).transpose(1, 0, 2).reshape(P, 256)
            o = PC["s5_c"].start + 256 * r
            q[:, o:o + 256] = c5.reshape(8, P, 32).transpose(1, 0, 2).reshape(P, 256)
        q[:, PC["glu_w"]] = rows(f["s5_glu_w"][l]).reshape(P, 512)
        router_w[l, :, :, :E] = kp(f["router_w"][l])
        router_b[l] = bc(f["router_bias"][l])
        mod_b = np.stack([f["mod1_b"][l], f["mod2_b"][l]]).reshape(2, 3, D)
        ahead[l][:, AC["mod_b"]] = mod_b[:, :2].reshape(2, 2, P, KD).transpose(2, 0, 1, 3).reshape(P, 32)
        gate_b[l] = mod_b[:, 2].reshape(4, 512)
        norms[l, 0] = np.concatenate([f["ln1_g"][l], f["ln1_b"][l]])
        norms[l, 1] = np.concatenate([f["ln2_g"][l], f["ln2_b"][l]])
        state = lambda v: v.reshape(8, P).T
        ahead[l][:, AC["lam_re"]] = state(f["s5_lam_re"][l])
        ahead[l][:, AC["lam_im"]] = state(f["s5_lam_im"][l])
        ahead[l][:, AC["log_step"]] = state(np.repeat(f["s5_log_step"][l], 64))
        before = (f["ln2_g"][l - 1], f["ln2_b"][l - 1]) if l else (np.ones(D, np.float32), z(D))
        for name, pair in (("norm_g", (before[0], f["ln1_g"][l])), ("norm_b", (before[1], f["ln1_b"][l]))):
            ahead[l][:, AC[name]] = np.stack(pair).reshape(2, P, KD).transpose(1, 0, 2).reshape(P, 16)
        for j, name in enumerate(("mod1_w", "mod2_w")):
            mods[l, :, j] = f[name][l].reshape(P, KD, 3 * D).transpose(1, 0, 2)
    ahead[L], mods[L], gate_b[L] = ahead[0], mods[0], gate_b[0]
    CC, NCONST = columns(CONST_COLS)
    con = z(P, NCONST)
    i = np.arange(P)
    con[:, CC["ident"]] = np.eye(P)
    con[:, CC["upper"]] = i[None, :] >= i[:, None]
    con[:, CC["lower"]] = i[None, :] <= i[:, None]
    con[:, CC["floor"]] = np.where(i[None, :] <= i[:, None], 0.0, FLOOR)
    con[:, CC["ones"]] = 1.0
    con[:, CC["time"]] = np.arange(S)
    con[:, CC["inv"]] = (np.float32(500000.0) ** (-np.arange(0, 16, 2, dtype=np.float32) / np.float32(16)))
    con[:, CC["before"]] = (np.arange(8)[None, :] < np.arange(8)[:, None]).reshape(1, 64)
    pos = np.ascontiguousarray(f["positions"].reshape(NB, P).T.astype(np.int32))
    return dict(x=f["x"][0], pos=pos, cvec=f["c"].reshape(P, KD), consts=con, params=params,
                router_w=router_w.reshape(L, P, KD * P), router_b=router_b,
                gate_b=gate_b, ahead=ahead, norms=norms, mods=mods, stream=packed)


def kernel(**inputs):
    import concourse.bacc as bacc
    from concourse.bass_utils import run_bass_kernel_spmd

    nc = bacc.Bacc("TRN2", target_bir_lowering=False, num_devices=1)
    arrays = {k: np.ascontiguousarray(v) for k, v in _pack(inputs).items()}
    args = {k: nc.dram_tensor(k, v.shape, mybir.dt.from_np(v.dtype), kind="ExternalInput").ap()
            for k, v in arrays.items()}
    gate_rows = nc.dram_tensor("gate_rows", (2, D), F32, kind="Internal").ap()
    gates_t = nc.dram_tensor("gates_t", (E, S), F32, kind="Internal").ap()
    out = nc.dram_tensor("out", (S, D), F32, kind="ExternalOutput").ap()
    bass_trunk(nc, **args, gate_rows=gate_rows, gates_t=gates_t, out=out)
    r = run_bass_kernel_spmd(nc, [arrays], core_ids=[0])
    return r.results[0]["out"].reshape(1, S, D)
```

```python
import math
from contextlib import ExitStack

import numpy as np

import concourse.bass as bass
from concourse import mybir

F32 = mybir.dt.float32
F32R = mybir.dt.float32r
I32 = mybir.dt.int32
ACT = mybir.ActivationFunctionType
ALU = mybir.AluOpType
AX = mybir.AxisListType

P = 128
D = 1024
KD = D // P
S = 256
NB = S // P
DEPTH = 2
W = 256
CW = W // P
E = 32
TOPK = 8
NSEL = 64
EPS_LN = 1e-5
EPS_RMS = 1e-6
ALPHA = (2 * DEPTH) ** 0.25
NPROJ = 9
NGATE = 16
N_W1S = NPROJ + NGATE + 4 + 4
NUNIT = N_W1S + 3 * (E + 1)
UC = 2048
MODH = 3 * D // 2
MODQ = D
LAG = 4
TWO_PI = 2 * math.pi
PI_A = 6.28125
PI_B = float(np.float32(TWO_PI - PI_A) - np.float32(TWO_PI - PI_A) % np.float32(2.0 ** -20))
PI_C = TWO_PI - PI_A - PI_B
ROUND = 1.5 * 2.0 ** 23
ROUND14 = 1.5 * 2.0 ** 9
FLOOR = -3.0e38
TAKEN = -3.4e38
AWAY = 1.0e30

CONST_COLS = dict(ident=128, upper=128, lower=128, floor=128, ones=128, time=256, inv=8, before=64)
PARAM_COLS = dict(conv_w=16, conv_b=4, dt_bias=4, a_log=4, ssd_d=4, s5_d=2, glu_b=2, gm_g=256, gm_b=256,
                  norm_g=256, sg_b=256, sg_w=512, s5_b=512, s5_c=512, glu_w=512)
AHEAD_COLS = dict(lam_re=8, lam_im=8, log_step=8, mod_b=32, norm_g=16, norm_b=16)
TINY_COLS = dict(var=2, mv=4, stats=24, phi_hi=8, phi_lo=8, s5a=8, s5b=8, s5c=8, s5d=8, sin=8, half=8, rope_a=16,
                 rope_b=16, dt_v=8, dt_e=8, dt=8, shift=1, exp_a=4, adt=8, acum=8, acum_e=4, ms=4, wi=8, top=8, neg=8,
                 den=8, glu_hb=2, mvg=4)


def columns(table):
    at, out = 0, {}
    for name, n in table.items():
        out[name] = slice(at, at + n)
        at += n
    return out, at


ORDER = ("P0 P1 P2 P3 ssd1 P4 ssd2 P6 att1 P7 index gm ssd3 P8 ssd4 G0 G1 logits G2 ssd5 G3 B0 P5 G4 s5a att3 G5 "
         "att4 s5b G6 G7 B1 s51 G8 G9 s52 G10 G11 B2 s53 G12 G13 s54 G14 glu sums G15 columns B3 O0 O1 O2 O3").split()
ACT_ORDER = ("P0 P1 P2 silu_xbc softplus P3 x_tok P4 decay P6 qk_t v_root P7 relu state P8 G0 rms_root G1 G2 y0 G3 "
             "B0 y1 P5 exp G4 prob_t G5 G6 G7 B1 y2 G8 G9 G10 G11 B2 G12 G13 gelu G14 tanh y3 sums G15 B3 "
             "O0 O1 O2 O3").split()
UNITS = [x for x in ORDER if x[0] in "PGBO"]
TURNS = [(x, part) for x in UNITS if x[0] != "O" for part in range(4 if x[0] == "B" else 1)]
BRANCH_OF = (3, 0, 1, 2)


def made(n):
    return n // 3


def uses(n):
    return n // 3 + 1


def loads(n):
    return n // 2 - (n % 2 == 0)


def turn(x, part=0):
    return TURNS.index((x, part))


def bass_trunk(nc, x, pos, cvec, consts, params, router_w, router_b, gate_b, ahead, norms, mods, stream, gate_rows, gates_t,
               out):
    CC, NCONST = columns(CONST_COLS)
    PC, NPARAM = columns(PARAM_COLS)
    TC, NTINY = columns(TINY_COLS)
    AC, NAHEAD = columns(AHEAD_COLS)

    ctx = ExitStack()
    with ctx:
        layer_go = ctx.enter_context(nc.semaphore("layer_go"))
        counters = []

        def sem(name):
            counters.append(ctx.enter_context(nc.semaphore(name)))
            return counters[-1]

        layer_done = sem("layer_done")
        raw_in = [sem(f"raw_in{i}") for i in range(2)]
        hi_done = [sem(f"hi_done{i}") for i in range(3)]
        lo_done = [sem(f"lo_done{i}") for i in range(3)]
        used = [sem(f"used{i}") for i in range(3)]
        turn_free = [sem(f"turn_free{i}") for i in range(2)]
        mod_in = [sem(f"mod_in{i}") for i in range(4)]
        mod_used = [sem(f"mod_used{i}") for i in range(4)]
        mod2_in = [sem(f"mod2_in{i}") for i in range(2)]
        mod2_used = [sem(f"mod2_used{i}") for i in range(2)]
        acc2_zero = sem("acc2_zero")
        g_in = [sem(f"g_in{i}") for i in range(2)]
        const_in, c_in, pos_in, x_in = sem("const_in"), sem("c_in"), sem("pos_in"), sem("x_in")
        ahead_in, params_in, router_in, gate_b_in, norm_in = (
            sem("ahead_in"), sem("params_in"), sem("router_in"), sem("gate_b_in"), sem("norm_in"))
        angle_ready, acc_zero = sem("angle_ready"), sem("acc_zero")
        step_exp, decay_in, turns_ready, trig_ready, phase_ready, sines_ready = (
            sem("step_exp"), sem("decay_in"), sem("turns_ready"), sem("trig_ready"), sem("phase_ready"),
            sem("sines_ready"))
        sums_ps, sums_sb, cols_ps, rows_ps, rows_sb, rows_out, sc_ready = (
            sem("sums_ps"), sem("sums_sb"), sem("cols_ps"), sem("rows_ps"), sem("rows_sb"), sem("rows_out"), sem("sc_ready"))
        xt_ps, h_hi, h_ready = sem("xt_ps"), sem("h_hi"), sem("h_ready")
        conv_ready, xbc_ready, dt_abs, dt_log, adt_ready = (
            sem("conv_ready"), sem("xbc_ready"), sem("dt_abs"), sem("dt_log"), sem("adt_ready"))
        ssd1_ps, x_tok, ssd2_ps, decay_log, decay_exp, mask_ready, ssd3_ps, state_sb, ssd4_ps = (
            sem("ssd1_ps"), sem("x_tok"), sem("ssd2_ps"), sem("decay_log"), sem("decay_exp"), sem("mask_ready"),
            sem("ssd3_ps"), sem("state_sb"), sem("ssd4_ps"))
        rms_sq, rms_root, ssd_ready, ssd5_ps = sem("rms_sq"), sem("rms_root"), sem("ssd_ready"), sem("ssd5_ps")
        qk_ready, att1_ps, qk_t, index_ps, logit_ps, relu_sb, logit_max, exp_ready, prob_ready, att3_ps, prob_t, \
            att4_ps = (sem("qk_ready"), sem("att1_ps"), sem("qk_t"), sem("index_ps"), sem("logit_ps"),
                       sem("relu_sb"), sem("logit_max"), sem("exp_ready"), sem("prob_ready"), sem("att3_ps"),
                       sem("prob_t"), sem("att4_ps"))
        v_var, v_root, v_ready, gm_ps, gm_ready = (
            sem("v_var"), sem("v_root"), sem("v_ready"), sem("gm_ps"), sem("gm_ready"))
        c_ready, s5v_ps, s5v_read, s5h_ready, s5y_ps, s5y_ready, s5_gelu, glu_ps, glu_tanh, glu_ready = (
            sem("c_ready"), sem("s5v_ps"), sem("s5v_read"), sem("s5h_ready"), sem("s5y_ps"), sem("s5y_ready"),
            sem("s5_gelu"), sem("glu_ps"), sem("glu_tanh"), sem("glu_ready"))
        y_hi, y_lo, y_used, branch_ps, merged, mix_hi, mix_ready, wout_ps = (
            sem("y_hi"), sem("y_lo"), sem("y_used"), sem("branch_ps"), sem("merged"), sem("mix_hi"),
            sem("mix_ready"), sem("wout_ps"))
        ln_var, ln_root, ln_scale, xn0_ready, xn1_ready, ln_done = (
            sem("ln_var"), sem("ln_root"), sem("ln_scale"), sem("xn0_ready"), sem("xn1_ready"), sem("ln_done"))
        router_w_in, router_hi, router_ready, route_ps, sig_ready, sig_ps, gates_ready, gates_ps, gates_sb, gates_out = (
            sem("router_w_in"), sem("router_hi"), sem("router_ready"), sem("route_ps"), sem("sig_ready"), sem("sig_ps"),
            sem("gates_ready"),
            sem("gates_ps"), sem("gates_sb"), sem("gates_out"))
        silu_done, b_read, act_ready, act_hi, act_lo, moe_ps = (
            sem("silu_done"), sem("b_read"), sem("act_ready"), sem("act_hi"), sem("act_lo"),
            sem("moe_ps"))
        numbers = sorted(s.num for s in counters)
        assert numbers == list(range(numbers[0], numbers[-1] + 1))
        out_in = ctx.enter_context(nc.semaphore("out_in"))

        class Region:
            def __init__(self, at):
                self.at = at

            def put(self, name, cols, dt=F32):
                t = nc.alloc_sbuf_tensor_at(name, [P, cols], dt, offset=self.at)
                self.at += -(-4 * cols // 32) * 32
                return t[:, :]

        keep = Region(-(-nc.sbuf_base // 32) * 32)
        X = keep.put("X", NB * D)
        HH, HL = keep.put("HH", KD * S, F32R), keep.put("HL", KD * S, F32R)
        RAW = [keep.put(f"RAW{i}", UC) for i in range(2)]
        WH = [keep.put(f"WH{i}", UC, F32R) for i in range(3)]
        WL = [keep.put(f"WL{i}", UC, F32R) for i in range(3)]
        COS, SIN = keep.put("COS", 8 * S), keep.put("SIN", 8 * S)
        YH, YL = [keep.put("YH0", 512, F32R)], [keep.put("YL0", 512, F32R)]
        CON = keep.put("CON", NCONST)
        ROUT = keep.put("ROUT", E)
        SC = keep.put("SC", 32)
        AHEAD, S5D = keep.put("AHEAD", NAHEAD), keep.put("S5D", 24)
        TINY = keep.put("TINY", NTINY)
        CVEC = keep.put("CVEC", KD)
        ROPE = keep.put("ROPE", 32)

        mix = Region(keep.at)
        SIG = mix.put("SIG", 8 * 512)
        PAR = mix.put("PAR", NPARAM)
        MISC = mix.put("MISC", 512)
        QK = mix.put("QK", NB * 12 * 64)
        UT, V, GU, Z = (mix.put(n, 512) for n in ("UT", "V", "GU", "Z"))
        conv_at = mix.at
        CIN = mix.put("CIN", 4 * (S + 4))
        XBC = mix.put("XBC", 4 * S)
        WORK = mix.put("WORK", 3072)
        QT = mix.put("QT", 1536)
        SCORE = [mix.put("SCORE0", P), mix.put("SCORE1", S)]
        LEFT = [mix.put("LEFT0", P), mix.put("LEFT1", S)]
        ACC2 = mix.put("ACC2", 3 * D)
        MR = [mix.put(f"MR{i}", MODQ) for i in range(2)]
        MG = Region(conv_at).put("MG", KD * S)

        moe = Region(keep.at)
        stage_at = [moe.at]
        NRM = moe.put("NRM", 3 * D)
        acc_at = moe.at
        ACC = moe.put("ACC", 3 * D)
        stage_at.append(moe.at)
        MODR = [moe.put(f"MODR{i}", MODH) for i in range(2)]
        stage_at.append(moe.at)
        G = [moe.put(f"G{i}", S) for i in range(2)]
        SL = [moe.put(f"SL{i}", 512) for i in range(2)]
        T = [moe.put(f"T{i}", 512) for i in range(2)]
        YH.append(moe.put("YH1", 512, F32R))
        YL.append(moe.put("YL1", 512, F32R))
        GT = moe.put("GT", S)
        RT = moe.put("RT", 1024)
        HT = moe.put("HT", KD * S)
        GROW, GBR = moe.put("GROW", 512), moe.put("GBR", 512)
        SUMS = HT[:, 0:D]
        stage_at.append(moe.at)
        STAGE = [Region(at).put(f"STAGE{i}", 3 * D) for i, at in enumerate(stage_at)]
        router_at = Region(stage_at[3])
        RW, RWH, RWL = (router_at.put("RW", KD * P), router_at.put("RWH", KD * P, F32R),
                        router_at.put("RWL", KD * P, F32R))
        XN = Region(acc_at).put("XN", NB * D)
        LNT = Region(stage_at[1]).put("LNT", NB * D)
        moe.at += 4 * 3 * D
        assert max(mix.at, moe.at) <= nc.sbuf_usable_end, (mix.at, moe.at, nc.sbuf_usable_end)

        PS = ctx.enter_context(nc.psum_tensor("PS", [P, 8, 512], F32))

        def con(name):
            return CON[:, CC[name]]

        def par(name):
            return PAR[:, PC[name]]

        def tiny(name, a=0, b=None):
            s = TC[name]
            return TINY[:, s.start + a:s.stop if b is None else s.start + b]

        def wide(ap, n):
            return ap.unsqueeze(2).broadcast_to([ap.shape[0], ap.shape[1], n])

        def rep(ap, n):
            return ap.unsqueeze(1).broadcast_to([ap.shape[0], n, ap.shape[1]])

        X3 = X.rearrange("p (b d) -> p b d", b=NB)
        hh, hl = (t.rearrange("p (k t) -> p k t", k=KD) for t in (HH, HL))
        sc4 = SC.rearrange("p (j s k) -> p j s k", j=2, s=2)
        SUMS2, GROW2, GBR2 = SIG[:, 0:D], SIG[:, D:D + 512], SIG[:, D + 512:2 * D]
        qk4 = QK.rearrange("p (b g d) -> p b g d", b=NB, g=12)
        misc3 = MISC.rearrange("p (b n) -> p b n", b=NB)
        cin3 = CIN.rearrange("p (c t) -> p c t", c=4)
        xbc3 = XBC.rearrange("p (c t) -> p c t", c=4)
        XT, BT, LM = WORK[:, 0:512], WORK[:, 512:640], WORK[:, 640:1664]
        XDT, DECX, ST, YS = WORK[:, 1664:2176], WORK[:, 2176:2432], WORK[:, 2432:2560], WORK[:, 2560:3072]
        RL = [QK[:, 0:512], QK[:, 512:1536]]
        PT = [QT[:, 0:512], QT[:, 512:1536]]
        CRE, CIM = (par("s5_c")[:, a:a + 256] for a in (0, 256))
        B5 = [WORK[:, 512 * i:512 * i + 512] for i in range(6)]
        NKEY = (P, S)

        def psum(a, b=None):
            return PS[:, a:(b or a + 1), :].rearrange("p a n -> p (a n)")

        def turn_wait(eng, i):
            if i >= 2:
                eng.wait_ge(turn_free[i % 2], i // 2)

        def phases(eng, chunks):
            at = slice(chunks.start * S, chunks.stop * S)
            n = chunks.stop - chunks.start
            turns, other = COS[:, at], SIN[:, at]
            turns3, other3 = (t.rearrange("p (j t) -> p j t", j=n) for t in (turns, other))
            time = rep(con("time"), n)

            def fraction():
                eng.drain()
                eng.tensor_scalar(other, turns, ROUND, ROUND, ALU.add, ALU.subtract)
                eng.drain()
                eng.tensor_tensor(turns, turns, other, ALU.subtract)
                eng.drain()

            eng.tensor_tensor(turns3, wide(tiny("phi_hi", chunks.start, chunks.stop), S), time, ALU.mult)
            fraction()
            eng.tensor_tensor(other3, wide(tiny("phi_lo", chunks.start, chunks.stop), S), time, ALU.mult)
            eng.drain()
            eng.tensor_tensor(turns, turns, other, ALU.add)
            fraction()
            eng.drain().then_inc(phase_ready, 1)

        def cosines(eng):
            eng.wait_ge(sines_ready, 1)
            eng.tensor_tensor(COS, COS, COS, ALU.mult)
            eng.drain()
            eng.tensor_scalar(COS, COS, -2.0, 1.0, ALU.mult, ALU.add)

        def end_of_layer(eng, l):
            eng.drain().then_inc(layer_done, 1)
            if eng is nc.sync:
                eng.wait_ge(layer_done, 5)
                eng.sem_clear(range(numbers[0], numbers[-1] + 1))
                eng.drain().then_inc(layer_go, 1)
            else:
                eng.wait_ge(layer_go, l + 1)

        block = ctx.enter_context(nc.Block())

        @block.sync
        def _(sp):
            sp.dma_start(CON, consts).then_inc(const_in, 16)
            sp.dma_start(RT[:, 0:NB].bitcast(I32), pos).then_inc(pos_in, 16)
            sp.dma_start(AHEAD, ahead[0]).then_inc(ahead_in, 16)
            sp.dma_start(CVEC, cvec).then_inc(c_in, 16)

            def mod_whole(k):
                if k >= 4:
                    sp.wait_ge(mod_used[k % 4], 1)
                sp.dma_start(STAGE[k % 4], mods[0, k, 0]).then_inc(mod_in[k % 4], 16)

            def mod_half(layer, k, i):
                if not isinstance(k, int):
                    sp.wait_ge(mod_used[i], k)
                sp.dma_start(MODR[i], mods[layer, k, 0, :, i * MODH:(i + 1) * MODH]).then_inc(mod_in[i], 16)

            def mod2_third(layer, p):
                if p >= 2:
                    sp.wait_ge(mod2_used[p % 2], p // 2)
                sp.dma_start(MR[p % 2], mods[layer, p // 3, 1, :, p % 3 * MODQ:(p % 3 + 1) * MODQ]
                             ).then_inc(mod2_in[p % 2], 16)

            def load_gate_b(layer, j, dst):
                for r in range(2):
                    sp.dma_start(dst[64 * r:64 * r + 64, :], gate_b[layer, 2 * j + r:2 * j + r + 1, :].to_broadcast(
                        [64, 512])).then_inc(gate_b_in, 16)

            def store_gate_row(j, src, times):
                sp.wait_ge(rows_sb, times)
                for r in range(2):
                    sp.dma_start(gate_rows[j:j + 1, r * 512:r * 512 + 512], src[64 * r:64 * r + 1, :]
                                 ).then_inc(rows_out, 16)
                sp.wait_ge(rows_out, 32 * times)

            for k in range(KD // 2):
                mod_whole(k)
            sp.dma_start(RAW[0], stream[0]).then_inc(raw_in[0], 16)
            for k in range(KD // 2, KD):
                mod_whole(k)
            sp.dma_start(X3, x.rearrange("(b p) d -> p b d", p=P)).then_inc(x_in, 16)
            sp.dma_start(RAW[1], stream[1]).then_inc(raw_in[1], 16)
            sp.wait_ge(hi_done[0], 1)
            sp.wait_ge(lo_done[0], 1)
            sp.dma_start(RAW[0], stream[2]).then_inc(raw_in[0], 16)
            load_gate_b(0, 0, GBR)
            store_gate_row(0, GROW, 1)
            end_of_layer(sp, 0)

            with sp.Fori(0, DEPTH) as l:
                def unit(n, k=0):
                    if n >= 5:
                        sp.wait_ge(hi_done[(n - 2) % 3], 4 * k + made(n - 2))
                        sp.wait_ge(lo_done[(n - 2) % 3], 4 * k + made(n - 2))
                    sp.dma_start(RAW[n % 2], stream[NUNIT * l + 12 * k + n]).then_inc(raw_in[n % 2], 16)

                unit(3)
                sp.dma_start(PAR, params[l]).then_inc(params_in, 16)
                mod2_third(l, 0)
                mod2_third(l, 1)
                unit(4)
                sp.dma_start(ROUT, router_b[l]).then_inc(router_in, 16)
                for n in range(5, N_W1S + 1):
                    unit(n)
                    if 2 <= n - LAG < 3 * KD:
                        mod2_third(l, n - LAG)
                    if n == N_W1S - 2:
                        store_gate_row(1, GROW2, 1)
                    if n - LAG == 3 * KD:
                        load_gate_b(l, 1, GBR2)

                def load_norm(which):
                    for r in range(2):
                        sp.dma_start(NRM[:, r * D:(r + 1) * D],
                                     norms[l, which:which + 1, r * D:(r + 1) * D].to_broadcast([P, D])
                                     ).then_inc(norm_in, 16)
                    sp.dma_start(NRM[:, 2 * D:3 * D], gate_rows[which:which + 1, :].to_broadcast([P, D])
                                 ).then_inc(norm_in, 16)

                sp.wait_ge(merged, 4)
                load_norm(0)
                sp.dma_start(AHEAD, ahead[l + 1]).then_inc(ahead_in, 16)
                sp.dma_start(RW, router_w[l]).then_inc(router_w_in, 16)
                unit(N_W1S + 1)
                unit(N_W1S + 2)
                unit(N_W1S + 3)

                def store_gates():
                    sp.wait_ge(gates_sb, 1)
                    sp.dma_start(gates_t, GT[0:E, :]).then_inc(gates_out, 16)
                    sp.wait_ge(gates_out, 16)

                def four_experts(k):
                    for i in range(4):
                        for u in range(1, 4):
                            first = i == 0 and isinstance(k, int)
                            if u > 1 or not first:
                                unit(N_W1S + 2 + 3 * i + u, k)
                            if u == 2 and first:
                                load_gate_b(l + 1, 0, GBR)
                                sp.wait_ge(ln_done, 2)
                                load_norm(1)
                                store_gates()
                        if i or not isinstance(k, int):
                            sp.wait_ge(act_ready, 4 * k + i)
                        sp.dma_start(G[(i + 1) % 2], gates_t[bass.ds(4 * k + i, 1), :].to_broadcast([P, S])
                                     ).then_inc(g_in[(i + 1) % 2], 16)
                        if i % 2 == 0:
                            mod_half(l + 1, k, i // 2)

                four_experts(0)
                with sp.Fori(1, KD) as k:
                    four_experts(k)
                for n in range(NUNIT, NUNIT + 3):
                    unit(n)
                sp.wait_ge(norm_in, 96)
                store_gate_row(0, GROW, 2)
                end_of_layer(sp, l + 1)
            sp.dma_start(out.rearrange("(b p) d -> p b d", p=P), X3).then_inc(out_in, 16)
            sp.wait_ge(out_in, 16)

        @block.gpsimd
        def _(pool):
            def lo_part(n, times):
                pool.wait_ge(hi_done[n % 3], times)
                pool.tensor_tensor(WL[n % 3], RAW[n % 2], WH[n % 3].bitcast(F32), ALU.subtract
                                   ).then_inc(lo_done[n % 3], 1)

            def affine(i):
                pool.wait_ge(xn1_ready, i)
                pool.tensor_tensor(X[:, 3 * 512:], XN[:, 3 * 512:], NRM[:, 512:D], ALU.mult)
                pool.drain()
                pool.tensor_tensor(X[:, 3 * 512:], X[:, 3 * 512:], NRM[:, D + 512:2 * D], ALU.add)
                pool.drain().then_inc(ln_done, 1)

            pool.memset(ACC, 0.0).then_inc(acc_zero, 1)
            pool.wait_ge(turns_ready, 1)
            phases(pool, slice(4, 8))
            lo_part(0, 1)
            cosines(pool)
            lo_part(1, 1)
            end_of_layer(pool, 0)
            with pool.Fori(0, DEPTH) as l:
                pool.memset(ACC2, 0.0).then_inc(acc2_zero, 1)
                for n in range(3, N_W1S + 1):
                    lo_part(n, made(n))
                affine(1)
                lo_part(N_W1S + 2, made(N_W1S + 2))
                lo_part(N_W1S + 3, made(N_W1S + 3))
                pool.wait_ge(ln_done, 2)
                pool.wait_ge(h_ready, 8)
                pool.memset(ACC, 0.0).then_inc(acc_zero, 1)
                pool.wait_ge(turns_ready, 1)
                phases(pool, slice(0, 8))
                cosines(pool)
                lo_part(NUNIT, made(NUNIT))
                lo_part(NUNIT + 1, made(NUNIT + 1))
                lo_part(NUNIT + 2, made(NUNIT + 2))
                affine(2)
                end_of_layer(pool, l + 1)

        @block.scalar
        def _(act):
            def hi_part(n, k=0):
                act.wait_ge(raw_in[n % 2], 16 * (6 * k + loads(n)))
                act.wait_ge(used[n % 3], 4 * k + uses(n - 3))
                act.activation(WH[n % 3], RAW[n % 2], ACT.Copy).then_inc(hi_done[n % 3], 1)

            def step(times):
                act.wait_ge(ahead_in, 16 * times)
                act.activation(tiny("half"), AHEAD[:, AC["log_step"]], ACT.Exp).then_inc(step_exp, 1)

            def tables(parts):
                act.wait_ge(turns_ready, 1)
                act.activation(S5D[:, 0:8], tiny("s5a"), ACT.Exp)
                act.activation(tiny("sin"), tiny("s5b"), ACT.Sin)
                act.activation(tiny("half"), tiny("s5b"), ACT.Sin, scale=0.5)
                act.drain().then_inc(trig_ready, 1)
                act.wait_ge(phase_ready, parts)
                act.activation(SIN, COS, ACT.Sin, scale=TWO_PI)
                act.drain()
                act.activation(COS, COS, ACT.Sin, scale=math.pi).then_inc(sines_ready, 1)

            def copy_sums(dst, bank, times):
                act.wait_ge(sums_ps, times)
                act.activation(dst, psum(bank, bank + 2), ACT.Copy).then_inc(sums_sb, 1)

            ht3 = HT.rearrange("p (k t) -> p k t", k=KD)

            def make_h(j, banks, quarters, transposed=0):
                for g in quarters:
                    if j or g < 2:
                        act.wait_ge(xt_ps, transposed + g + 1)
                    for dst in (hh, ht3) if g == 3 else (hh,):
                        for k in (2 * g, 2 * g + 1):
                            ins = act.activation(dst[:, k, :], PS[:, banks[g], k % 2 * S:k % 2 * S + S], ACT.Identity,
                                                 scale=sc4[:, j, 1, k:k + 1], bias=sc4[:, j, 0, k:k + 1])
                    ins.then_inc(h_hi, 1)

            step(1)
            act.wait_ge(angle_ready, 1)
            act.activation(ROPE[:, 16:32], tiny("rope_a"), ACT.Sin)
            act.activation(ROPE[:, 0:16], tiny("rope_a"), ACT.Sin, scale=0.5)
            act.drain().then_inc(angle_ready, 1)
            tables(2)
            for n in range(2):
                act.wait_ge(raw_in[n], 16)
                act.activation(WH[n], RAW[n], ACT.Copy).then_inc(hi_done[n], 1)
            copy_sums(SUMS, 6, 1)
            act.wait_ge(raw_in[0], 32)
            act.activation(WH[2], RAW[0], ACT.Copy).then_inc(hi_done[2], 1)
            act.wait_ge(sc_ready, 1)
            make_h(0, (0, 1, 4, 5), range(2))
            end_of_layer(act, 0)

            with act.Fori(0, DEPTH) as l:
                def evacuate(name):
                    n, i = UNITS.index(name), turn(name)
                    act.wait_ge(used[n % 3], uses(n))
                    src = psum(i % 2)
                    src3 = src.rearrange("p (c t) -> p c t", c=2)
                    if name in ("P0", "P1"):
                        c0 = 2 * int(name[1])
                        ins = act.activation(cin3[:, c0:c0 + 2, 3:3 + S], src3, ACT.Copy)
                    elif name == "P5":
                        ins = act.activation(UT, src, ACT.Copy)
                    elif name == "P6":
                        ins = act.activation(V, src, ACT.Gelu_apprx_tanh)
                    elif name == "P7":
                        ins = act.activation(GU, src, ACT.Gelu_apprx_tanh)
                    elif name == "P8":
                        ins = act.activation(Z, src, ACT.Silu)
                    else:
                        g = int(name[1:])
                        ins = act.activation(SIG[:, g % 8 * 512:(g % 8 + 1) * 512], src, ACT.Tanh, scale=0.5)
                    ins.then_inc(turn_free[i % 2], 1)

                def branch_hi(i, src, scale=1.0):
                    if i:
                        act.wait_ge(y_used, i)
                    act.activation(YH[0], src, ACT.Copy, scale=scale).then_inc(y_hi, 1)

                def relu_index(b):
                    act.wait_ge(index_ps, b + 1)
                    act.activation(RL[b], psum(5) if b == 0 else psum(2, 4), ACT.Relu).then_inc(relu_sb, 1)

                def softmax_exp(b):
                    n = NKEY[b]
                    act.wait_ge(logit_max, b + 1)
                    for h in range(4):
                        act.activation(RL[b][:, h * n:(h + 1) * n], RL[b][:, h * n:(h + 1) * n], ACT.Exp,
                                       bias=tiny("neg", 4 * b + h, 4 * b + h + 1),
                                       accum_out=tiny("den", 4 * b + h, 4 * b + h + 1))
                    act.drain().then_inc(exp_ready, 1)

                make_h(0, (0, 1, 4, 5), range(2, 4))
                for name in ACT_ORDER:
                    if name == "silu_xbc":
                        act.wait_ge(conv_ready, 1)
                        act.activation(XBC, XBC, ACT.Silu).then_inc(xbc_ready, 1)
                    elif name == "softplus":
                        act.wait_ge(dt_abs, 1)
                        act.activation(tiny("dt_e"), tiny("dt_e"), ACT.Exp, scale=-1.0)
                        act.activation(tiny("exp_a"), par("a_log"), ACT.Exp)
                        act.drain()
                        act.activation(tiny("dt_e"), tiny("dt_e"), ACT.Ln, bias=1.0)
                        act.drain().then_inc(dt_log, 1)
                    elif name == "x_tok":
                        act.wait_ge(ssd1_ps, 1)
                        act.activation(XT, psum(2), ACT.Copy)
                        act.activation(BT, PS[:, 3, 0:P], ACT.Copy)
                        act.drain().then_inc(x_tok, 1)
                    elif name == "decay":
                        act.wait_ge(decay_log, 1)
                        act.activation(LM, LM, ACT.Exp)
                        act.activation(tiny("acum_e"), tiny("acum", 4, 8), ACT.Exp)
                        act.drain().then_inc(decay_exp, 1)
                    elif name == "state":
                        act.wait_ge(ssd3_ps, 1)
                        act.activation(ST, PS[:, 7, 0:P], ACT.Copy).then_inc(state_sb, 1)
                    elif name == "rms_root":
                        act.wait_ge(rms_sq, 1)
                        act.activation(tiny("ms"), tiny("ms"), ACT.Sqrt).then_inc(rms_root, 1)
                    elif name == "y0":
                        act.wait_ge(ssd5_ps, 1)
                        branch_hi(0, psum(6))
                    elif name == "v_root":
                        act.wait_ge(v_var, 1)
                        act.activation(tiny("mvg", 0, 2), tiny("mvg", 0, 2), ACT.Sqrt).then_inc(v_root, 1)
                    elif name == "qk_t":
                        act.wait_ge(att1_ps, 1)
                        act.activation(QT[:, 0:1024], psum(2, 4), ACT.Copy)
                        act.activation(QT[:, 1024:1536], psum(5), ACT.Copy)
                        act.drain().then_inc(qk_t, 1)
                    elif name == "y1":
                        act.wait_ge(gm_ready, 1)
                        branch_hi(1, V)
                    elif name == "relu":
                        relu_index(0)
                        relu_index(1)
                    elif name == "exp":
                        softmax_exp(0)
                        softmax_exp(1)
                    elif name == "prob_t":
                        act.wait_ge(att3_ps, 1)
                        act.activation(PT[0], psum(7), ACT.Copy).then_inc(prob_t, 1)
                        act.wait_ge(att3_ps, 2)
                        act.activation(PT[1], psum(5, 7), ACT.Copy).then_inc(prob_t, 1)
                    elif name == "y2":
                        act.wait_ge(att4_ps, 1)
                        branch_hi(2, psum(4))
                    elif name == "gelu":
                        act.wait_ge(s5y_ready, 1)
                        act.activation(B5[0], B5[0], ACT.Gelu_apprx_tanh).then_inc(s5_gelu, 1)
                    elif name == "tanh":
                        act.wait_ge(glu_ps, 1)
                        for c in range(CW):
                            act.activation(B5[1][:, c * S:(c + 1) * S], PS[:, 4, c * S:(c + 1) * S], ACT.Tanh,
                                           scale=0.5, bias=tiny("glu_hb", c, c + 1))
                        act.drain().then_inc(glu_tanh, 1)
                    elif name == "y3":
                        act.wait_ge(glu_ready, 1)
                        branch_hi(3, B5[2], 0.5)
                    elif name == "sums":
                        copy_sums(SUMS2, 2, 1)
                    if name[0] in "PG" and name not in ("P2", "P3", "P4"):
                        evacuate(name)
                    if name == "B3":
                        for g in range(4):
                            act.wait_ge(merged, g + 1)
                            act.activation(HH[:, g * 512:(g + 1) * 512], MG[:, g * 512:(g + 1) * 512], ACT.Copy,
                                           scale=0.5).then_inc(mix_hi, 1)
                    if name == "O2":
                        act.wait_ge(router_w_in, 16)
                        act.activation(RWH, RW, ACT.Copy).then_inc(router_hi, 1)
                    if name[0] in "PGBO" and UNITS.index(name) + 3 < N_W1S + 1:
                        hi_part(UNITS.index(name) + 3)

                def norm(i):
                    act.wait_ge(ln_var, 2 * i - 1)
                    act.activation(tiny("var", 0, 1), tiny("var", 0, 1), ACT.Sqrt).then_inc(ln_root, 1)
                    act.wait_ge(ln_scale, i)
                    act.activation(XN[:, 0:D], X[:, 0:D], ACT.Identity, scale=tiny("var", 0, 1), bias=tiny("shift")
                                   ).then_inc(xn0_ready, 1)
                    act.wait_ge(ln_var, 2 * i)
                    act.activation(tiny("var", 1, 2), tiny("var", 1, 2), ACT.Sqrt).then_inc(ln_root, 1)

                norm(1)
                make_h(1, (6, 7, 0, 1), range(4))
                hi_part(N_W1S + 1)
                hi_part(N_W1S + 2)
                act.wait_ge(route_ps, 1)
                act.activation(GT[0:E, :], PS[0:E, 3, 0:S], ACT.Sigmoid).then_inc(sig_ready, 1)
                step(1)

                def silu(x, k=0):
                    n = N_W1S - 1 + 3 * x if x else N_W1S
                    act.wait_ge(used[n % 3], 4 * k + uses(n))
                    if x > 1 or not isinstance(k, int):
                        act.wait_ge(b_read, 4 * k + x - 1)
                    act.activation(SL[x % 2], psum(4 + 2 * (x % 2)), ACT.Silu).then_inc(silu_done, 1)

                def activation_hi(x, k=0):
                    act.wait_ge(act_ready, 4 * k + x + 1)
                    act.wait_ge(used[1], 4 * k + uses(N_W1S + 1) - 1 + x)
                    act.activation(YH[x % 2], T[x % 2], ACT.Copy).then_inc(act_hi, 1)

                def four_experts(k):
                    for i in range(4):
                        n = N_W1S + 2 + 3 * i
                        hi_part(n + 1, k)
                        activation_hi(i, k)
                        hi_part(n + 2, k)
                        silu(i + 1, k)
                        hi_part(n + 3, k)

                silu(0)
                four_experts(0)
                tables(1)
                with act.Fori(1, KD) as k:
                    four_experts(k)
                hi_part(NUNIT)
                activation_hi(E)
                copy_sums(SUMS, 6, 2)
                hi_part(NUNIT + 1)
                hi_part(NUNIT + 2)
                norm(2)
                act.wait_ge(sc_ready, 2)
                make_h(0, (0, 1, 4, 5), range(2), 4)
                end_of_layer(act, l + 1)

        @block.vector
        def _(dve):
            def lo_part(n, k=0):
                dve.wait_ge(hi_done[n % 3], 4 * k + made(n))
                dve.tensor_tensor(WL[n % 3], RAW[n % 2], WH[n % 3].bitcast(F32), ALU.subtract
                                  ).then_inc(lo_done[n % 3], 1)

            def reduce_angle(a, turns):
                dve.tensor_scalar(turns, a, 1 / TWO_PI, ROUND, ALU.mult, ALU.add)
                dve.drain()
                dve.tensor_scalar(turns, turns, ROUND, None, ALU.subtract)
                for part in (PI_A, PI_B, PI_C):
                    dve.drain()
                    dve.scalar_tensor_tensor(a, turns, -part, a, ALU.mult, ALU.add)
                dve.drain()

            lam_re, lam_im = AHEAD[:, AC["lam_re"]], AHEAD[:, AC["lam_im"]]
            decay, factor_re, factor_im = S5D[:, 0:8], S5D[:, 8:16], S5D[:, 16:24]

            def phase():
                a, b, cc = tiny("s5a"), tiny("s5b"), tiny("s5c")
                dve.wait_ge(step_exp, 1)
                dve.tensor_tensor(a, lam_re, tiny("half"), ALU.mult)
                dve.tensor_tensor(b, lam_im, tiny("half"), ALU.mult)
                dve.drain()
                reduce_angle(b, cc)
                dve.tensor_scalar(cc, b, 1 / TWO_PI, None, ALU.mult)
                dve.drain()
                dve.tensor_scalar(tiny("phi_hi"), cc, ROUND14, ROUND14, ALU.add, ALU.subtract)
                dve.drain()
                dve.tensor_tensor(tiny("phi_lo"), cc, tiny("phi_hi"), ALU.subtract)
                dve.drain().then_inc(turns_ready, 1)

            def factor():
                a, b, cc, d = tiny("s5a"), tiny("s5b"), tiny("s5c"), tiny("s5d")
                dve.wait_ge(trig_ready, 1)
                dve.tensor_tensor(a, tiny("half"), tiny("half"), ALU.mult)
                dve.drain()
                dve.tensor_scalar(a, a, -2.0, 1.0, ALU.mult, ALU.add)
                dve.tensor_tensor(b, tiny("sin"), decay, ALU.mult)
                dve.drain()
                dve.tensor_tensor(a, a, decay, ALU.mult)
                dve.tensor_tensor(cc, lam_re, lam_re, ALU.mult)
                dve.tensor_tensor(d, lam_im, lam_im, ALU.mult)
                dve.drain()
                dve.tensor_scalar(a, a, -1.0, None, ALU.add)
                dve.tensor_tensor(cc, cc, d, ALU.add)
                dve.drain()
                dve.reciprocal(cc, cc)
                dve.tensor_tensor(factor_re, a, lam_re, ALU.mult)
                dve.tensor_tensor(d, b, lam_im, ALU.mult)
                dve.tensor_tensor(factor_im, b, lam_re, ALU.mult)
                dve.tensor_tensor(a, a, lam_im, ALU.mult)
                dve.drain()
                dve.tensor_tensor(factor_re, factor_re, d, ALU.add)
                dve.tensor_tensor(factor_im, factor_im, a, ALU.subtract)
                dve.drain()
                dve.tensor_tensor(factor_re, factor_re, cc, ALU.mult)
                dve.tensor_tensor(factor_im, factor_im, cc, ALU.mult)
                dve.drain()

            def mod_half(k, i):
                dve.wait_ge(mod_in[i], 16 * (k + 1))
                half = ACC[:, i * MODH:(i + 1) * MODH]
                dve.scalar_tensor_tensor(half, MODR[i], CVEC[:, bass.ds(k, 1)], half, ALU.mult, ALU.add
                                         ).then_inc(mod_used[i], 1)

            def mod2_third(p):
                dve.wait_ge(mod2_in[p % 2], 16 * (p // 2 + 1))
                third = ACC2[:, p % 3 * MODQ:(p % 3 + 1) * MODQ]
                dve.scalar_tensor_tensor(third, MR[p % 2], CVEC[:, p // 3:p // 3 + 1], third, ALU.mult, ALU.add
                                         ).then_inc(mod2_used[p % 2], 1)

            def make_gate_row(bank, grow, gbr, times):
                dve.wait_ge(rows_ps, times)
                dve.wait_ge(gate_b_in, 32 * times)
                dve.scalar_tensor_tensor(grow, psum(bank), 1.0, gbr, ALU.add, ALU.add).then_inc(rows_sb, 1)

            def make_columns(j, bank, times):
                norm_g, norm_b = (AHEAD[:, AC[x]][:, j * KD:(j + 1) * KD] for x in ("norm_g", "norm_b"))
                dve.wait_ge(cols_ps, times)
                dve.tensor_tensor(sc4[:, j], psum(bank, bank + 2).rearrange("p (k s x) -> p s k x", k=KD, s=2)[:, :, :, 0],
                                  AHEAD[:, AC["mod_b"]].rearrange("p (j s k) -> p j s k", j=2, s=2)[:, j], ALU.add)
                dve.drain()
                dve.tensor_scalar(sc4[:, j, 1, :], sc4[:, j, 1, :], 1.0, None, ALU.add)
                dve.drain()
                dve.tensor_tensor(tiny("rope_b", 0, 8), sc4[:, j, 1, :], norm_b, ALU.mult)
                dve.drain()
                dve.tensor_tensor(sc4[:, j, 1, :], sc4[:, j, 1, :], norm_g, ALU.mult)
                dve.tensor_tensor(sc4[:, j, 0, :], sc4[:, j, 0, :], tiny("rope_b", 0, 8), ALU.add)
                dve.drain().then_inc(sc_ready, 1)

            def make_h(j, banks):
                ht3 = HT.rearrange("p (k t) -> p k t", k=KD)
                for g in range(4):
                    if j or g >= 2:
                        dve.wait_ge(h_hi, 2 + g + 1 if j else g - 1)
                    if g < 3:
                        for k in (2 * g, 2 * g + 1):
                            dve.tensor_scalar(ht3[:, k, :], PS[:, banks[g], k % 2 * S:k % 2 * S + S],
                                              sc4[:, j, 1, k:k + 1], sc4[:, j, 0, k:k + 1], ALU.mult, ALU.add)
                        dve.drain()
                    dve.tensor_tensor(HL[:, g * 512:(g + 1) * 512], HT[:, g * 512:(g + 1) * 512],
                                      HH[:, g * 512:(g + 1) * 512].bitcast(F32), ALU.subtract).then_inc(h_ready, 1)

            dve.wait_ge(const_in, 16)
            dve.wait_ge(pos_in, 16)
            dve.tensor_copy(RT[:, 2:4], RT[:, 0:NB].bitcast(I32))
            dve.drain()
            dve.tensor_tensor(tiny("rope_a").rearrange("p (b i) -> p b i", b=NB), wide(RT[:, 2:4], 8),
                              rep(con("inv"), NB), ALU.mult)
            dve.drain()
            reduce_angle(tiny("rope_a"), tiny("rope_b"))
            dve.drain().then_inc(angle_ready, 1)
            dve.wait_ge(ahead_in, 16)
            phase()
            dve.wait_ge(angle_ready, 2)
            dve.tensor_tensor(ROPE[:, 0:16], ROPE[:, 0:16], ROPE[:, 0:16], ALU.mult)
            dve.drain()
            dve.tensor_scalar(ROPE[:, 0:16], ROPE[:, 0:16], -2.0, 1.0, ALU.mult, ALU.add)
            dve.wait_ge(c_in, 16)
            dve.wait_ge(acc_zero, 1)
            phases(dve, slice(0, 4))
            for k in range(KD):
                if k == KD // 2:
                    factor()
                dve.drain()
                dve.wait_ge(mod_in[k % 4], 16 * (k // 4 + 1))
                dve.scalar_tensor_tensor(ACC, STAGE[k % 4], CVEC[:, k:k + 1], ACC, ALU.mult, ALU.add
                                         ).then_inc(mod_used[k % 4], 1)
            make_gate_row(2, GROW, GBR, 1)
            make_columns(0, 6, 1)
            dve.wait_ge(hi_done[2], 1)
            dve.tensor_tensor(WL[2], RAW[0], WH[2].bitcast(F32), ALU.subtract).then_inc(lo_done[2], 1)
            end_of_layer(dve, 0)

            with dve.Fori(0, DEPTH) as l:
                make_h(0, (0, 1, 4, 5))

                def projection(name):
                    n, i = UNITS.index(name), turn(name)
                    dve.wait_ge(used[n % 3], uses(n))
                    return psum(i % 2).rearrange("p (b n) -> p b n", b=NB), turn_free[i % 2]

                dve.memset(cin3[:, :, 0:3], 0.0)
                dve.wait_ge(acc2_zero, 1)
                mod2_third(0)
                dve.wait_ge(params_in, 16)
                dve.wait_ge(turn_free[0], 1)
                dve.wait_ge(turn_free[1], 1)
                dve.drain()
                for tap in range(4):
                    for c in range(4):
                        w = par("conv_w")[:, 4 * c + tap:4 * c + tap + 1]
                        src = cin3[:, c, tap:tap + S]
                        if tap == 0:
                            dve.tensor_scalar(xbc3[:, c, :], src, w, par("conv_b")[:, c:c + 1], ALU.mult, ALU.add)
                        else:
                            dve.scalar_tensor_tensor(xbc3[:, c, :], src, w, xbc3[:, c, :], ALU.mult, ALU.add)
                    dve.drain()
                dve.drain().then_inc(conv_ready, 1)
                mod2_third(1)

                src, free = projection("P2")
                dve.tensor_copy(misc3[:, :, 0:200], src[:, :, 0:200]).then_inc(free, 1)
                dve.drain()
                dt_v, dt_e = tiny("dt_v"), tiny("dt_e")
                dt_v3 = dt_v.rearrange("p (b h) -> p b h", b=NB)
                dve.tensor_tensor(dt_v3, misc3[:, :, 196:200], rep(par("dt_bias"), NB), ALU.add)
                dve.tensor_scalar(tiny("wi").rearrange("p (b h) -> p b h", b=NB), misc3[:, :, 192:196], 1 / 16, None,
                                  ALU.mult)
                dve.tensor_scalar(tiny("glu_hb"), par("glu_b"), 0.5, None, ALU.mult)
                dve.drain()
                dve.scalar_tensor_tensor(dt_e, dt_v, -1.0, dt_v, ALU.mult, ALU.max).then_inc(dt_abs, 1)
                for g in (8, 9):
                    dve.tensor_copy(qk4[:, :, g, :], misc3[:, :, 0:64])
                    dve.tensor_copy(qk4[:, :, g + 2, :], misc3[:, :, 128:192])
                def rope_source(name, g):
                    src, free = projection(name)
                    dve.tensor_copy(qk4[:, :, g:g + 4, :], src.rearrange("p b (g d) -> p b g d", g=4)).then_inc(free, 1)

                rope_source("P3", 0)
                dt, adt = tiny("dt"), tiny("adt")
                dve.wait_ge(dt_log, 1)
                dve.scalar_tensor_tensor(dt, dt_v, 0.0, dt_e, ALU.max, ALU.add)
                dve.drain()
                dve.scalar_tensor_tensor(adt.rearrange("p (b h) -> p b h", b=NB), dt.rearrange("p (b h) -> p b h", b=NB),
                                         -1.0, rep(tiny("exp_a"), NB), ALU.mult, ALU.mult)
                dve.drain().then_inc(adt_ready, 1)
                rope_source("P4", 4)
                mod2_third(2)
                dve.drain()
                cos, sin = (ROPE[:, a:a + 16].rearrange("p (b i) -> p b i", b=NB).unsqueeze(2)
                            .broadcast_to([P, NB, 12, 8]) for a in (0, 16))
                first, second = qk4[:, :, :, 0:8], qk4[:, :, :, 8:16]
                r = [WORK[:, 2304 + 192 * i:2496 + 192 * i].rearrange("p (b g i) -> p b g i", b=NB, g=12) for i in range(4)]
                dve.tensor_tensor(r[0], first, cos, ALU.mult)
                dve.tensor_tensor(r[1], second, sin, ALU.mult)
                dve.tensor_tensor(r[2], second, cos, ALU.mult)
                dve.tensor_tensor(r[3], first, sin, ALU.mult)
                dve.drain()
                dve.tensor_tensor(first, r[0], r[1], ALU.subtract)
                dve.tensor_tensor(second, r[2], r[3], ALU.add)
                dve.drain().then_inc(qk_ready, 1)

                dve.wait_ge(x_tok, 1)
                heads = lambda t, n: t.rearrange("p (h d) -> p h d", h=n)
                dve.tensor_tensor(heads(XDT, 8), heads(XT, 8), wide(dt, 64), ALU.mult)
                dve.tensor_tensor(YS.rearrange("p (b h d) -> p b h d", b=NB, h=4), XT.rearrange(
                    "p (b h d) -> p b h d", b=NB, h=4), wide(par("ssd_d"), 64).unsqueeze(1).broadcast_to(
                        [P, NB, 4, 64]), ALU.mult)
                dve.wait_ge(ssd2_ps, 1)
                dve.tensor_copy(tiny("acum"), PS[:, 4, 0:8])
                dve.drain()
                for bh in range(8):
                    dve.tensor_scalar(LM[:, bh * P:(bh + 1) * P], PS[:, 5 + bh // 4, bh % 4 * P:bh % 4 * P + P],
                                      tiny("acum", bh, bh + 1), 0.0, ALU.subtract, ALU.min)
                dve.drain().then_inc(decay_log, 1)
                dve.wait_ge(decay_exp, 1)
                dve.tensor_tensor(heads(DECX, 4), heads(XDT[:, 0:256], 4), heads(LM[:, 0:512], 4)[:, :, P - 1:P]
                                  .broadcast_to([P, 4, 64]), ALU.mult)
                dve.drain()
                dve.tensor_tensor(heads(LM, 8), heads(LM, 8), rep(con("upper"), 8), ALU.mult)
                dve.drain()
                dve.tensor_tensor(LM.rearrange("p (g j l) -> p g j l", g=4, j=2),
                                  LM.rearrange("p (g j l) -> p g j l", g=4, j=2),
                                  psum(7).rearrange("p (g l) -> p g l", g=4).unsqueeze(2).broadcast_to([P, 4, 2, P]),
                                  ALU.mult)
                dve.drain().then_inc(mask_ready, 1)
                def norm_stats(src, b, width, mv):
                    st = tiny("stats", 12 * b, 12 * b + 12)
                    for c in range(width // 512 or 1):
                        dve.bn_stats(st[:, 6 * c:6 * c + 6], src[:, 512 * c:512 * c + min(width, 512)])
                    dve.drain()
                    dve.bn_aggr(mv, st[:, 0:6 * (width // 512 or 1)])

                vi = turn("P6")
                dve.wait_ge(turn_free[vi % 2], vi // 2 + 1)
                for b in range(NB):
                    norm_stats(V[:, b * W:(b + 1) * W], b, W, tiny("mv", 2 * b, 2 * b + 2))
                dve.drain()
                means = tiny("mv").rearrange("p (b s) -> p b s", b=NB)
                dve.tensor_scalar(tiny("mvg", 0, 2), means[:, :, 1], EPS_LN, None, ALU.add)
                dve.drain().then_inc(v_var, 1)
                dve.wait_ge(v_root, 1)
                dve.reciprocal(tiny("mvg", 0, 2), tiny("mvg", 0, 2))
                dve.drain()
                for b in range(NB):
                    dve.tensor_scalar(V[:, b * W:(b + 1) * W], V[:, b * W:(b + 1) * W], tiny("mv", 2 * b, 2 * b + 1),
                                      tiny("mvg", b, b + 1), ALU.subtract, ALU.mult)
                dve.drain()
                dve.tensor_tensor(heads(V, 2), heads(V, 2), rep(par("gm_g"), 2), ALU.mult)
                dve.drain()
                dve.tensor_tensor(heads(V, 2), heads(V, 2), rep(par("gm_b"), 2), ALU.add)
                dve.tensor_tensor(heads(par("sg_w"), 4), heads(par("sg_w"), 4), rep(con("upper"), 4), ALU.mult)
                dve.drain().then_inc(v_ready, 1)

                def branch_lo(i, src, scale=None):
                    dve.wait_ge(y_hi, i + 1)
                    if scale is None:
                        ins = dve.tensor_tensor(YL[0], src, YH[0].bitcast(F32), ALU.subtract)
                    else:
                        ins = dve.scalar_tensor_tensor(YL[0], src, scale, YH[0].bitcast(F32), ALU.mult, ALU.subtract)
                    ins.then_inc(y_lo, 1)

                def mix_lo(g):
                    at = slice(g * 512, (g + 1) * 512)
                    dve.wait_ge(mix_hi, g + 1)
                    dve.scalar_tensor_tensor(HL[:, at], MG[:, at], 0.5, HH[:, at].bitcast(F32), ALU.mult,
                                             ALU.subtract).then_inc(mix_ready, 1)

                def merge(i):
                    for part in range(4):
                        t, gate = turn(f"B{i}", part), turn(f"G{4 * i + part}")
                        dve.wait_ge(turn_free[gate % 2], gate // 2 + 1)
                        sig = SIG[:, (4 * i + part) % 8 * 512:((4 * i + part) % 8 + 1) * 512]
                        mg = MG[:, part * 512:(part + 1) * 512]
                        dve.wait_ge(branch_ps, 4 * i + part + 1)
                        dve.scalar_tensor_tensor(V if i else mg, sig, 1.0, psum(t % 2), ALU.add, ALU.mult
                                                 ).then_inc(turn_free[t % 2], 1)
                        dve.drain()
                        if i:
                            ins = dve.tensor_tensor(mg, mg, V, ALU.add)
                            if i == 3:
                                ins.then_inc(merged, 1)
                            dve.drain()
                        if i == 3 and part:
                            mix_lo(part - 1)

                mod2_third(3)

                dve.wait_ge(gm_ps, 1)
                dve.tensor_tensor(V.rearrange("p (c b t) -> p c b t", c=2, b=NB), psum(6).rearrange(
                    "p (c b t) -> p c b t", c=2, b=NB), heads(par("sg_b"), 2).unsqueeze(2).broadcast_to([P, 2, NB, P]),
                    ALU.add)
                dve.drain()
                ui = turn("P7")
                dve.wait_ge(turn_free[ui % 2], ui // 2 + 1)
                dve.tensor_tensor(V, V, GU, ALU.mult).then_inc(gm_ready, 1)
                def score(b, piece):
                    n, s, left = NKEY[b], SCORE[b], LEFT[b]
                    dve.wait_ge(relu_sb, b + 1)
                    for h in range(4):
                        w = tiny("wi", 4 * b + h, 4 * b + h + 1)
                        rl = RL[b][:, h * n:(h + 1) * n]
                        if h == 0:
                            dve.tensor_scalar(s, rl, w, None, ALU.mult)
                        else:
                            dve.scalar_tensor_tensor(s, rl, w, s, ALU.mult, ALU.add)
                        dve.drain()
                    late_keys = s[:, n - P:n]
                    dve.tensor_tensor(late_keys, late_keys, con("lower"), ALU.mult)
                    dve.drain()
                    dve.tensor_tensor(late_keys, late_keys, con("floor"), ALU.add)
                    dve.drain()
                    src = s
                    for eight in range(NSEL // 8):
                        if eight == 4:
                            mod2_third(piece)
                        if eight == 6 and b == 1:
                            branch_lo(0, psum(6))
                        dve.max(tiny("top"), src)
                        dve.drain()
                        dve.match_replace(left, tiny("top"), src, TAKEN)
                        dve.drain()
                        src = left
                    dve.tensor_tensor(left, left, s, ALU.not_equal)
                    dve.drain()
                    dve.tensor_tensor(left[:, n - P:n], left[:, n - P:n], con("lower"), ALU.mult)
                    dve.drain()
                    dve.tensor_scalar(left, left, -1.0, AWAY, ALU.add, ALU.mult)
                    dve.drain()

                def masked_logits(b):
                    n = NKEY[b]
                    dve.wait_ge(logit_ps, b + 1)
                    lg = psum(5) if b == 0 else psum(2, 4)
                    dve.scalar_tensor_tensor(heads(RL[b], 4), heads(lg, 4), 0.125, rep(LEFT[b], 4), ALU.mult, ALU.add)
                    dve.drain()
                    neg = tiny("neg", 4 * b, 4 * b + 4)
                    dve.tensor_reduce(neg, heads(RL[b], 4), AX.X, ALU.max)
                    dve.drain()
                    dve.tensor_scalar(neg, neg, -1.0, None, ALU.mult)
                    dve.drain().then_inc(logit_max, 1)

                def probabilities(b):
                    den = tiny("den", 4 * b, 4 * b + 4)
                    dve.wait_ge(exp_ready, b + 1)
                    dve.reciprocal(den, den)
                    dve.drain()
                    dve.tensor_tensor(heads(RL[b], 4), heads(RL[b], 4), wide(den, NKEY[b]), ALU.mult
                                      ).then_inc(prob_ready, 1)

                mod2_third(4)
                score(0, 5)
                mod2_third(6)
                dve.wait_ge(ssd3_ps, 1)
                dve.tensor_tensor(YS, YS, psum(4), ALU.add)
                dve.wait_ge(ssd4_ps, 1)
                dve.tensor_tensor(heads(XDT[:, 0:256], 4), heads(PS[:, 7, 0:256], 4), wide(tiny("acum_e"), 64), ALU.mult)
                dve.drain()
                dve.tensor_tensor(YS[:, 256:512], YS[:, 256:512], XDT[:, 0:256], ALU.add)
                dve.drain()
                zi = turn("P8")
                dve.wait_ge(turn_free[zi % 2], zi // 2 + 1)
                dve.tensor_tensor(YS, YS, Z, ALU.mult)
                dve.drain()
                dve.tensor_tensor(XDT, YS, YS, ALU.mult)
                dve.drain()
                dve.tensor_reduce(tiny("ms"), heads(XDT, 4), AX.X, ALU.add)
                dve.drain()
                dve.tensor_scalar(tiny("ms"), tiny("ms"), 1 / 128, EPS_RMS, ALU.mult, ALU.add).then_inc(rms_sq, 1)
                mod2_third(7)
                dve.wait_ge(rms_root, 1)
                dve.reciprocal(tiny("ms"), tiny("ms"))
                dve.drain()
                dve.tensor_tensor(heads(YS, 4), heads(YS, 4), wide(tiny("ms"), P), ALU.mult)
                dve.drain()
                dve.tensor_tensor(heads(YS, 2), heads(YS, 2), rep(par("norm_g"), 2), ALU.mult)
                dve.drain().then_inc(ssd_ready, 1)

                score(1, 8)
                mod2_third(9)
                merge(0)
                mod2_third(10)
                masked_logits(0)
                masked_logits(1)
                mod2_third(11)
                probabilities(0)
                probabilities(1)
                branch_lo(1, V)
                mod2_third(12)

                s5c = par("s5_c").rearrange("p (r j c) -> p r j c", r=2, j=8)
                fre, fim = (wide(S5D[:, a:a + 8], 32) for a in (8, 16))
                t = [WORK[:, 256 * i:256 * i + 256] for i in range(4)]
                t3 = [x.rearrange("p (j c) -> p j c", j=8) for x in t]
                dve.wait_ge(ssd5_ps, 1)
                dve.tensor_tensor(t3[0], s5c[:, 0], fre, ALU.mult)
                dve.tensor_tensor(t3[1], s5c[:, 1], fim, ALU.mult)
                dve.tensor_tensor(t3[2], s5c[:, 0], fim, ALU.mult)
                dve.tensor_tensor(t3[3], s5c[:, 1], fre, ALU.mult)
                dve.drain()
                dve.tensor_tensor(CRE, t[0], t[1], ALU.subtract)
                dve.scalar_tensor_tensor(CIM, t[2], -1.0, t[3], ALU.mult, ALU.subtract)
                dve.drain().then_inc(c_ready, 1)
                mod2_third(13)

                def quarter_inputs(i):
                    cos, sin = COS[:, 512 * i:512 * i + 512], SIN[:, 512 * i:512 * i + 512]
                    vre, vim = (psum(2), psum(3)) if i % 2 == 0 else (psum(5), psum(6))
                    dve.wait_ge(s5v_ps, i + 1)
                    dve.tensor_tensor(B5[0], vre, cos, ALU.mult)
                    dve.tensor_tensor(B5[1], vim, sin, ALU.mult)
                    dve.tensor_tensor(B5[2], vim, cos, ALU.mult)
                    dve.tensor_tensor(B5[3], vre, sin, ALU.mult).then_inc(s5v_read, 1)
                    dve.drain()
                    dve.tensor_tensor(B5[0], B5[0], B5[1], ALU.add)
                    dve.tensor_tensor(B5[2], B5[2], B5[3], ALU.subtract)
                    dve.drain()

                def quarter(i, piece=None):
                    if i not in (1, 3):
                        quarter_inputs(i)
                    cos, sin = COS[:, 512 * i:512 * i + 512], SIN[:, 512 * i:512 * i + 512]
                    for src, dst in ((B5[0], B5[1]), (B5[2], B5[3])):
                        for c in range(2):
                            at = slice(c * S, (c + 1) * S)
                            j = 2 * i + c
                            dve.tensor_tensor_scan(dst[:, at], S5D[:, j:j + 1].broadcast_to([P, S]), src[:, at], 0.0,
                                                   ALU.mult, ALU.add)
                    dve.drain()
                    if piece is not None:
                        mod2_third(piece)
                    if i:
                        dve.wait_ge(s5y_ps, i)
                    dve.tensor_tensor(B5[0], B5[1], cos, ALU.mult)
                    dve.tensor_tensor(B5[2], B5[3], sin, ALU.mult)
                    dve.drain()
                    dve.tensor_tensor(B5[4], B5[0], B5[2], ALU.subtract)
                    dve.drain()
                    dve.tensor_tensor(B5[0], B5[3], cos, ALU.mult)
                    dve.tensor_tensor(B5[2], B5[1], sin, ALU.mult)
                    dve.drain()
                    dve.tensor_tensor(B5[5], B5[0], B5[2], ALU.add)
                    dve.drain().then_inc(s5h_ready, 1)

                quarter(0)
                mod2_third(14)
                quarter_inputs(1)
                mod2_third(15)
                merge(1)
                mod2_third(16)
                branch_lo(2, psum(4))
                quarter(1, 17)
                mod2_third(18)
                quarter(2, 19)
                mod2_third(20)
                quarter_inputs(3)
                merge(2)
                mod2_third(21)
                quarter(3, 22)
                mod2_third(23)
                dve.wait_ge(s5y_ps, 4)
                for c in range(CW):
                    at = slice(c * S, (c + 1) * S)
                    dve.scalar_tensor_tensor(B5[0][:, at], UT[:, at], par("s5_d")[:, c:c + 1], PS[:, 7, at], ALU.mult,
                                             ALU.add)
                dve.drain().then_inc(s5y_ready, 1)
                dve.wait_ge(glu_tanh, 1)
                dve.scalar_tensor_tensor(B5[2], B5[1], 1.0, B5[0], ALU.add, ALU.mult)
                dve.drain().then_inc(glu_ready, 1)
                branch_lo(3, B5[2], 0.5)
                make_gate_row(5, GROW2, GBR2, 1)
                make_columns(1, 2, 1)
                merge(3)
                mix_lo(3)

                def norm(i, bank, done):
                    def gated(b):
                        at = slice(b * D, (b + 1) * D)
                        dve.tensor_tensor(LNT[:, at], psum(bank + 2 * b, bank + 2 * b + 2), NRM[:, 2 * D:3 * D], ALU.mult)

                    def residual(b):
                        at = slice(b * D, (b + 1) * D)
                        dve.drain()
                        dve.scalar_tensor_tensor(X[:, at], X[:, at], ALPHA, LNT[:, at], ALU.mult, ALU.add)
                        dve.drain()
                        norm_stats(X[:, at], b, D, tiny("mv", 2 * b, 2 * b + 2))
                        dve.drain()
                        dve.tensor_scalar(tiny("var", b, b + 1), tiny("mv", 2 * b + 1, 2 * b + 2), EPS_LN, None, ALU.add
                                          ).then_inc(ln_var, 1)

                    dve.wait_ge(norm_in, 48 * i)
                    dve.wait_ge(done, 1)
                    gated(0)
                    residual(0)
                    dve.wait_ge(done, 2)
                    gated(1)
                    dve.wait_ge(ln_root, 2 * i - 1)
                    dve.reciprocal(tiny("var", 0, 1), tiny("var", 0, 1))
                    dve.drain()
                    dve.scalar_tensor_tensor(tiny("shift"), tiny("mv", 0, 1), -1.0, tiny("var", 0, 1), ALU.mult, ALU.mult
                                             ).then_inc(ln_scale, 1)
                    residual(1)
                    dve.wait_ge(ln_root, 2 * i)
                    dve.reciprocal(tiny("var", 1, 2), tiny("var", 1, 2))
                    dve.drain()
                    dve.tensor_scalar(XN[:, D:2 * D], X[:, D:2 * D], tiny("mv", 2, 3), tiny("var", 1, 2),
                                      ALU.subtract, ALU.mult).then_inc(xn1_ready, 1)

                def affine(i):
                    dve.wait_ge(xn0_ready, i)
                    for op, a in ((ALU.mult, 0), (ALU.add, D)):
                        src = XN if op == ALU.mult else X
                        dve.drain()
                        dve.tensor_tensor(X[:, 0:D], src[:, 0:D], NRM[:, a:a + D], op)
                        dve.tensor_tensor(X[:, D:3 * 512], src[:, D:3 * 512], NRM[:, a:a + 512], op)
                    dve.drain().then_inc(ln_done, 1)

                norm(1, 2, wout_ps)
                dve.wait_ge(router_hi, 1)
                dve.tensor_tensor(RWL, RW, RWH.bitcast(F32), ALU.subtract).then_inc(router_ready, 1)
                make_h(1, (6, 7, 0, 1))
                lo_part(N_W1S + 1)
                affine(1)

                sig, biased, left = RT[:, 0:64], RT[:, 64:128], RT[:, 128:192]
                m4 = lambda t: t.rearrange("p (g i) -> p g i", i=4)
                hi2, lo2 = RT[:, 192:224], RT[:, 224:256]
                s2 = lambda t: t.rearrange("p (g i) -> p g i", i=2)
                best, second_, both = RT[:, 256:272], RT[:, 272:288], RT[:, 288:304]
                better, equal = RT[:, 320:448], RT[:, 448:576]
                g8 = lambda t: t.rearrange("p (b i) -> p b i", b=NB)
                g88 = lambda t: t.rearrange("p (b i j) -> p b i j", b=NB, i=8)
                dve.wait_ge(sig_ps, 1)
                dve.tensor_copy(sig, PS[:, 2, 0:64])
                dve.tensor_tensor(g8(biased), g8(PS[:, 2, 0:64]), rep(ROUT, NB), ALU.add)
                dve.drain()
                dve.tensor_tensor(s2(hi2), m4(biased)[:, :, 0:2], m4(biased)[:, :, 2:4], ALU.max)
                dve.tensor_tensor(s2(lo2), m4(biased)[:, :, 0:2], m4(biased)[:, :, 2:4], ALU.min)
                dve.drain()
                dve.tensor_tensor(best, s2(hi2)[:, :, 0], s2(hi2)[:, :, 1], ALU.max)
                dve.tensor_tensor(second_, s2(hi2)[:, :, 0], s2(hi2)[:, :, 1], ALU.min)
                dve.tensor_tensor(both, s2(lo2)[:, :, 0], s2(lo2)[:, :, 1], ALU.max)
                dve.drain()
                dve.tensor_tensor(second_, second_, both, ALU.max)
                dve.drain()
                dve.tensor_tensor(both, best, second_, ALU.add)
                dve.drain()
                mine = g8(both).unsqueeze(3).broadcast_to([P, NB, 8, 8])
                other = g8(both).unsqueeze(2).broadcast_to([P, NB, 8, 8])
                dve.tensor_tensor(g88(better), other, mine, ALU.is_gt)
                dve.tensor_tensor(g88(equal), other, mine, ALU.is_equal)
                dve.drain()
                dve.tensor_tensor(g8(equal), g8(equal), rep(con("before"), NB), ALU.mult)
                dve.drain()
                dve.tensor_tensor(better, better, equal, ALU.add)
                dve.drain()
                dve.tensor_reduce(best, better.rearrange("p (g j) -> p g j", j=8), AX.X, ALU.add)
                dve.drain()
                dve.tensor_scalar(best, best, 3.5, None, ALU.is_lt)
                dve.drain()
                dve.tensor_scalar(second_, best, -1.0, AWAY, ALU.add, ALU.mult)
                dve.tensor_tensor(m4(biased), m4(biased), wide(best, 4), ALU.mult)
                dve.drain()
                dve.tensor_tensor(m4(biased), m4(biased), wide(second_, 4), ALU.add)
                dve.drain()
                for b in range(NB):
                    dve.max(tiny("top"), biased[:, b * E:(b + 1) * E])
                    dve.drain()
                    dve.match_replace(left[:, b * E:(b + 1) * E], tiny("top"), biased[:, b * E:(b + 1) * E], TAKEN)
                    dve.drain()
                dve.tensor_tensor(left, left, biased, ALU.not_equal)
                dve.drain()
                dve.tensor_tensor(left, left, sig, ALU.mult)
                dve.drain()
                dve.tensor_reduce(best[:, 0:2], g8(left), AX.X, ALU.add)
                dve.drain()
                dve.reciprocal(best[:, 0:2], best[:, 0:2])
                dve.drain()
                for b in range(NB):
                    dve.tensor_scalar(left[:, b * E:(b + 1) * E], left[:, b * E:(b + 1) * E], best[:, b:b + 1], 2.5,
                                      ALU.mult, ALU.mult)
                dve.memset(G[0], 1.0)
                dve.drain().then_inc(gates_ready, 1)

                def products(x, k, n):
                    dve.wait_ge(silu_done, 4 * k + x + 1)
                    dve.wait_ge(used[n % 3], 4 * k + uses(n))
                    dve.tensor_tensor(T[x % 2], SL[x % 2], psum(5 + 2 * (x % 2)), ALU.mult).then_inc(b_read, 1)
                    dve.drain()
                    if n != N_W1S + 1:
                        dve.wait_ge(g_in[x % 2], 16 * (2 * k + (x + 1) // 2))
                    dve.tensor_tensor(heads(T[x % 2], 2), heads(T[x % 2], 2), rep(G[x % 2], 2), ALU.mult
                                      ).then_inc(act_ready, 1)
                    dve.drain()

                def activation_lo(x, k=0):
                    dve.wait_ge(act_hi, 4 * k + x + 1)
                    dve.tensor_tensor(YL[x % 2], T[x % 2], YH[x % 2].bitcast(F32), ALU.subtract).then_inc(act_lo, 1)

                def four_experts(k):
                    for i in range(4):
                        n = N_W1S + 2 + 3 * i
                        if i or not isinstance(k, int):
                            lo_part(n + 1, k)
                        activation_lo(i, k)
                        lo_part(n + 2, k)
                        products(i + 1, k, n + 1)
                        lo_part(n + 3, k)
                        if i == 0 and isinstance(k, int):
                            dve.wait_ge(acc_zero, 1)
                        if i % 2 == 0:
                            mod_half(k, i // 2)

                products(0, 0, N_W1S + 1)
                dve.wait_ge(gates_ps, 1)
                dve.tensor_copy(GT[0:E, :], PS[0:E, 2, 0:S]).then_inc(gates_sb, 1)
                phase()
                four_experts(0)
                factor()
                with dve.Fori(1, KD) as k:
                    four_experts(k)
                activation_lo(E)
                dve.wait_ge(ahead_in, 16)
                make_gate_row(4, GROW, GBR, 2)
                norm(2, 0, moe_ps)
                make_columns(0, 6, 2)
                affine(2)
                end_of_layer(dve, l + 1)

        @block.tensor
        def _(pe):
            def product(out, parts, first=True, last=True):
                total = 3 * len(parts)
                done = 0
                for (wh, wl), (mh, ml) in parts:
                    for a, b in ((wh, mh), (wl, mh), (wh, ml)):
                        ins = pe.matmul(out, a, b, start=first and done == 0, stop=last and done == total - 1)
                        done += 1
                return ins

            def slot(n, k=0):
                if n >= 3:
                    pe.wait_ge(lo_done[n % 3], 4 * k + made(n))
                return WH[n % 3], WL[n % 3]

            def h_times(out, wh, wl, h_from=None):
                for k in range(KD):
                    if h_from is not None and k % 2 == 0:
                        pe.wait_ge(h_ready, h_from + k // 2 + 1)
                    ins = product(out, [((wh[:, k, :], wl[:, k, :]), (hh[:, k, :], hl[:, k, :]))], k == 0, k == KD - 1)
                return ins

            def by_channel(out, wh, wl, h_from=None):
                wh, wl = (t.rearrange("p (k n) -> p k n", k=KD) for t in (wh, wl))
                for m in range(2):
                    at = slice(m * P, (m + 1) * P)
                    ins = h_times(out[:, m * S:(m + 1) * S], wh[:, :, at], wl[:, :, at], None if m else h_from)
                return ins

            def by_token(out, wh, wl):
                w = [t.rearrange("p (k n) -> p k n", k=KD) for t in (wh, wl)]
                for b in range(NB):
                    ins = product(out[:, b * W:(b + 1) * W],
                                  [((hh[:, k, b * P:(b + 1) * P], hl[:, k, b * P:(b + 1) * P]),
                                    (w[0][:, k, :], w[1][:, k, :])) for k in range(KD)])
                return ins

            def transpose_x(src, b, banks):
                by_k = src.rearrange("p (b q k) -> p b k q", b=NB, k=KD)
                for g in range(4):
                    for k in (2 * g, 2 * g + 1):
                        at = k % 2 * S + b * P
                        ins = pe.transpose(PS[:, banks[g], at:at + P], by_k[:, b, k, :], con("ident"))
                    if b == NB - 1:
                        ins.then_inc(xt_ps, 1)

            def sum_rows(acc, bank, gate_bank):
                ones = con("ones")[:, 0:64]
                for half in range(2):
                    for r in range(2):
                        at = r * D + half * 512
                        ins = pe.matmul(PS[64 * r:64 * r + 64, bank + half, :], ones, acc[:, at:at + 512],
                                        start=True, stop=True)
                ins.then_inc(sums_ps, 1)
                for r in range(2):
                    at = 2 * D + r * 512
                    ins = pe.matmul(PS[64 * r:64 * r + 64, gate_bank, :], ones, acc[:, at:at + 512],
                                    start=True, stop=True)
                ins.then_inc(rows_ps, 1)

            def sum_columns(sums, bank, times):
                pe.wait_ge(sums_sb, times)
                by_k = sums.rearrange("p (q k) -> p k q", k=KD)
                for k in range(KD):
                    ins = pe.transpose(PS[:, bank + k // 4, k % 4 * P:k % 4 * P + P], by_k[:, k, :], con("ident"))
                ins.then_inc(cols_ps, 1)

            for i in range(4):
                pe.wait_ge(mod_used[i], 2)
            sum_rows(ACC, 6, 2)
            pe.wait_ge(x_in, 16)
            for b in range(NB):
                transpose_x(X, b, (0, 1, 4, 5))
            sum_columns(SUMS, 6, 1)
            end_of_layer(pe, 0)
            with pe.Fori(0, DEPTH) as l:
                def xbc_t(c, b):
                    return xbc3[:, c, b * P:(b + 1) * P]

                def qk_rows(chunk, h, a, n):
                    return QT[64 * (h % 2):64 * (h % 2) + 64, chunk * S + a:chunk * S + a + n]

                def heads_by_rows(queries, keys, done):
                    for half in range(2):
                        pe.drain()
                        for h in (half, half + 2):
                            ins = pe.matmul(PS[:, 5, h * P:(h + 1) * P], qk_rows(queries + h // 2, h, 0, P),
                                            qk_rows(keys, h, 0, P), start=True, stop=True)
                        if half:
                            ins.then_inc(done, 1)
                        for h in (half, half + 2):
                            ins = pe.matmul(PS[:, 2 + h // 2, h % 2 * S:h % 2 * S + S],
                                            qk_rows(queries + h // 2, h, P, P), qk_rows(keys, h, 0, S),
                                            start=True, stop=True)
                        if half:
                            ins.then_inc(done, 1)

                def small(name):
                    if name == "ssd1":
                        pe.wait_ge(xbc_ready, 1)
                        for b in range(NB):
                            for c in range(2):
                                pe.transpose(PS[:, 2, b * W + c * P:b * W + (c + 1) * P], xbc_t(c, b), con("ident"))
                        pe.transpose(PS[:, 3, 0:P], xbc_t(2, 0), con("ident")).then_inc(ssd1_ps, 1)
                    elif name == "ssd2":
                        pe.wait_ge(adt_ready, 1)
                        for b in range(NB):
                            pe.matmul(PS[:, 4, 4 * b:4 * b + 4], con("upper"), tiny("adt", 4 * b, 4 * b + 4),
                                      start=True, stop=True)
                            for h in range(4):
                                pe.matmul(PS[:, 5 + b, h * P:(h + 1) * P],
                                          tiny("adt", 4 * b + h, 4 * b + h + 1).broadcast_to([P, P]), con("upper"),
                                          start=True, stop=True)
                        for g in range(2):
                            pe.drain()
                            rows = slice(64 * g, 64 * g + 64)
                            for b in range(NB):
                                ins = pe.matmul(PS[:, 7, (2 * b + g) * P:(2 * b + g + 1) * P],
                                                xbc3[rows, 2, b * P:(b + 1) * P], xbc3[rows, 3, b * P:(b + 1) * P],
                                                start=True, stop=True)
                        ins.then_inc(ssd2_ps, 1)
                    elif name == "ssd3":
                        pe.wait_ge(mask_ready, 1)
                        for bh in range(8):
                            pe.matmul(PS[:, 4, bh * 64:(bh + 1) * 64], LM[:, bh * P:(bh + 1) * P],
                                      XDT[:, bh * 64:(bh + 1) * 64], start=True, stop=True)
                        for h in range(4):
                            g = h // 2
                            ins = pe.matmul(PS[64 * g:64 * g + 64, 7, h % 2 * 64:h % 2 * 64 + 64],
                                            BT[:, 64 * g:64 * g + 64], DECX[:, h * 64:(h + 1) * 64],
                                            start=True, stop=True)
                        ins.then_inc(ssd3_ps, 1)
                    elif name == "ssd4":
                        pe.wait_ge(state_sb, 1)
                        for h in range(4):
                            if h % 2 == 0:
                                pe.drain()
                            rows = slice(64 * (h // 2), 64 * (h // 2) + 64)
                            ins = pe.matmul(PS[:, 7, h * 64:(h + 1) * 64], xbc3[rows, 3, P:S],
                                            ST[rows, h % 2 * 64:h % 2 * 64 + 64], start=True, stop=True)
                        ins.then_inc(ssd4_ps, 1)
                    elif name == "ssd5":
                        pe.wait_ge(ssd_ready, 1)
                        for b in range(NB):
                            for c in range(CW):
                                ins = pe.transpose(PS[:, 6, c * S + b * P:c * S + (b + 1) * P],
                                                   YS[:, b * W + c * P:b * W + (c + 1) * P], con("ident"))
                        ins.then_inc(ssd5_ps, 1)
                    elif name == "att1":
                        pe.wait_ge(qk_ready, 1)
                        pe.wait_ge(x_tok, 1)
                        pe.wait_ge(decay_log, 1)
                        for c in range(6):
                            for b in range(NB):
                                bank = (2, 2, 3, 3, 5, 5)[c]
                                at = c % 2 * S + b * P
                                ins = pe.transpose(PS[:, bank, at:at + P],
                                                   QK[:, b * 768 + c * P:b * 768 + (c + 1) * P], con("ident"))
                        ins.then_inc(att1_ps, 1)
                    elif name == "gm":
                        pe.wait_ge(v_ready, 1)
                        for b in range(NB):
                            for g in range(4):
                                at = g // 2 * S + b * P
                                ins = pe.matmul(PS[64 * (g % 2):64 * (g % 2) + 64, 6, at:at + P],
                                                V[:, b * W + g * 64:b * W + (g + 1) * 64],
                                                par("sg_w")[:, g * P:(g + 1) * P], start=True, stop=True)
                        ins.then_inc(gm_ps, 1)
                    elif name == "index":
                        pe.wait_ge(qk_t, 1)
                        heads_by_rows(2, 5, index_ps)
                    elif name == "logits":
                        pe.wait_ge(relu_sb, 2)
                        heads_by_rows(0, 4, logit_ps)
                    elif name == "att3":
                        pe.wait_ge(prob_ready, 1)
                        for h in range(4):
                            ins = pe.transpose(PS[:, 7, h * P:(h + 1) * P], RL[0][:, h * P:(h + 1) * P], con("ident"))
                        ins.then_inc(att3_ps, 1)
                        pe.wait_ge(prob_ready, 2)
                        for i in range(8):
                            ins = pe.transpose(PS[:, 5 + i // 4, i % 4 * P:i % 4 * P + P], RL[1][:, i * P:(i + 1) * P],
                                               con("ident"))
                        ins.then_inc(att3_ps, 1)
                    elif name == "att4":
                        pe.wait_ge(prob_t, 2)
                        for h in range(4):
                            rows = slice(64 * (h % 2), 64 * (h % 2) + 64)
                            for b in range(NB):
                                out_ = PS[rows, 4, h // 2 * S + b * P:h // 2 * S + (b + 1) * P]
                                for s in range(b + 1):
                                    prob = PT[b][:, (h * (b + 1) + s) * P:(h * (b + 1) + s + 1) * P]
                                    ins = pe.matmul(out_, misc3[:, s, 64:128], prob, start=s == 0, stop=s == b)
                        ins.then_inc(att4_ps, 1)
                    elif name == "glu":
                        pe.wait_ge(s5_gelu, 1)
                        glu = par("glu_w").rearrange("p (k n) -> p k n", k=2)
                        for c in range(CW):
                            for k in range(CW):
                                ins = pe.matmul(PS[:, 4, c * S:(c + 1) * S], glu[:, k, c * P:(c + 1) * P],
                                                B5[0][:, k * S:(k + 1) * S], start=k == 0, stop=k == CW - 1)
                        ins.then_inc(glu_ps, 1)

                def s5_input(i):
                    if i >= 2:
                        pe.wait_ge(s5v_read, i - 1)
                    s5b = par("s5_b").rearrange("p (r c n) -> p r c n", r=2, c=2)
                    for cc in range(2):
                        pe.drain()
                        for part in range(2):
                            j = 2 * i + cc
                            rows, c = slice(32 * (j % 4), 32 * (j % 4) + 32), j // 4
                            ins = pe.matmul(PS[:, (2 if i % 2 == 0 else 5) + part, cc * S:(cc + 1) * S],
                                            s5b[rows, part, c, :], UT[rows, c * S:(c + 1) * S], start=True, stop=True)
                    ins.then_inc(s5v_ps, 1)

                def s5_output(i):
                    if i == 0:
                        pe.wait_ge(c_ready, 1)
                    pe.wait_ge(s5h_ready, i + 1)
                    for cc in range(2):
                        j = 2 * i + cc
                        out_ = PS[32 * (j % 4):32 * (j % 4) + 32, 7, j // 4 * S:(j // 4 + 1) * S]
                        at = slice(cc * S, (cc + 1) * S)
                        pe.matmul(out_, CRE[:, 32 * j:32 * j + 32], B5[4][:, at], start=True, stop=False)
                        ins = pe.matmul(out_, CIM[:, 32 * j:32 * j + 32], B5[5][:, at], start=False, stop=True)
                    ins.then_inc(s5y_ps, 1)

                for name in ORDER:
                    if name == "sums":
                        pe.wait_ge(mod2_used[0], 3 * KD // 2)
                        pe.wait_ge(mod2_used[1], 3 * KD // 2)
                        sum_rows(ACC2, 2, 5)
                        continue
                    if name == "columns":
                        sum_columns(SUMS2, 2, 1)
                        continue
                    if name[:2] == "s5":
                        if name == "s5a":
                            pe.wait_ge(turn_free[turn("P5") % 2], turn("P5") // 2 + 1)
                            pe.wait_ge(logit_max, 2)
                            s5_input(0)
                        elif name == "s5b":
                            s5_input(1)
                        else:
                            i = int(name[2])
                            s5_output(i - 1)
                            if i < 3:
                                s5_input(i + 1)
                        continue
                    if name[0] not in "PGBO":
                        small(name)
                        continue
                    n = UNITS.index(name)
                    if name[0] in "PG":
                        i = turn(name)
                        turn_wait(pe, i)
                        tok = name in ("P2", "P3", "P4", "P6", "P8")
                        wh, wl = slot(n)
                        if tok:
                            ins = by_token(psum(i % 2), wh, wl)
                        else:
                            ins = by_channel(psum(i % 2), wh, wl, 0 if name == "P0" else None)
                        ins.then_inc(used[n % 3], 1)
                    elif name[0] == "B":
                        bi = int(name[1])
                        wh, wl = (t.rearrange("p (k n) -> p k n", k=CW) for t in slot(n))
                        pe.wait_ge(y_lo, bi + 1)
                        for part in range(4):
                            i = turn(name, part)
                            turn_wait(pe, i)
                            for m in range(2):
                                at = slice((2 * part + m) * P, (2 * part + m + 1) * P)
                                ins = product(PS[:, i % 2, m * S:(m + 1) * S],
                                              [((wh[:, k, at], wl[:, k, at]),
                                                (YH[0][:, k * S:(k + 1) * S], YL[0][:, k * S:(k + 1) * S]))
                                               for k in range(CW)])
                            ins.then_inc(branch_ps, 1)
                        pe.drain().then_inc(used[n % 3], 1)
                        pe.drain().then_inc(y_used, 1)
                    else:
                        o = int(name[1])
                        wh, wl = (t.rearrange("p (m n) -> p m n", m=2) for t in slot(n))
                        pe.wait_ge(mix_ready, o + 1)
                        for b in range(NB):
                            for half in range(2):
                                parts = []
                                for m in range(2):
                                    at = slice(b * P, (b + 1) * P)
                                    parts.append(((hh[:, 2 * o + m, at], hl[:, 2 * o + m, at]),
                                                  (wh[:, m, half * 512:(half + 1) * 512],
                                                   wl[:, m, half * 512:(half + 1) * 512])))
                                ins = product(PS[:, 2 + 2 * b + half, :], parts, o == 0, o == 3)
                            if o == 3 and b == 0:
                                ins.then_inc(wout_ps, 1)
                        ins.then_inc(used[n % 3], 1)
                        if o == 3:
                            pe.drain().then_inc(wout_ps, 1)

                def transposed_norm(i, banks):
                    pe.wait_ge(xn0_ready, i)
                    transpose_x(XN, 0, banks)
                    pe.wait_ge(xn1_ready, i)
                    transpose_x(XN, 1, banks)

                transposed_norm(1, (6, 7, 0, 1))
                pe.wait_ge(router_ready, 1)
                rwh, rwl = (t.rearrange("p (k e) -> p k e", k=KD) for t in (RWH, RWL))
                h_times(PS[:, 3, 0:S], rwh, rwl, 4).then_inc(route_ps, 1)

                def up(x, which, n, k=0):
                    wh, wl = slot(n, k)
                    if x > 1 or not isinstance(k, int):
                        pe.wait_ge(b_read if which else silu_done, 4 * k + x - 1)
                    by_channel(psum(4 + 2 * (x % 2) + which), wh, wl).then_inc(used[n % 3], 1)

                def down(x, n, k=0, first=False, last=False):
                    wh, wl = (t.rearrange("p (f n) -> p f n", f=2) for t in slot(n, k))
                    pe.wait_ge(act_lo, 4 * k + x + 1)
                    for b in range(NB):
                        for half in range(2):
                            parts = []
                            for f in range(2):
                                at = slice(f * S + b * P, f * S + (b + 1) * P)
                                parts.append(((YH[x % 2][:, at], YL[x % 2][:, at]),
                                              (wh[:, f, half * 512:(half + 1) * 512],
                                               wl[:, f, half * 512:(half + 1) * 512])))
                            ins = product(PS[:, 2 * b + half, :], parts, first, last)
                        if last and b == 0:
                            ins.then_inc(moe_ps, 1)
                    ins.then_inc(used[n % 3], 1)

                def transposed_gates():
                    pe.wait_ge(gates_ready, 1)
                    for b in range(NB):
                        ins = pe.transpose(PS[0:E, 2, b * P:(b + 1) * P], RT[:, 128 + b * E:128 + (b + 1) * E],
                                           con("ident"))
                    ins.then_inc(gates_ps, 1)

                def four_experts(k):
                    for i in range(4):
                        n = N_W1S + 2 + 3 * i
                        first = i == 0 and isinstance(k, int)
                        up(i + 1, 0, n, k)
                        if first:
                            transposed_gates()
                        up(i + 1, 1, n + 1, k)
                        if first:
                            pe.wait_ge(gates_sb, 1)
                        down(i, n + 2, k, first=first)

                up(0, 0, N_W1S)
                pe.wait_ge(sig_ready, 1)
                for b in range(NB):
                    ins = pe.transpose(PS[:, 2, b * E:(b + 1) * E], GT[0:E, b * P:(b + 1) * P],
                                       CON[0:E, CC["ident"].start:CC["ident"].start + E])
                ins.then_inc(sig_ps, 1)
                up(0, 1, N_W1S + 1)
                four_experts(0)
                with pe.Fori(1, KD) as k:
                    four_experts(k)
                pe.wait_ge(mod_used[0], KD)
                pe.wait_ge(mod_used[1], KD)
                pe.wait_ge(silu_done, E + 1)
                pe.wait_ge(b_read, E)
                sum_rows(ACC, 6, 4)
                down(E, NUNIT - 1, last=True)
                pe.drain().then_inc(moe_ps, 1)
                sum_columns(SUMS, 6, 2)
                pe.wait_ge(rows_sb, 2)
                transposed_norm(2, (0, 1, 4, 5))
                end_of_layer(pe, l + 1)


def _pack(inp):
    f = {k: np.asarray(v) for k, v in inp.items()}
    L = DEPTH
    z = lambda *s: np.zeros(s, np.float32)

    def kp(w):
        return w.reshape(P, KD, -1)

    def rows(w):
        return w.reshape(-1, P, w.shape[-1]).transpose(1, 0, 2)

    def bc(v):
        return np.broadcast_to(v.reshape(1, -1), (P, v.size))

    proj_cols = [(1732, 1988), (1988, 2244), None, (512, 768), (896, 1152), (1220, 1476), (256, 512), (0, 256),
                 (1476, 1732)]
    packed = z(L * NUNIT + 3, P, UC)
    stream = packed[:L * NUNIT].reshape(L, NUNIT, P, UC)
    for l in range(L):
        w_in = kp(f["w_in"][l])
        for n, name in enumerate(UNITS):
            i = int(name[1:])
            if name[0] == "P":
                if proj_cols[i] is None:
                    u = np.concatenate([w_in[:, :, 768:896], w_in[:, :, 1152:1220], w_in[:, :, 2244:2248],
                                        z(P, KD, 56)], 2)
                else:
                    u = w_in[:, :, proj_cols[i][0]:proj_cols[i][1]]
            elif name[0] == "G":
                u = kp(f["w_gate"][l, BRANCH_OF[i // 4]])[:, :, i % 4 * 256:(i % 4 + 1) * 256]
            elif name[0] == "B":
                u = rows(f["w_branch"][l, BRANCH_OF[i]])
            else:
                u = rows(f["w_out"][l])[:, 2 * i:2 * i + 2]
            stream[l, n] = u.reshape(P, UC)
        stream[l, N_W1S] = kp(f["sh_w1"][l]).reshape(P, UC)
        stream[l, N_W1S + 1] = kp(f["sh_w3"][l]).reshape(P, UC)
        n = N_W1S + 2
        stream[l, n:NUNIT - 1:3] = f["exp_w1"][l].reshape(E, P, UC)
        stream[l, n + 1:NUNIT - 1:3] = f["exp_w3"][l].reshape(E, P, UC)
        stream[l, n + 2] = rows(f["sh_w2"][l]).reshape(P, UC)
        w2 = f["exp_w2"][l].reshape(E, 2, P, D).transpose(0, 2, 1, 3).reshape(E, P, UC)
        stream[l, n + 5::3] = w2[:E - 1]
        stream[l, NUNIT - 1] = w2[E - 1]

    PC, NPARAM = columns(PARAM_COLS)
    params = z(L, P, NPARAM)
    router_w, router_b = z(L, P, KD, P), z(L, P, E)
    AC, NAHEAD = columns(AHEAD_COLS)
    ahead = z(L + 1, P, NAHEAD)
    mods = np.empty((L + 1, KD, 2, P, 3 * D), np.float32)
    gate_b = z(L + 1, 4, 512)
    norms = np.empty((L, 2, 2 * D), np.float32)
    for l in range(L):
        q = params[l]
        conv_w = f["ssd_conv_w"][l].reshape(4, 4, P)
        q[:, PC["conv_w"]] = conv_w.transpose(2, 1, 0).reshape(P, 16)
        q[:, PC["conv_b"]] = f["ssd_conv_b"][l].reshape(4, P).T
        for a, b in (("dt_bias", "ssd_dt_bias"), ("a_log", "ssd_a_log"), ("ssd_d", "ssd_d"), ("gm_g", "gm_ln_g"),
                     ("gm_b", "gm_ln_b"), ("norm_g", "ssd_norm_g")):
            q[:, PC[a]] = bc(f[b][l])
        q[:, PC["s5_d"]] = f["s5_d"][l].reshape(2, P).T
        q[:, PC["glu_b"]] = f["s5_glu_b"][l].reshape(2, P).T
        q[:, PC["sg_b"]] = np.repeat(f["gm_b"][l].reshape(2, 2, 1, P), 64, 2).reshape(2, P, P).transpose(
            1, 0, 2).reshape(P, 256)
        q[:, PC["sg_w"]] = f["gm_w"][l].transpose(2, 0, 1).reshape(P, 512)
        for r, (bn, cn) in enumerate((("s5_b_re", "s5_c_re"), ("s5_b_im", "s5_c_im"))):
            b5 = z(8, 2, 16, 2, 64)
            c5 = z(8, 2, 64, 2, 16)
            for gg in range(2):
                b5[:, gg, :, gg] = f[bn][l].reshape(8, 2, 64, 16)[:, gg].transpose(0, 2, 1)
                c5[:, gg, :, gg] = f[cn][l].reshape(8, 2, 16, 64)[:, gg].transpose(0, 2, 1)
            o = PC["s5_b"].start + 256 * r
            q[:, o:o + 256] = b5.reshape(2, P, P).transpose(1, 0, 2).reshape(P, 256)
            o = PC["s5_c"].start + 256 * r
            q[:, o:o + 256] = c5.reshape(8, P, 32).transpose(1, 0, 2).reshape(P, 256)
        q[:, PC["glu_w"]] = rows(f["s5_glu_w"][l]).reshape(P, 512)
        router_w[l, :, :, :E] = kp(f["router_w"][l])
        router_b[l] = bc(f["router_bias"][l])
        mod_b = np.stack([f["mod1_b"][l], f["mod2_b"][l]]).reshape(2, 3, D)
        ahead[l][:, AC["mod_b"]] = mod_b[:, :2].reshape(2, 2, P, KD).transpose(2, 0, 1, 3).reshape(P, 32)
        gate_b[l] = mod_b[:, 2].reshape(4, 512)
        norms[l, 0] = np.concatenate([f["ln1_g"][l], f["ln1_b"][l]])
        norms[l, 1] = np.concatenate([f["ln2_g"][l], f["ln2_b"][l]])
        state = lambda v: v.reshape(8, P).T
        ahead[l][:, AC["lam_re"]] = state(f["s5_lam_re"][l])
        ahead[l][:, AC["lam_im"]] = state(f["s5_lam_im"][l])
        ahead[l][:, AC["log_step"]] = state(np.repeat(f["s5_log_step"][l], 64))
        before = (f["ln2_g"][l - 1], f["ln2_b"][l - 1]) if l else (np.ones(D, np.float32), z(D))
        for name, pair in (("norm_g", (before[0], f["ln1_g"][l])), ("norm_b", (before[1], f["ln1_b"][l]))):
            ahead[l][:, AC[name]] = np.stack(pair).reshape(2, P, KD).transpose(1, 0, 2).reshape(P, 16)
        for j, name in enumerate(("mod1_w", "mod2_w")):
            mods[l, :, j] = f[name][l].reshape(P, KD, 3 * D).transpose(1, 0, 2)
    ahead[L], mods[L], gate_b[L] = ahead[0], mods[0], gate_b[0]
    CC, NCONST = columns(CONST_COLS)
    con = z(P, NCONST)
    i = np.arange(P)
    con[:, CC["ident"]] = np.eye(P)
    con[:, CC["upper"]] = i[None, :] >= i[:, None]
    con[:, CC["lower"]] = i[None, :] <= i[:, None]
    con[:, CC["floor"]] = np.where(i[None, :] <= i[:, None], 0.0, FLOOR)
    con[:, CC["ones"]] = 1.0
    con[:, CC["time"]] = np.arange(S)
    con[:, CC["inv"]] = (np.float32(500000.0) ** (-np.arange(0, 16, 2, dtype=np.float32) / np.float32(16)))
    con[:, CC["before"]] = (np.arange(8)[None, :] < np.arange(8)[:, None]).reshape(1, 64)
    pos = np.ascontiguousarray(f["positions"].reshape(NB, P).T.astype(np.int32))
    return dict(x=f["x"][0], pos=pos, cvec=f["c"].reshape(P, KD), consts=con, params=params,
                router_w=router_w.reshape(L, P, KD * P), router_b=router_b,
                gate_b=gate_b, ahead=ahead, norms=norms, mods=mods, stream=packed)


def kernel(**inputs):
    import concourse.bacc as bacc
    from concourse.bass_utils import run_bass_kernel_spmd

    nc = bacc.Bacc("TRN2", target_bir_lowering=False, num_devices=1)
    arrays = {k: np.ascontiguousarray(v) for k, v in _pack(inputs).items()}
    args = {k: nc.dram_tensor(k, v.shape, mybir.dt.from_np(v.dtype), kind="ExternalInput").ap()
            for k, v in arrays.items()}
    gate_rows = nc.dram_tensor("gate_rows", (2, D), F32, kind="Internal").ap()
    gates_t = nc.dram_tensor("gates_t", (E, S), F32, kind="Internal").ap()
    out = nc.dram_tensor("out", (S, D), F32, kind="ExternalOutput").ap()
    bass_trunk(nc, **args, gate_rows=gate_rows, gates_t=gates_t, out=out)
    r = run_bass_kernel_spmd(nc, [arrays], core_ids=[0])
    return r.results[0]["out"].reshape(1, S, D)
```
